# Optimizing a Trainium2 kernel written in Bass

```python
import jax
import jax.numpy as jnp
from jax import lax
import numpy as np

D_MODEL = 1024
BATCH = 1
SEQ = 256
DEPTH = 2

CTX_LEN = 256
GRID_W = 64
EPS = 1e-6
ALPHA = (2 * DEPTH) ** 0.25
BETA = (8 * DEPTH) ** -0.25
N_MOD = 6

CONV_CH = D_MODEL // 2
CONV_WIDTH = 31
ATT_HEADS = 8
ATT_KV_HEADS = 2
HEAD_DIM = 64
ATT_W = ATT_HEADS * HEAD_DIM
KV_W = ATT_KV_HEADS * HEAD_DIM
Q_BLOCK = 128
ROPE_BASE = 10000.0
AB_IN = 2 * CONV_CH + ATT_W + 2 * KV_W
AB_OUT = CONV_CH + ATT_W

ML_HEADS = 4
ML_DQK = D_MODEL // 8
ML_DV = D_MODEL // 4
ML_CHUNK = 64
ML_QK_W = ML_HEADS * ML_DQK
ML_V_W = ML_HEADS * ML_DV
C_IN = 2 * ML_QK_W + 2 * ML_V_W + 4 * ML_HEADS
C_OUT = ML_V_W

PEER_HEADS = 8
PEER_DK = 256
N_KEYS = 128
N_EXPERTS = N_KEYS * N_KEYS
PEER_TOPK = 16
PEER_BLOCK = 128

N_EVEN = (DEPTH + 1) // 2
N_ODD = DEPTH // 2

kernel_name = 'hybrid_conv_gqa_mlstm_peer_diffusion_block'

def layer_norm(x, g=None, b=None):
    xf = x.astype(jnp.float32)
    mu = jnp.mean(xf, axis=-1, keepdims=True)
    var = jnp.mean(jnp.square(xf - mu), axis=-1, keepdims=True)
    y = (xf - mu) * lax.rsqrt(var + EPS)
    if g is not None:
        y = y * g.astype(jnp.float32)
    if b is not None:
        y = y + b.astype(jnp.float32)
    return y.astype(x.dtype)

def rms_norm(x, g):
    xf = x.astype(jnp.float32)
    y = xf * lax.rsqrt(jnp.mean(jnp.square(xf), axis=-1, keepdims=True) + EPS)
    return (y * g.astype(jnp.float32)).astype(x.dtype)

def modulate(x, shift, scale):
    return layer_norm(x) * (1 + scale) + shift

def rope_1d(x, pos):
    f = x.shape[-1] // 2
    inv_freq = ROPE_BASE ** (-jnp.arange(f, dtype=jnp.float32) / f)
    ang = pos[:, None] * inv_freq[None, :]
    cos = jnp.cos(ang)[None, :, None, :]
    sin = jnp.sin(ang)[None, :, None, :]
    xf = x.astype(jnp.float32)
    x1, x2 = xf[..., :f], xf[..., f:]
    return jnp.concatenate([x1 * cos - x2 * sin, x2 * cos + x1 * sin], axis=-1).astype(x.dtype)

def axial_rope(x, row, col):
    half = x.shape[-1] // 2
    return jnp.concatenate([rope_1d(x[..., :half], row), rope_1d(x[..., half:], col)], axis=-1)

def grid_positions(n_tokens):
    rows = n_tokens // GRID_W
    row = jnp.repeat(jnp.arange(rows, dtype=jnp.float32), GRID_W)
    col = jnp.tile(jnp.arange(GRID_W, dtype=jnp.float32), rows)
    return row, col

def depthwise_conv(x, w, b):
    pad = CONV_WIDTH // 2
    y = lax.conv_general_dilated(x, w[:, None, :].astype(x.dtype), window_strides=(1,),
                                 padding=[(pad, pad)], dimension_numbers=('NWC', 'WIO', 'NWC'),
                                 feature_group_count=x.shape[-1])
    return y + b

def gqa_attend(q, k, v):
    s = jnp.einsum('bqkgd,bskd->bkgqs', q, k).astype(jnp.float32)
    p = jax.nn.softmax(s, axis=-1).astype(v.dtype)
    return jnp.einsum('bkgqs,bskd->bqkgd', p, v)

def mixer_conv_gqa(hc, hl, w_in, b_in, conv_w, conv_b, conv_ln_g, conv_ln_b, q_norm_g, k_norm_g,
                   w_out, b_out, need_ctx):
    B, L, _ = hl.shape
    Lc = hc.shape[1]
    G = ATT_HEADS // ATT_KV_HEADS
    cuts = [CONV_CH, 2 * CONV_CH, 2 * CONV_CH + ATT_W, 2 * CONV_CH + ATT_W + KV_W]

    def project(h):
        n = h.shape[1]
        a_val, a_gate, q, k, v = jnp.split(h @ w_in + b_in, cuts, axis=-1)
        q = rms_norm(q.reshape(B, n, ATT_HEADS, HEAD_DIM), q_norm_g)
        k = rms_norm(k.reshape(B, n, ATT_KV_HEADS, HEAD_DIM), k_norm_g)
        v = v.reshape(B, n, ATT_KV_HEADS, HEAD_DIM)
        return a_val, a_gate, q, k, v

    def conv_group(a_val, a_gate):
        u = depthwise_conv(a_val * jax.nn.sigmoid(a_gate), conv_w, conv_b)
        return jax.nn.silu(layer_norm(u, conv_ln_g, conv_ln_b))

    def merge(conv_out, att_out):
        return jnp.concatenate([conv_out, att_out], axis=-1) @ w_out + b_out

    ac_v, ac_g, qc, kc, vc = project(hc)
    al_v, al_g, ql, kl, vl = project(hl)
    row, col = grid_positions(L)
    ql = axial_rope(ql, row, col)
    kl = axial_rope(kl, row, col)
    scale = HEAD_DIM ** -0.5
    k_all = jnp.concatenate([kc, kl], axis=1)
    v_all = jnp.concatenate([vc, vl], axis=1)
    q_blocks = (ql * scale).reshape(B, L // Q_BLOCK, Q_BLOCK, ATT_KV_HEADS, G, HEAD_DIM).transpose(1, 0, 2, 3, 4, 5)
    o_blocks = lax.map(lambda qb: gqa_attend(qb, k_all, v_all), q_blocks)
    ol = o_blocks.transpose(1, 0, 2, 3, 4, 5).reshape(B, L, ATT_W)
    yl = merge(conv_group(al_v, al_g), ol)
    yc = None
    if need_ctx:
        oc = gqa_attend((qc * scale).reshape(B, Lc, ATT_KV_HEADS, G, HEAD_DIM), kc, vc).reshape(B, Lc, ATT_W)
        yc = merge(conv_group(ac_v, ac_g), oc)
    return yc, yl

def mlstm_scan(q, k, v, ig, lf, state):
    B, L = q.shape[:2]
    nc = L // ML_CHUNK

    def chunks(t):
        t = t.reshape((B, nc, ML_CHUNK) + t.shape[2:])
        return jnp.moveaxis(jnp.moveaxis(t, 1, 0), 3, 2)

    mask = jnp.tril(jnp.ones((ML_CHUNK, ML_CHUNK), dtype=bool))

    def step(carry, inp):
        C, n, m = carry
        qc, kc, vc, ic, fc = inp
        b = jnp.cumsum(fc, axis=-1)
        a = b + m[..., None]
        dlog = jnp.where(mask, b[..., :, None] - b[..., None, :] + ic[..., None, :], -jnp.inf)
        mt = jnp.maximum(a, jnp.max(dlog, axis=-1))
        w = jnp.exp(dlog - mt[..., None])
        aw = jnp.exp(a - mt)
        s = jnp.einsum('bhtd,bhsd->bhts', qc, kc) * w
        num = jnp.einsum('bhts,bhsv->bhtv', s, vc) + aw[..., None] * jnp.einsum('bhtd,bhvd->bhtv', qc, C)
        den = jnp.sum(s, axis=-1) + aw * jnp.einsum('bhtd,bhd->bht', qc, n)
        h = num / jnp.maximum(jnp.abs(den), jnp.exp(-mt))[..., None]
        bl = b[..., -1]
        wl = bl[..., None] - b + ic
        mn = jnp.maximum(bl + m, jnp.max(wl, axis=-1))
        wc = jnp.exp(wl - mn[..., None])
        dc = jnp.exp(bl + m - mn)
        C = dc[..., None, None] * C + jnp.einsum('bhs,bhsv,bhsd->bhvd', wc, vc, kc)
        n = dc[..., None] * n + jnp.einsum('bhs,bhsd->bhd', wc, kc)
        return (C, n, mn), h

    state, h = lax.scan(step, state, (chunks(q), chunks(k), chunks(v), chunks(ig), chunks(lf)))
    h = jnp.swapaxes(jnp.moveaxis(h, 0, 1), 2, 3).reshape(B, L, ML_HEADS, ML_DV)
    return state, h

def mixer_mlstm(hc, hl, w_in, b_in, norm_g, w_out, b_out, need_ctx):
    B = hl.shape[0]
    cuts = [ML_QK_W, 2 * ML_QK_W, 2 * ML_QK_W + ML_V_W, 2 * ML_QK_W + 2 * ML_V_W]
    f32 = jnp.float32

    def project(h):
        n = h.shape[1]
        q, k, v, o, g = jnp.split(h @ w_in + b_in, cuts, axis=-1)
        q = q.reshape(B, n, ML_HEADS, ML_DQK).astype(f32)
        k = k.reshape(B, n, ML_HEADS, ML_DQK).astype(f32) * (ML_DQK ** -0.5)
        v = v.reshape(B, n, ML_HEADS, ML_DV).astype(f32)
        g = g.reshape(B, n, 4, ML_HEADS).astype(f32)
        fwd = (g[:, :, 0], jax.nn.log_sigmoid(g[:, :, 1]))
        bwd = (g[:, :, 2], jax.nn.log_sigmoid(g[:, :, 3]))
        return q, k, v, o, fwd, bwd

    def flip(t):
        return jnp.flip(t, axis=1)

    qc, kc, vc, oc, gc_f, gc_b = project(hc)
    ql, kl, vl, ol, gl_f, gl_b = project(hl)
    init = (jnp.zeros((B, ML_HEADS, ML_DV, ML_DQK), f32), jnp.zeros((B, ML_HEADS, ML_DQK), f32),
            jnp.zeros((B, ML_HEADS), f32))
    st_cf, h_cf = mlstm_scan(qc, kc, vc, gc_f[0], gc_f[1], init)
    _, h_lf = mlstm_scan(ql, kl, vl, gl_f[0], gl_f[1], st_cf)
    st_cb, h_cb = mlstm_scan(flip(qc), flip(kc), flip(vc), flip(gc_b[0]), flip(gc_b[1]), init)
    _, h_lb = mlstm_scan(flip(ql), flip(kl), flip(vl), flip(gl_b[0]), flip(gl_b[1]), st_cb)

    def finish(hf, hb, o):
        n = o.shape[1]
        hn = layer_norm(hf + hb, norm_g.reshape(ML_HEADS, ML_DV))
        y = hn.reshape(B, n, C_OUT).astype(o.dtype) * jax.nn.sigmoid(o)
        return y @ w_out + b_out

    yl = finish(h_lf, flip(h_lb), ol)
    yc = finish(h_cf, flip(h_cb), oc) if need_ctx else None
    return yc, yl

def peer(h, w_q, sub_k1, sub_k2, u_tab, v_tab):
    B, L, D = h.shape
    xt = h.reshape(B * L // PEER_BLOCK, PEER_BLOCK, D)

    def block(xb):
        qh = (xb @ w_q).reshape(PEER_BLOCK, PEER_HEADS, 2, PEER_DK // 2)
        s1 = jnp.einsum('thd,hkd->thk', qh[:, :, 0], sub_k1).astype(jnp.float32)
        s2 = jnp.einsum('thd,hkd->thk', qh[:, :, 1], sub_k2).astype(jnp.float32)
        v1, i1 = lax.top_k(s1, PEER_TOPK)
        v2, i2 = lax.top_k(s2, PEER_TOPK)
        cand = (v1[..., :, None] + v2[..., None, :]).reshape(PEER_BLOCK, PEER_HEADS, PEER_TOPK * PEER_TOPK)
        cid = (i1[..., :, None] * N_KEYS + i2[..., None, :]).reshape(PEER_BLOCK, PEER_HEADS, PEER_TOPK * PEER_TOPK)
        sc, pos = lax.top_k(cand, PEER_TOPK)
        eid = jnp.take_along_axis(cid, pos, axis=-1)
        g = jax.nn.softmax(sc, axis=-1)
        act = jax.nn.gelu(jnp.einsum('thed,td->the', u_tab[eid], xb).astype(jnp.float32), approximate=False)
        return jnp.einsum('the,thed->td', (g * act).astype(xb.dtype), v_tab[eid])

    return lax.map(block, xt).reshape(B, L, D)

def setup_inputs(seed: int = 0) -> dict:
    key = jax.random.key(seed)
    keys = iter(list(jax.random.split(key, 40)))

    def nrm(shape, s):
        return jax.random.normal(next(keys), shape, jnp.float32) * s

    D = D_MODEL
    g0 = C_IN - 4 * ML_HEADS
    forget_bias = jnp.linspace(3.0, 6.0, ML_HEADS, dtype=jnp.float32)
    ml_b_in = nrm((N_ODD, C_IN), 0.02)
    ml_b_in = ml_b_in.at[:, g0 + ML_HEADS:g0 + 2 * ML_HEADS].add(forget_bias).at[:, g0 + 3 * ML_HEADS:].add(forget_bias)
    return {
        'x': nrm((BATCH, SEQ, D), 1.0),
        'c': nrm((BATCH, D), 1.0),
        'ctx': nrm((BATCH, CTX_LEN, D), 1.0),
        'c_ctx': nrm((D,), 1.0),
        'w_mod': nrm((DEPTH, D, N_MOD * D), D ** -0.5),
        'b_mod': nrm((DEPTH, N_MOD * D), 0.02),
        'ln1_g': 1.0 + nrm((DEPTH, D), 0.02),
        'ln1_b': nrm((DEPTH, D), 0.02),
        'ln2_g': 1.0 + nrm((DEPTH, D), 0.02),
        'ln2_b': nrm((DEPTH, D), 0.02),
        'ab_w_in': nrm((N_EVEN, D, AB_IN), D ** -0.5),
        'ab_b_in': nrm((N_EVEN, AB_IN), 0.02),
        'ab_conv_w': nrm((N_EVEN, CONV_WIDTH, CONV_CH), CONV_WIDTH ** -0.5),
        'ab_conv_b': nrm((N_EVEN, CONV_CH), 0.02),
        'ab_conv_ln_g': 1.0 + nrm((N_EVEN, CONV_CH), 0.02),
        'ab_conv_ln_b': nrm((N_EVEN, CONV_CH), 0.02),
        'ab_q_norm_g': 1.0 + nrm((N_EVEN, HEAD_DIM), 0.02),
        'ab_k_norm_g': 1.0 + nrm((N_EVEN, HEAD_DIM), 0.02),
        'ab_w_out': nrm((N_EVEN, AB_OUT, D), BETA * AB_OUT ** -0.5),
        'ab_b_out': nrm((N_EVEN, D), 0.02),
        'ml_w_in': nrm((N_ODD, D, C_IN), D ** -0.5),
        'ml_b_in': ml_b_in,
        'ml_norm_g': 1.0 + nrm((N_ODD, C_OUT), 0.02),
        'ml_w_out': nrm((N_ODD, C_OUT, D), BETA * C_OUT ** -0.5),
        'ml_b_out': nrm((N_ODD, D), 0.02),
        'peer_w_q': nrm((DEPTH, D, PEER_HEADS * PEER_DK), D ** -0.5),
        'peer_k1': nrm((DEPTH, PEER_HEADS, N_KEYS, PEER_DK // 2), (PEER_DK // 2) ** -0.5),
        'peer_k2': nrm((DEPTH, PEER_HEADS, N_KEYS, PEER_DK // 2), (PEER_DK // 2) ** -0.5),
        'peer_u': nrm((DEPTH, N_EXPERTS, D), D ** -0.5),
        'peer_v': nrm((DEPTH, N_EXPERTS, D), BETA),
    }

def reference(x, c, ctx, c_ctx, w_mod, b_mod, ln1_g, ln1_b, ln2_g, ln2_b,
              ab_w_in, ab_b_in, ab_conv_w, ab_conv_b, ab_conv_ln_g, ab_conv_ln_b, ab_q_norm_g, ab_k_norm_g,
              ab_w_out, ab_b_out, ml_w_in, ml_b_in, ml_norm_g, ml_w_out, ml_b_out,
              peer_w_q, peer_k1, peer_k2, peer_u, peer_v):
    for i in range(DEPTH):
        need_ctx = i < DEPTH - 1
        j = i // 2
        mod_l = (jax.nn.silu(c) @ w_mod[i] + b_mod[i])[:, None, :]
        mod_c = (jax.nn.silu(c_ctx) @ w_mod[i] + b_mod[i])[None, None, :]
        sh1l, sc1l, g1l, sh2l, sc2l, g2l = jnp.split(mod_l, N_MOD, axis=-1)
        sh1c, sc1c, g1c, sh2c, sc2c, g2c = jnp.split(mod_c, N_MOD, axis=-1)
        hl = modulate(x, sh1l, sc1l)
        hc = modulate(ctx, sh1c, sc1c)
        if i % 2 == 0:
            yc, yl = mixer_conv_gqa(hc, hl, ab_w_in[j], ab_b_in[j], ab_conv_w[j], ab_conv_b[j],
                                    ab_conv_ln_g[j], ab_conv_ln_b[j], ab_q_norm_g[j], ab_k_norm_g[j],
                                    ab_w_out[j], ab_b_out[j], need_ctx)
        else:
            yc, yl = mixer_mlstm(hc, hl, ml_w_in[j], ml_b_in[j], ml_norm_g[j], ml_w_out[j], ml_b_out[j], need_ctx)
        x = layer_norm(ALPHA * x + g1l * yl, ln1_g[i], ln1_b[i])
        x = layer_norm(ALPHA * x + g2l * peer(modulate(x, sh2l, sc2l), peer_w_q[i], peer_k1[i], peer_k2[i],
                                              peer_u[i], peer_v[i]), ln2_g[i], ln2_b[i])
        if need_ctx:
            ctx = layer_norm(ALPHA * ctx + g1c * yc, ln1_g[i], ln1_b[i])
            ctx = layer_norm(ALPHA * ctx + g2c * peer(modulate(ctx, sh2c, sc2c), peer_w_q[i], peer_k1[i],
                                                      peer_k2[i], peer_u[i], peer_v[i]), ln2_g[i], ln2_b[i])
    return x


_drawn_inputs = setup_inputs


def setup_inputs(seed=0):
    import zlib

    import numpy as np

    out = dict(_drawn_inputs(seed))
    spreads = {}
    factors = {'ab_b_in': 3.254,
     'ab_conv_b': 3.969,
     'ab_conv_ln_g': 4.246,
     'ab_conv_ln_b': 4.162,
     'ab_q_norm_g': 8.0,
     'ab_k_norm_g': 8.0,
     'ml_norm_g': 19.442,
     'ml_b_out': 10.66}
    for name, (base, spread) in spreads.items():
        noise = np.random.default_rng([zlib.crc32(name.encode()), seed]).standard_normal(out[name].shape)
        drawn = base * np.exp(spread * noise) if base else spread * noise
        out[name] = jnp.asarray(drawn.astype(out[name].dtype))
    for name, factor in factors.items():
        out[name] = (out[name] * factor).astype(out[name].dtype)
    return out
```

```python
import concourse.bass as bass
import numpy as np
from concourse import mybir
from contextlib import ExitStack

F32 = mybir.dt.float32
U32 = mybir.dt.uint32
ALU = mybir.AluOpType
ACT = mybir.ActivationFunctionType
AX = mybir.AxisListType

P = 128
D = 1024
KD = D // P
TILES = 4
LAT = (2, 3)
EPS = 1e-6
ALPHA = 4 ** 0.25
HEAD = 64
NQH, NKV = 8, 2
QKW = (NQH + NKV) * HEAD
CC = 4
TAPS = 31
PAD = TAPS // 2
CW = 256 + 2 * PAD
UW = 512
MH, MDQ, MDV = 4, 128, 256
PH, NK, TOPK = 8, 128, 16
E = PH * TOPK
NB = 6
RING = 8
STEP = 16
GROUP = 2
NDIAG = 4
NEG = -1.0e30
LOWEST = -3.0e38

C_ID, C_LT, C_UT, C_ONE, C_COS, C_SIN, C_IOTA, C_END = 0, 128, 256, 384, 512, 640, 768, 784
Q_VB, Q_GB, Q_CB, Q_LG, Q_LB, Q_CW, Q_MQ, Q_MK, Q_END = 0, 4, 8, 12, 16, 20, 144, 148, 152


def plan():
    base, n, units = {}, 0, []

    def stage(name, count):
        nonlocal n
        base[name] = n
        n += count

    def unit(last):
        units.append(last)

    for l in (0, 1):
        stage(f"mod{l}", 12)
        for u in range(12):
            unit(base[f"mod{l}"] + u)
        stage(f"ht1_{l}", 8)
        if l == 0:
            for s in ("gate", "val", "q", "kv"):
                stage(s, 4)
                unit(base[s] + 3)
            stage("qt", 4)
            stage("kt", 1)
            groups = [(t, g) for t in range(TILES) for g in range(NKV)]
            stage("att_s0", 4)
            for i, (t, g) in enumerate(groups):
                if i + 1 < len(groups):
                    stage(f"att_s{i + 1}", 4)
                stage(f"att_t{i}", 2 if t < 2 else 4)
                stage(f"att_o{i}", 1)
            stage("ut", 4)
            stage("ct", 4)
            stage("merge0", 8)
            unit(base["merge0"] + 3)
            unit(base["merge0"] + 7)
            stage("ht2_0", 8)
        else:
            stage("mq", 4)
            unit(base["mq"] + 3)
            stage("mk", 4)
            unit(base["mk"] + 3)
            stage("mv", 8)
            unit(base["mv"] + 3)
            unit(base["mv"] + 7)
            stage("mo", 4)
            unit(base["mo"] + 1)
            unit(base["mo"] + 3)
            stage("mg", 1)
            unit(base["mg"])
            stage("cum", 1)
            stage("ctr", 1)
            for h in range(MH):
                stage(f"ml{h}", 8)
            stage("yt", 4)
            stage("merge1", 4)
            unit(base["merge1"] + 1)
            unit(base["merge1"] + 3)
            stage("ht2_1", 4)
        stage(f"route{l}", 32)
        for u in range(4):
            unit(base[f"route{l}"] + 8 * u + 7)
    return base, units


def build(nc, a, debug):
    J, UNIT_LAST = plan()
    groups = [(t, g) for t in range(TILES) for g in range(NKV)]
    with ExitStack() as ctx:
        def sb(name, shape, dt=F32):
            return ctx.enter_context(nc.sbuf_tensor(name, shape, dt))

        def sem(name):
            return ctx.enter_context(nc.semaphore(name))

        banks = [ctx.enter_context(nc.psum_tensor(f"bank{i}", [P, 512], F32)) for i in range(NB)]
        expert_sum = ctx.enter_context(nc.psum_tensor("expert_sum", [P, D], F32))

        x = sb("x", [P, TILES, D])
        h = sb("h", [P, TILES, D])
        ht = sb("ht", [P, KD, TILES * P])
        shsc = sb("shsc", [P, 2, 2, D])
        gmod = sb("gmod", [P, 2, D])
        lngb = sb("lngb", [P, 2, D])
        bout = sb("bout", [P, D])
        w = sb("w", [P, 2, KD, UW])
        con = sb("con", [P, C_END])
        col = sb("col", [P, Q_END])
        cvec = sb("cvec", [P, KD, 2])
        stats = sb("stats", [P, 12])
        mv = sb("mv", [P, 8, 2])
        std = sb("std", [P, 40])
        rstd = sb("rstd", [P, 40])
        gates = sb("gates", [P, TILES * E])
        eid = sb("eid", [P, TILES * E + 2 * RING], U32)
        rows_idx = sb("rows_idx", [P, 2, RING], U32)
        dots = sb("dots", [P, STEP])
        gel = sb("gel", [P, STEP])
        wexp = sb("wexp", [P, STEP])
        diag = sb("diag", [P, NDIAG, P])
        small = sb("small", [P, 64])
        arena = sb("arena", [P, 18800])
        at = 0

        def cut(n):
            nonlocal at
            at += n
            assert at <= 18800, at
            return arena[:, at - n:at]

        ident = con[:, C_ID:C_ID + P]

        bm, mrow = arena[0:2, 0:6 * D], arena[0:2, 6 * D:12 * D]
        at = 0
        sg = cut(2048).rearrange("p (c n) -> p c n", c=4)
        ut = sg
        cin = cut(CC * 2 * CW).rearrange("p (c s n) -> p c s n", c=CC, s=2)
        u = cut(2048).rearrange("p (c n) -> p c n", c=4)
        pr1 = u
        pr0 = cut(2048).rearrange("p (c n) -> p c n", c=4)
        probs = (pr0, pr1)
        pt = cut(2048).rearrange("p (c n) -> p c n", c=4)
        qk = cut(TILES * QKW).rearrange("p (t n) -> p t n", t=TILES)
        tmp1, tmp2 = cut(QKW), cut(QKW)
        vv = cut(TILES * P).rearrange("p (t n) -> p t n", t=TILES)
        qt = cut(4 * 512).rearrange("p (c n) -> p c n", c=4)
        kt = cut(512)
        qkvb = cut(768)
        qkg = cut(QKW)
        at = 0
        keys = cut(2048).rearrange("p (c n) -> p c n", c=16)
        qh = cut(1024).rearrange("p (s n) -> p s n", s=2)
        tv = cut(1024).rearrange("p (t c k) -> p t c k", t=TILES, c=16)
        ti = cut(1024).bitcast(U32).rearrange("p (t c k) -> p t c k", t=TILES, c=16)
        tif = cut(256).rearrange("p (c k) -> p c k", c=16)
        cand = cut(2048).rearrange("p (h i j) -> p h i j", h=PH, i=TOPK)
        hot = cut(2048).rearrange("p (h i j) -> p h i j", h=PH, i=TOPK)
        sc = cut(128).rearrange("p (h k) -> p h k", h=PH)
        pos = cut(128).bitcast(U32).rearrange("p (h k) -> p h k", h=PH)
        posi = cut(128).bitcast(U32).rearrange("p (h k) -> p h k", h=PH)
        posf = cut(128).rearrange("p (h k) -> p h k", h=PH)
        e1 = cut(128).rearrange("p (h k) -> p h k", h=PH)
        e2 = cut(128).rearrange("p (h k) -> p h k", h=PH)
        left = cut(256)
        ring = arena[:, 0:RING * 2048].rearrange("p (r n) -> p r n", r=RING)
        at = 0
        mqt = cut(1024).rearrange("p (h n) -> p h n", h=MH)
        mkt = cut(2048).rearrange("p (h n) -> p h n", h=MH)
        mv_ = cut(4096).rearrange("p (t n) -> p t n", t=TILES)
        mask = cut(2048).rearrange("p (r n) -> p r n", r=4)
        sel = cut(1024).rearrange("p (r n) -> p r n", r=8)
        cm = cut(2048).rearrange("p (r n) -> p r n", r=4)
        am = cut(1024).rearrange("p (r n) -> p r n", r=2)
        att = cut(1024).rearrange("p (r n) -> p r n", r=2)
        ct_ = cut(512)
        mlb = cut(2064)
        normg = cut(1024)
        gt = cut(64).rearrange("p (t n) -> p t n", t=TILES)
        lf = cut(32).rearrange("p (t n) -> p t n", t=TILES)
        la = cut(32).rearrange("p (t n) -> p t n", t=TILES)
        le = cut(32).rearrange("p (t n) -> p t n", t=TILES)
        bc = cut(32).rearrange("p (t n) -> p t n", t=TILES)
        cg = cut(32).rearrange("p (t n) -> p t n", t=TILES)
        nm = cut(8)
        thr = cut(8)
        den = cut(8)
        og = h[:, 0:2, :]
        hh = h[:, 2:4, :]

        bank_full = [sem(f"bank_full{i}") for i in range(NB)]
        bank_drained = [sem(f"bank_drained{i}") for i in range(NB)]
        w_loaded = [sem(f"w_loaded{i}") for i in range(2)]
        loads = {n: sem(f"in_{n}") for n in (
            "const", "x", "cvec", "bmod", "modstore", "shsc", "gmod", "lngb", "bout", "qkvb", "keys", "mlc")}
        dve_step = sem("dve_step")
        act_step = sem("act_step")
        pool_step = sem("pool_step")
        silu_ready = sem("silu_ready")
        h_ready = sem("h_ready")
        h_freed = sem("shsc_used")
        var_ready = sem("var_ready")
        std_ready = sem("std_ready")
        post_done = sem("post_done")
        qk_ready = sem("qk_ready")
        rowmax_ready = sem("rowmax_ready")
        exp_ready = sem("exp_ready")
        probs_ready = sem("probs_ready")
        conv_done = sem("conv_done")
        un_ready = sem("un_ready")
        cin_zero = sem("cin_zero")
        sc_ready = sem("sc_ready")
        scexp_ready = sem("scexp_ready")
        eid_ready = sem("eid_ready")
        idx_staged = sem("idx_staged")
        slots_free = sem("slots_free")
        row_in = [sem(f"row_in{i}") for i in range(RING)]
        dots_ready = sem("dots_ready")
        gelu_ready = sem("gelu_ready")
        wexp_ready = sem("wexp_ready")
        diag_ready = sem("diag_ready")
        sum_taken = sem("sum_taken")
        lf_a = sem("lf_a")
        lf_e = sem("lf_e")
        lf_ready = sem("lf_ready")
        cg_ready = sem("cg_ready")
        nm_ready = sem("nm_ready")
        wm_ready = sem("wm_ready")
        am_ready = sem("am_ready")
        o_ready = sem("o_ready")
        sig_ready = sem("sig_ready")
        y_ready = sem("y_ready")
        stored = sem("stored")

        def bank(n):
            return banks[n % NB]

        def job_done(eng, n):
            eng.wait_ge(bank_full[n % NB], n // NB + 1)

        def job_drained(eng, n):
            eng.wait_ge(bank_drained[n % NB], n // NB + 1)

        def drains(ins, n):
            ins.then_inc(bank_drained[n % NB], 1)

        block = ctx.enter_context(nc.Block())

        @block.sync
        def _(sp):
            unit_no = [0]

            def load_unit(src):
                n = unit_no[0]
                unit_no[0] += 1
                if n >= 2:
                    job_done(sp, UNIT_LAST[n - 2])
                cols = src.shape[1]
                sp.dma_start(w[:, n % 2, :, 0:cols], src.rearrange("(k p) n -> p k n", p=P)).then_inc(w_loaded[n % 2], 16)

            def load_mod(l, first, dst, name):
                for s in range(2):
                    for i in range(dst.shape[2] if len(dst.shape) == 4 else 1):
                        d = dst[:, s, i, :] if len(dst.shape) == 4 else dst[:, s, :]
                        sp.dma_start(d, a["mod_d"][l, s, (first + i) * D:(first + i + 1) * D].partition_broadcast(P)).then_inc(loads[name], 16)

            sp.dma_start(cvec[:, :, :], a["cvec"]).then_inc(loads["cvec"], 16)
            for t in range(TILES):
                sp.dma_start(x[:, t, :], (a["ctx"] if t < 2 else a["x"])[(t % 2) * P:(t % 2 + 1) * P, :]).then_inc(loads["x"], 16)
            sp.dma_start(con[:, :], a["con"]).then_inc(loads["const"], 16)
            sp.dma_start(col[:, :], a["col"]).then_inc(loads["const"], 16)
            for l in (0, 1):
                if l == 1:
                    sp.wait_ge(slots_free, RING + 4 * E)
                sp.dma_start(bm, a["b_mod"][l].partition_broadcast(2)).then_inc(loads["bmod"], 16)
                for u in range(12):
                    load_unit(a["w_mod"][l, :, u * UW:(u + 1) * UW])
                    if u % 4 == 3 and u > 3:
                        pass
                for part in range(3):
                    for k in range(4):
                        job_drained(sp, J[f"mod{l}"] + 4 * part + k)
                    sp.dma_start(a["mod_d"][l, :, part * 2 * D:(part + 1) * 2 * D],
                                 mrow[:, part * 2 * D:(part + 1) * 2 * D]).then_inc(loads["modstore"], 16)
                sp.wait_ge(loads["modstore"], 16 * 3 * (l + 1))
                load_mod(l, 0, shsc, "shsc")
                if l == 1:
                    sp.wait_ge(post_done, 8)
                load_mod(l, 2, gmod, "gmod")
                sp.dma_start(lngb[:, 0, :], a["ln1_g"][l].partition_broadcast(P)).then_inc(loads["lngb"], 16)
                sp.dma_start(lngb[:, 1, :], a["ln1_b"][l].partition_broadcast(P)).then_inc(loads["lngb"], 16)
                if l == 0:
                    sp.dma_start(bout[:, :], a["ab_b_out"].partition_broadcast(P)).then_inc(loads["bout"], 16)
                    sp.dma_start(qkvb, a["ab_b_in"][1024:1792].partition_broadcast(P)).then_inc(loads["qkvb"], 16)
                    sp.dma_start(qkg, a["qk_g"].partition_broadcast(P)).then_inc(loads["qkvb"], 16)
                    load_unit(a["ab_w_in"][:, 512:1024])
                    load_unit(a["ab_w_in"][:, 0:512])
                    load_unit(a["ab_w_in"][:, 1024:1536])
                    load_unit(a["ab_w_in"][:, 1536:1792])
                    load_unit(a["ab_w_out"][:, 0:512])
                    load_unit(a["ab_w_out"][:, 512:1024])
                else:
                    sp.dma_start(bout[:, :], a["ml_b_out"].partition_broadcast(P)).then_inc(loads["bout"], 16)
                    job_drained(sp, J["mod1"] + 11)
                    sp.wait_ge(loads["modstore"], 96)
                    sp.dma_start(mask[:, :, :], a["mask"]).then_inc(loads["mlc"], 16)
                    sp.dma_start(sel[0:8, :, :], a["sel"]).then_inc(loads["mlc"], 16)
                    sp.dma_start(mlb[:, :], a["ml_b_in"][1024:3088].partition_broadcast(P)).then_inc(loads["mlc"], 16)
                    sp.dma_start(normg, a["ml_norm_g"].partition_broadcast(P)).then_inc(loads["mlc"], 16)
                    for lo in (0, 512, 1024, 1536, 2048, 2560):
                        load_unit(a["ml_w_in"][:, lo:lo + 512])
                    load_unit(a["ml_w_in"][:, 3072:3088])
                    load_unit(a["ml_w_out"][:, 0:512])
                    load_unit(a["ml_w_out"][:, 512:1024])
                sp.wait_ge(h_freed, 1 + 2 * l)
                load_mod(l, 3, shsc, "shsc")
                for u in range(2):
                    load_unit(a["w_q"][l, :, u * UW:(u + 1) * UW])
                sp.wait_ge(post_done, 4 if l == 0 else 10)
                load_mod(l, 5, gmod, "gmod")
                sp.dma_start(lngb[:, 0, :], a["ln2_g"][l].partition_broadcast(P)).then_inc(loads["lngb"], 16)
                sp.dma_start(lngb[:, 1, :], a["ln2_b"][l].partition_broadcast(P)).then_inc(loads["lngb"], 16)
                sp.dma_start(keys[:, :, :], a["keys"][l]).then_inc(loads["keys"], 16)
                for u in range(2, 4):
                    load_unit(a["w_q"][l, :, u * UW:(u + 1) * UW])
            for n in range(2):
                sp.wait_ge(post_done, 11 + n)
                sp.dma_start(a["out"][n * P:(n + 1) * P, :], x[:, 2 + n, :]).then_inc(stored, 16)
            sp.wait_ge(stored, 32)

        @block.gpsimd
        def _(pool):
            pool.sem_inc(slots_free, RING)
            for p in range(6):
                l = 0 if p < 4 else 1
                if p in (0, 4):
                    pool.wait_ge(eid_ready, 4 if l == 0 else 6)
                with pool.Fori(0, E // STEP) as i:
                    for j in range(STEP):
                        n = p * E + i * STEP + j
                        pool.wait_ge(slots_free, n + 1)
                        pool.sem_inc(pool_step, 1)
                        pool.wait_ge(idx_staged, p * (E // RING) + i * (STEP // RING) + j // RING + 1 + 2 * l)
                        pool.sem_inc(pool_step, 1)
                        pool.indirect_dma_start(
                            out=ring[:, j % RING, :], out_offset=None, in_=a[f"uv{l}"][:, :],
                            in_offset=bass.IndirectOffsetOnAxis(ap=rows_idx[:, j // RING, j % RING:j % RING + 1], axis=0),
                        ).then_inc(row_in[j % RING], 16)

        @block.tensor
        def _(pe):
            unit_no = [0]

            def next_unit():
                n = unit_no[0]
                unit_no[0] += 1
                pe.wait_ge(w_loaded[n % 2], 16 * (n // 2 + 1))
                return w[:, n % 2]

            def group(n, out, pairs):
                if n >= NB:
                    job_drained(pe, n - NB)
                for i, (l, r) in enumerate(pairs):
                    mm = pe.matmul(out, l, r, start=(i == 0), stop=(i == len(pairs) - 1))
                mm.then_inc(bank_full[n % NB], 1)

            def turn(n, parts):
                if n >= NB:
                    job_drained(pe, n - NB)
                for out, src in parts:
                    k = src.shape[0]
                    mm = pe.transpose(out, src, con[0:k, C_ID:C_ID + k])
                mm.then_inc(bank_full[n % NB], 1)

            def modulation(l):
                for u in range(12):
                    n = J[f"mod{l}"] + u
                    wu = next_unit()
                    group(n, bank(n)[0:2, :], [(cvec[:, k, :], wu[:, k, :]) for k in range(KD)])

            def h_transposed(name, tiles, count):
                for i, t in enumerate(tiles):
                    pe.wait_ge(h_ready, count + i + 1)
                    for j in range(2):
                        n = J[name] + 2 * i + j
                        turn(n, [(bank(n)[:, c * P:(c + 1) * P], h[:, t, (4 * j + c) * P:(4 * j + c + 1) * P]) for c in range(4)])

            def by_channel(name, wu, lo, hi):
                for c in range(4):
                    n = J[name] + c
                    group(n, bank(n)[:, 0:hi - lo], [(wu[:, k, c * P:(c + 1) * P], ht[:, k, lo:hi]) for k in range(KD)])

            def by_token(n, wu, t, cols):
                group(n, bank(n)[:, 0:cols], [(ht[:, k, t * P:(t + 1) * P], wu[:, k, 0:cols]) for k in range(KD)])

            def ht_written(last):
                for n in range(last - NB + 1, last + 1):
                    if n >= 0:
                        job_drained(pe, n)

            def router(l, tiles):
                lo, hi = tiles[0] * P, (tiles[-1] + 1) * P
                ht_written(J[f"route{l}"] - 1)
                for c in range(16):
                    if c % 4 == 0:
                        wu = next_unit()
                    n = J[f"route{l}"] + 2 * c
                    group(n, bank(n)[:, 0:hi - lo], [(wu[:, k, (c % 4) * P:(c % 4 + 1) * P], ht[:, k, lo:hi]) for k in range(KD)])
                    if c == 0:
                        pe.wait_ge(loads["keys"], 16 * (l + 1))
                    if n + 1 >= NB:
                        job_drained(pe, n + 1 - NB)
                    job_drained(pe, n)
                    for i in range(len(tiles)):
                        mm = pe.matmul(bank(n + 1)[:, i * NK:(i + 1) * NK], qh[:, c % 2, i * P:(i + 1) * P], keys[:, c, :], start=True, stop=True)
                    mm.then_inc(bank_full[(n + 1) % NB], 1)

            def experts(p):
                def rows(i, first, last):
                    for j in range(STEP):
                        n = p * E + i * STEP + j
                        pe.wait_ge(diag_ready, n + 1)
                        for q in range(2):
                            mm = pe.matmul(expert_sum[:, q * 512:(q + 1) * 512], diag[:, j % NDIAG, :],
                                           ring[:, j % RING, D + q * 512:D + (q + 1) * 512],
                                           start=(first and j == 0), stop=(last and j == STEP - 1))
                        mm.then_inc(slots_free, 1)

                if p > 0:
                    pe.wait_ge(sum_taken, p)
                rows(0, True, False)
                with pe.Fori(1, E // STEP - 1) as i:
                    rows(i, False, False)
                rows(E // STEP - 1, False, True)

            pe.wait_ge(silu_ready, 1)
            pe.wait_ge(loads["const"], 32)
            modulation(0)
            h_transposed("ht1_0", range(TILES), 0)
            ht_written(J["gate"] - 1)
            by_channel("gate", next_unit(), 0, 512)
            by_channel("val", next_unit(), 0, 512)
            wu = next_unit()
            for t in range(TILES):
                by_token(J["q"] + t, wu, t, 512)
            wu = next_unit()
            for t in range(TILES):
                by_token(J["kv"] + t, wu, t, 256)
            for t in range(TILES):
                pe.wait_ge(qk_ready, t + 1)
                n = J["qt"] + t
                turn(n, [(bank(n)[:, c * P:(c + 1) * P], qk[:, t, c * P:(c + 1) * P]) for c in range(4)])
            n = J["kt"]
            turn(n, [(bank(n)[:, t * P:(t + 1) * P], qk[:, t, 512:640]) for t in range(TILES)])

            def scores(i):
                t, g = groups[i]
                nk = 256 if t < 2 else 512
                if i == 0:
                    for m in range(J["qt"], J["kt"] + 1):
                        job_drained(pe, m)
                for c in range(4):
                    n = J[f"att_s{i}"] + c
                    group(n, bank(n)[:, 0:nk], [(qt[64 * g:64 * g + 64, c, t * P:(t + 1) * P], kt[64 * g:64 * g + 64, 0:nk])])

            scores(0)
            for i, (t, g) in enumerate(groups):
                if i + 1 < len(groups):
                    scores(i + 1)
                pe.wait_ge(probs_ready, 4 * (i + 1))
                nkc = 2 if t < 2 else 4
                for kc in range(nkc):
                    n = J[f"att_t{i}"] + kc
                    turn(n, [(bank(n)[:, s * P:(s + 1) * P], probs[i % 2][:, hq, kc * P:(kc + 1) * P]) for s, hq in enumerate((0, 2, 1, 3))])
                n = J[f"att_o{i}"]
                job_drained(pe, n - NB)
                for kc in range(nkc):
                    job_drained(pe, J[f"att_t{i}"] + kc)
                for odd in range(2):
                    for kc in range(nkc):
                        mm = pe.matmul(bank(n)[64 * odd:64 * odd + 64, 0:256], vv[:, kc, g * 64:(g + 1) * 64],
                                       pt[:, kc, 256 * odd:256 * odd + 256], start=(kc == 0), stop=(kc == nkc - 1))
                mm.then_inc(bank_full[n % NB], 1)
            pe.wait_ge(conv_done, 1)
            for t in range(TILES):
                n = J["ut"] + t
                turn(n, [(bank(n)[:, c * P:(c + 1) * P], u[:, c, t * P:(t + 1) * P]) for c in range(CC)])
            pe.wait_ge(un_ready, 1)
            for c in range(CC):
                n = J["ct"] + c
                turn(n, [(bank(n)[:, t * P:(t + 1) * P], ut[:, t, c * P:(c + 1) * P]) for t in range(TILES)])
            ht_written(J["merge0"] - 1)
            for half in range(2):
                wu = next_unit()
                for t in range(TILES):
                    by_token(J["merge0"] + 4 * half + t, wu, t, 512)
            h_transposed("ht2_0", range(TILES), 4)
            router(0, range(TILES))
            for p in range(4):
                experts(p)

            modulation(1)
            h_transposed("ht1_1", range(TILES), 8)
            ht_written(J["mq"] - 1)
            by_channel("mq", next_unit(), 256, 512)
            by_channel("mk", next_unit(), 0, 512)
            for half in range(2):
                wu = next_unit()
                for t in range(TILES):
                    by_token(J["mv"] + 4 * half + t, wu, t, 512)
            for half in range(2):
                wu = next_unit()
                for i in range(2):
                    by_token(J["mo"] + 2 * half + i, wu, 2 + i, 512)
            n = J["mg"]
            job_drained(pe, n - NB)
            wu = next_unit()
            for t in range(TILES):
                for k in range(KD):
                    mm = pe.matmul(bank(n)[:, t * 16:(t + 1) * 16], ht[:, k, t * P:(t + 1) * P], wu[:, k, 0:16], start=(k == 0), stop=(k == KD - 1))
            mm.then_inc(bank_full[n % NB], 1)
            n = J["cum"]
            job_drained(pe, n - NB)
            pe.wait_ge(lf_ready, 1)
            lt, utr, one = con[:, C_LT:C_LT + P], con[:, C_UT:C_UT + P], con[:, C_ONE:C_ONE + P]
            before = {(0, t): list(range(t)) for t in range(TILES)}
            before.update({(1, 0): [1], (1, 1): [], (1, 2): [3, 0, 1], (1, 3): [0, 1]})
            for t in range(TILES):
                for d in range(2):
                    terms = [(utr if d else lt, t)] + [(one, s) for s in before[d, t]]
                    for i, (m, s) in enumerate(terms):
                        mm = pe.matmul(bank(n)[:, t * 8 + 4 * d:t * 8 + 4 * d + 4], m, lf[:, s, 4 * d:4 * d + 4], start=(i == 0), stop=(i == len(terms) - 1))
            mm.then_inc(bank_full[n % NB], 1)
            pe.wait_ge(cg_ready, 1)
            n = J["ctr"]
            turn(n, [(bank(n)[0:8, t * P:(t + 1) * P], cg[:, t, :]) for t in range(TILES)])
            job_drained(pe, n)
            pe.wait_ge(loads["mlc"], 64)
            for m in range(J["mq"], J["mo"]):
                if m >= J["mo"] - NB:
                    job_drained(pe, m)
            for hd in range(MH):
                b0 = J[f"ml{hd}"]
                for d in range(2):
                    group(b0 + d, bank(b0 + d)[:, :], [(sel[0:8, 4 * d + hd, :], ct_[0:8, :])])
                for i in range(2):
                    group(b0 + 2 + i, bank(b0 + 2 + i)[:, :], [(mqt[:, hd, i * P:(i + 1) * P], mkt[:, hd, :])])
                for i in range(2):
                    pe.wait_ge(am_ready, 2 * hd + i + 1)
                    n = b0 + 4 + i
                    turn(n, [(bank(n)[:, kc * P:(kc + 1) * P], am[:, i, kc * P:(kc + 1) * P]) for kc in range(4)])
                for i in range(2):
                    job_drained(pe, b0 + 4 + i)
                    n = b0 + 6 + i
                    group(n, bank(n)[:, 0:MDV], [(att[:, i, kc * P:(kc + 1) * P], mv_[:, kc, hd * MDV:(hd + 1) * MDV]) for kc in range(4)])
            for i in range(2):
                pe.wait_ge(y_ready, i + 1)
                for j in range(2):
                    n = J["yt"] + 2 * i + j
                    turn(n, [(bank(n)[:, c * P:(c + 1) * P], hh[:, i, (4 * j + c) * P:(4 * j + c + 1) * P]) for c in range(4)])
            ht_written(J["merge1"] - 1)
            for half in range(2):
                wu = next_unit()
                for i in range(2):
                    by_token(J["merge1"] + 2 * half + i, wu, 2 + i, 512)
            h_transposed("ht2_1", LAT, 12)
            router(1, LAT)
            for p in (4, 5):
                experts(p)

        @block.scalar
        def _(act):
            stds = [0]

            def copy_out(n, dst, src):
                job_done(act, n)
                drains(act.activation(dst, src, ACT.Copy), n)

            def square_root(cols):
                stds[0] += 1
                act.wait_ge(var_ready, stds[0])
                act.activation(std[:, 0:cols], std[:, 0:cols], ACT.Sqrt).then_inc(std_ready, 1)

            def h_transposed(name, tiles):
                for i, t in enumerate(tiles):
                    for j in range(2):
                        n = J[name] + 2 * i + j
                        copy_out(n, ht[:, 4 * j:4 * j + 4, t * P:(t + 1) * P], bank(n)[:, :].rearrange("p (c n) -> p c n", c=4))

            def router(l, nt):
                for c in range(16):
                    n = J[f"route{l}"] + 2 * c
                    if c >= 2:
                        job_done(act, n - 3)
                    copy_out(n, qh[:, c % 2, 0:nt * P], bank(n)[:, 0:nt * P])
                for i in range(nt):
                    k = (0 if l == 0 else 4) + i
                    act.wait_ge(sc_ready, k + 1)
                    act.activation(sc[:, :, :], sc[:, :, :], ACT.Exp).then_inc(scexp_ready, 1)

            def experts(p):
                with act.Fori(0, E // STEP) as i:
                    for j in range(0, STEP, GROUP):
                        n = p * E + i * STEP + j
                        act.wait_ge(dots_ready, n + GROUP)
                        act.activation(gel[:, j:j + GROUP], dots[:, j:j + GROUP], ACT.Gelu).then_inc(gelu_ready, 1)
                        act.wait_ge(wexp_ready, p * (E // GROUP) + i * (STEP // GROUP) + j // GROUP + 1)
                        for q in range(j, j + GROUP):
                            act.wait_ge(slots_free, p * E + i * STEP + q + 1 + RING - NDIAG)
                            act.activation(diag[:, q % NDIAG, :], ident, ACT.Copy, scale=wexp[:, q:q + 1]).then_inc(diag_ready, 1)
                square_root(4)

            act.wait_ge(loads["cvec"], 16)
            act.activation(cvec[:, :, :], cvec[:, :, :], ACT.Silu).then_inc(silu_ready, 1)
            act.wait_ge(loads["const"], 32)
            square_root(4)
            h_transposed("ht1_0", range(TILES))
            for c in range(CC):
                n = J["gate"] + c
                job_done(act, n)
                drains(act.activation(sg[:, c, :], bank(n)[:, :], ACT.Sigmoid, bias=col[:, Q_GB + c:Q_GB + c + 1]), n)
            square_root(40)
            for t in range(TILES):
                n = J["qt"] + t
                copy_out(n, qt[:, :, t * P:(t + 1) * P], bank(n)[:, :].rearrange("p (c n) -> p c n", c=4))
            copy_out(J["kt"], kt, bank(J["kt"])[:, :])

            def exps(i):
                t, g = groups[i]
                nk = 256 if t < 2 else 512
                if i >= 2:
                    job_done(act, J[f"att_t{i - 2}"] + (1 if groups[i - 2][0] < 2 else 3))
                for c in range(4):
                    n = J[f"att_s{i}"] + c
                    act.wait_ge(rowmax_ready, 4 * i + c + 1)
                    job_done(act, n)
                    k = (4 * i + c) % 8
                    drains(act.activation(probs[i % 2][:, c, 0:nk], bank(n)[:, 0:nk], ACT.Exp, bias=small[:, k:k + 1],
                                          scale=HEAD ** -0.5, accum_out=small[:, 8 + k:9 + k]), n)

            exps(0)
            for i, (t, g) in enumerate(groups):
                if i + 1 < len(groups):
                    exps(i + 1)
                if i >= 1:
                    job_done(act, J[f"att_o{i - 1}"])
                for kc in range(2 if t < 2 else 4):
                    n = J[f"att_t{i}"] + kc
                    copy_out(n, pt[:, kc, :], bank(n)[:, :])
                n = J[f"att_o{i}"]
                copy_out(n, ht[:, 4 + 2 * g:6 + 2 * g, t * P:(t + 1) * P], bank(n)[:, 0:256].rearrange("p (c n) -> p c n", c=2))
            for t in range(TILES):
                n = J["ut"] + t
                copy_out(n, ut[:, t, :], bank(n)[:, :])
            square_root(4)
            for c in range(CC):
                n = J["ct"] + c
                job_done(act, n)
                drains(act.activation(ht[:, c, :], bank(n)[:, :], ACT.Silu, bias=col[:, Q_LB + c:Q_LB + c + 1],
                                      scale=col[:, Q_LG + c:Q_LG + c + 1]), n)
            square_root(4)
            square_root(4)
            h_transposed("ht2_0", range(TILES))
            router(0, TILES)
            for p in range(4):
                experts(p)

            square_root(4)
            h_transposed("ht1_1", range(TILES))
            for c in range(MH):
                n = J["mq"] + c
                job_done(act, n)
                drains(act.activation(mqt[:, c, :], bank(n)[:, 0:256], ACT.Identity, bias=col[:, Q_MQ + c:Q_MQ + c + 1]), n)
            for c in range(MH):
                n = J["mk"] + c
                job_done(act, n)
                drains(act.activation(mkt[:, c, :], bank(n)[:, :], ACT.Identity, bias=col[:, Q_MK + c:Q_MK + c + 1]), n)
            act.wait_ge(o_ready, 4)
            act.activation(og[:, :, :], og[:, :, :], ACT.Sigmoid).then_inc(sig_ready, 1)
            act.wait_ge(lf_a, 1)
            act.activation(le[:, :, :], la[:, :, :], ACT.Exp, scale=-1.0).then_inc(act_step, 1)
            act.wait_ge(act_step, 1)
            act.activation(le[:, :, :], le[:, :, :], ACT.Ln, bias=con[:, C_ONE:C_ONE + 1]).then_inc(lf_e, 1)
            copy_out(J["ctr"], ct_[0:8, :], bank(J["ctr"])[0:8, :])
            for hd in range(MH):
                for d in range(2):
                    for i in range(2):
                        k = 4 * hd + 2 * d + i
                        act.wait_ge(nm_ready, k + 1)
                        act.activation(cm[:, 2 * d + i, :], cm[:, 2 * d + i, :], ACT.Exp, bias=nm[:, 2 * d + i:2 * d + i + 1])
                        act.activation(thr[:, 2 * d + i:2 * d + i + 1], bc[:, 2 + i, 4 * d + hd:4 * d + hd + 1], ACT.Exp,
                                       bias=nm[:, 2 * d + i:2 * d + i + 1], scale=-1.0).then_inc(wm_ready, 1)
                for i in range(2):
                    n = J[f"ml{hd}"] + 4 + i
                    if hd:
                        job_done(act, J[f"ml{hd - 1}"] + 6 + i)
                    copy_out(n, att[:, i, :], bank(n)[:, :])
                for i in range(2):
                    n = J[f"ml{hd}"] + 6 + i
                    copy_out(n, hh[:, i, hd * MDV:(hd + 1) * MDV], bank(n)[:, 0:MDV])
            square_root(8)
            for i in range(2):
                for j in range(2):
                    n = J["yt"] + 2 * i + j
                    copy_out(n, ht[:, 4 * j:4 * j + 4, (2 + i) * P:(3 + i) * P], bank(n)[:, :].rearrange("p (c n) -> p c n", c=4))
            square_root(4)
            square_root(4)
            h_transposed("ht2_1", LAT)
            router(1, 2)
            for p in (4, 5):
                experts(p)

        @block.vector
        def _(dve):
            steps = [0]
            stds = [0]
            hs = [0]
            cnt = {}

            def do(ins):
                steps[0] += 1
                ins.then_inc(dve_step, 1)
                dve.wait_ge(dve_step, steps[0])

            def count(name, by=1):
                cnt[name] = cnt.get(name, 0) + by
                return cnt[name]

            def root(cols):
                stds[0] += 1
                dve.wait_ge(std_ready, stds[0])
                do(dve.reciprocal(rstd[:, 0:cols], std[:, 0:cols]))

            def mean_var(src, k):
                width = src.shape[1]
                parts = max(1, width // 512)
                for i in range(parts):
                    do(dve.bn_stats(stats[:, 6 * i:6 * i + 6], src[:, i * 512:min((i + 1) * 512, width)]))
                do(dve.bn_aggr(mv[:, k, :], stats[:, 0:6 * parts]))

            def var_out(cols, eps=EPS):
                dve.tensor_scalar(std[:, 0:cols], mv[:, 0:cols, 1], eps, None, ALU.add).then_inc(var_ready, 1)

            def normalize(tiles, src, dst):
                for i, t in enumerate(tiles):
                    mean_var(src(t), i)
                var_out(4)
                root(4)
                for i, t in enumerate(tiles):
                    do(dve.tensor_scalar(dst(t), src(t), mv[:, i, 0:1], rstd[:, i:i + 1], ALU.subtract, ALU.mult))

            def modulate(tiles):
                dve.wait_ge(loads["shsc"], 16 * 4 * count("shsc"))
                for s in range(2):
                    do(dve.tensor_scalar(shsc[:, s, 1, :], shsc[:, s, 1, :], 1.0, None, ALU.add))
                normalize(tiles, lambda t: x[:, t, :], lambda t: h[:, t, :])
                for t in tiles:
                    s = t // 2
                    s = 1 - s
                    do(dve.tensor_tensor(h[:, t, :], h[:, t, :], shsc[:, s, 1, :], ALU.mult))
                    dve.tensor_tensor(h[:, t, :], h[:, t, :], shsc[:, s, 0, :], ALU.add).then_inc(h_ready, 1)
                    hs[0] += 1
                dve.wait_ge(h_ready, hs[0])
                dve.sem_inc(h_freed, 1)

            def post_norm(tiles, y):
                for t in tiles:
                    s = 1 - t // 2
                    do(dve.tensor_tensor(h[:, t, :], y(t), gmod[:, s, :], ALU.mult) if y else
                       dve.tensor_tensor(h[:, t, :], h[:, t, :], gmod[:, s, :], ALU.mult))
                    do(dve.scalar_tensor_tensor(out=x[:, t, :], in0=x[:, t, :], scalar=ALPHA, in1=h[:, t, :], op0=ALU.mult, op1=ALU.add))
                normalize(tiles, lambda t: x[:, t, :], lambda t: x[:, t, :])
                for t in tiles:
                    do(dve.tensor_tensor(x[:, t, :], x[:, t, :], lngb[:, 0, :], ALU.mult))
                    dve.tensor_tensor(x[:, t, :], x[:, t, :], lngb[:, 1, :], ALU.add).then_inc(post_done, 1)
                    dve.wait_ge(post_done, count("post"))

            def modulation(l):
                dve.wait_ge(loads["bmod"], 16 * (l + 1))
                for q in range(12):
                    n = J[f"mod{l}"] + q
                    job_done(dve, n)
                    drains(dve.tensor_tensor(mrow[:, q * UW:(q + 1) * UW], bank(n)[0:2, :], bm[:, q * UW:(q + 1) * UW], ALU.add), n)

            def merged(name, tiles):
                dve.wait_ge(loads["bout"], 16 * count("bout"))
                last = {}
                for half in range(2):
                    for i, t in enumerate(tiles):
                        n = J[name] + len(tiles) * half + i
                        job_done(dve, n)
                        drains(dve.tensor_tensor(h[:, t, half * 512:(half + 1) * 512], bank(n)[:, :], bout[:, half * 512:(half + 1) * 512], ALU.add), n)
                for n in range(J[name], J[name] + 2 * len(tiles)):
                    if n >= J[name] + 2 * len(tiles) - NB:
                        job_drained(dve, n)

            def top16(dst_v, dst_i, src, spare):
                do(dve.max(dst_v[:, 0:8], src))
                do(dve.max_index(dst_i[:, 0:8], dst_v[:, 0:8], src))
                do(dve.match_replace(spare, dst_v[:, 0:8], src, LOWEST))
                do(dve.max(dst_v[:, 8:16], spare))

            def router(l, tiles):
                nt = len(tiles)
                for c in range(16):
                    n = J[f"route{l}"] + 2 * c + 1
                    job_done(dve, n)
                    for i in range(nt):
                        v, ix, src = tv[:, i, c, :], ti[:, i, c, :], bank(n)[:, i * NK:(i + 1) * NK]
                        top16(v, ix, src, left[:, 0:NK])
                        ins = dve.max_index(ix[:, 8:16], v[:, 8:16], left[:, 0:NK])
                        if i == nt - 1:
                            drains(ins, n)
                            job_drained(dve, n)
                        else:
                            do(ins)
                for i, t in enumerate(tiles):
                    k = cnt.get("tile", 0)
                    tvp = tv[:, i].rearrange("p (h s) k -> p h s k", s=2)
                    v1 = tvp[:, :, 0, :].unsqueeze(3).broadcast_to([P, PH, TOPK, TOPK])
                    v2 = tvp[:, :, 1, :].unsqueeze(2).broadcast_to([P, PH, TOPK, TOPK])
                    do(dve.tensor_copy(tif, ti[:, i]))
                    do(dve.tensor_tensor(cand, v1, v2, ALU.add))
                    for q in range(PH):
                        row = cand[:, q].rearrange("p i j -> p (i j)")
                        top16(sc[:, q, :], pos[:, q, :], row, left)
                        do(dve.max_index(pos[:, q, 8:16], sc[:, q, 8:16], left))
                    do(dve.tensor_copy(small[:, 0:8], sc[:, :, 0]))
                    dve.tensor_tensor(sc, sc, small[:, 0:8].unsqueeze(2).broadcast_to([P, PH, TOPK]), ALU.subtract).then_inc(sc_ready, 1)
                    tip = tif.rearrange("p (h s) k -> p h s k", s=2)
                    for s, dst in ((0, e1), (1, e2)):
                        if s == 0:
                            do(dve.tensor_scalar(posi, pos, 4, None, ALU.logical_shift_right))
                        else:
                            do(dve.tensor_scalar(posi, pos, TOPK - 1, None, ALU.bitwise_and))
                        do(dve.tensor_copy(posf, posi))
                        hot2 = hot.rearrange("p h i j -> p (h i) j")
                        do(dve.tensor_tensor(hot2, posf.rearrange("p h k -> p (h k)").unsqueeze(2).broadcast_to([P, E, TOPK]),
                                             con[:, C_IOTA:C_IOTA + TOPK].unsqueeze(1).broadcast_to([P, E, TOPK]), ALU.is_equal))
                        do(dve.tensor_tensor(hot, hot, tip[:, :, s, :].unsqueeze(2).broadcast_to([P, PH, TOPK, TOPK]), ALU.mult))
                        do(dve.tensor_reduce(dst, hot, AX.X, ALU.add))
                    do(dve.scalar_tensor_tensor(out=eid[:, i * E:(i + 1) * E].rearrange("p (h k) -> p h k", h=PH), in0=e1, scalar=float(NK), in1=e2, op0=ALU.mult, op1=ALU.add))
                    dve.wait_ge(scexp_ready, count("tile"))
                    do(dve.tensor_reduce(small[:, 8:16], sc, AX.X, ALU.add))
                    do(dve.reciprocal(small[:, 8:16], small[:, 8:16]))
                    dve.tensor_tensor(gates[:, i * E:(i + 1) * E].rearrange("p (h k) -> p h k", h=PH), sc,
                                      small[:, 8:16].unsqueeze(2).broadcast_to([P, PH, TOPK]), ALU.mult).then_inc(eid_ready, 1)
                    dve.wait_ge(eid_ready, cnt["tile"])
                if l == 0:
                    do(dve.memset(eid[:, TILES * E:TILES * E + 2 * RING], 0))

            def stage_rows(first, half):
                dve.tensor_copy(rows_idx[:, half, :], eid[:, bass.ds(first, RING)]).then_inc(idx_staged, 1)

            def experts(p, i_tile, t):
                if p in (0, 4):
                    stage_rows(0, 0)
                    stage_rows(RING, 1)
                with dve.Fori(0, E // STEP) as i:
                    for j in range(STEP):
                        dve.wait_ge(row_in[j % RING], (p * (E // RING) + i * (STEP // RING) + j // RING + 1) * 16)
                        r = ring[:, j % RING, 0:D]
                        dve.tensor_tensor_reduce(out=r, in0=r, in1=h[:, t, :], scale=1.0, scalar=0.0, op0=ALU.mult,
                                                 op1=ALU.add, accum_out=dots[:, j:j + 1]).then_inc(dots_ready, 1)
                        if j % GROUP == GROUP - 1:
                            dve.wait_ge(gelu_ready, p * (E // GROUP) + i * (STEP // GROUP) + j // GROUP + 1)
                            f = j - GROUP + 1
                            dve.tensor_tensor(wexp[:, f:j + 1], gel[:, f:j + 1],
                                              gates[:, bass.ds(i_tile * E + i * STEP + f, GROUP)], ALU.mult).then_inc(wexp_ready, 1)
                        if j % RING == RING - 1:
                            stage_rows(i_tile * E + i * STEP + (j // RING + 2) * RING, j // RING)
                dve.wait_ge(slots_free, RING + (p + 1) * E)
                s = 1 - t // 2
                do(dve.tensor_tensor(h[:, t, :], expert_sum[:, :], gmod[:, s, :], ALU.mult))
                dve.sem_inc(sum_taken, 1)
                do(dve.scalar_tensor_tensor(out=x[:, t, :], in0=x[:, t, :], scalar=ALPHA, in1=h[:, t, :], op0=ALU.mult, op1=ALU.add))
                normalize([t], lambda q: x[:, q, :], lambda q: x[:, q, :])
                do(dve.tensor_tensor(x[:, t, :], x[:, t, :], lngb[:, 0, :], ALU.mult))
                dve.tensor_tensor(x[:, t, :], x[:, t, :], lngb[:, 1, :], ALU.add).then_inc(post_done, 1)
                dve.wait_ge(post_done, count("post"))

            do(dve.memset(mv[:, :, :], 0.0))
            do(dve.memset(rstd[:, :], 1.0))
            modulation(0)
            dve.wait_ge(loads["x"], 64)
            dve.wait_ge(loads["const"], 32)
            modulate(range(TILES))
            for k in range(12):
                if k >= 12 - NB:
                    job_drained(dve, J["mod0"] + k)
            dve.wait_ge(loads["modstore"], 48)
            do(dve.memset(cin, 0.0))
            for c in range(CC):
                n = J["val"] + c
                job_done(dve, n)
                job_drained(dve, J["gate"] + c)
                drains(dve.scalar_tensor_tensor(
                    out=cin[:, c, :, PAD:PAD + 256], in0=bank(n)[:, :].rearrange("p (s n) -> p s n", s=2), scalar=col[:, Q_VB + c:Q_VB + c + 1],
                    in1=sg[:, c, :].rearrange("p (s n) -> p s n", s=2), op0=ALU.add, op1=ALU.mult), n)
            dve.wait_ge(loads["qkvb"], 32)
            for t in range(TILES):
                n = J["q"] + t
                job_done(dve, n)
                drains(dve.tensor_tensor(qk[:, t, 0:512], bank(n)[:, :], qkvb[:, 0:512], ALU.add), n)
            for t in range(TILES):
                n = J["kv"] + t
                job_done(dve, n)
                do(dve.tensor_tensor(qk[:, t, 512:640], bank(n)[:, 0:128], qkvb[:, 512:640], ALU.add))
                drains(dve.tensor_tensor(vv[:, t, :], bank(n)[:, 128:256], qkvb[:, 640:768], ALU.add), n)
            for t in range(TILES):
                job_drained(dve, J["q"] + t)
                job_drained(dve, J["kv"] + t)

            def heads(ap):
                return ap.rearrange("p (h d) -> p h d", d=HEAD)

            NH = NQH + NKV
            for t in range(TILES):
                do(dve.tensor_tensor(tmp1, qk[:, t, :], qk[:, t, :], ALU.mult))
                do(dve.tensor_reduce(std[:, NH * t:NH * (t + 1)], heads(tmp1), AX.X, ALU.add))
            dve.tensor_scalar(std[:, :], std[:, :], 1.0 / HEAD, EPS, ALU.mult, ALU.add).then_inc(var_ready, 1)
            root(40)
            for t in range(TILES):
                q = heads(qk[:, t, :])
                do(dve.tensor_tensor(q, q, rstd[:, NH * t:NH * (t + 1)].unsqueeze(2).broadcast_to([P, NH, HEAD]), ALU.mult))
                last = dve.tensor_tensor(qk[:, t, :], qk[:, t, :], qkg, ALU.mult)
                if t in LAT:
                    do(last)
                    cs = con[:, C_COS + (t - 2) * HEAD:C_COS + (t - 1) * HEAD]
                    sn = con[:, C_SIN + (t - 2) * HEAD:C_SIN + (t - 1) * HEAD].rearrange("p (a b f) -> p a b f", a=2, b=2)
                    do(dve.tensor_tensor(heads(tmp1), q, cs.unsqueeze(1).broadcast_to([P, NH, HEAD]), ALU.mult))
                    q4 = qk[:, t, :].rearrange("p (h a b f) -> p h a b f", a=2, b=2, f=16)
                    t4 = tmp2.rearrange("p (h a b f) -> p h a b f", a=2, b=2, f=16)
                    for b in range(2):
                        do(dve.tensor_tensor(t4[:, :, :, b, :], q4[:, :, :, 1 - b, :],
                                             sn[:, :, b, :].unsqueeze(1).broadcast_to([P, NH, 2, 16]), ALU.mult))
                    last = dve.tensor_tensor(qk[:, t, :], tmp1, tmp2, ALU.add)
                last.then_inc(qk_ready, 1)
                dve.wait_ge(qk_ready, t + 1)

            def row_max(i):
                t, g = groups[i]
                nk = 256 if t < 2 else 512
                for c in range(4):
                    n = J[f"att_s{i}"] + c
                    k = (4 * i + c) % 8
                    job_done(dve, n)
                    do(dve.tensor_reduce(small[:, 16 + k:17 + k], bank(n)[:, 0:nk], AX.X, ALU.max))
                    dve.tensor_scalar(small[:, k:k + 1], small[:, 16 + k:17 + k], -(HEAD ** -0.5), None, ALU.mult).then_inc(rowmax_ready, 1)

            row_max(0)
            for i, (t, g) in enumerate(groups):
                if i + 1 < len(groups):
                    row_max(i + 1)
                nk = 256 if t < 2 else 512
                for c in range(4):
                    k = (4 * i + c) % 8
                    job_drained(dve, J[f"att_s{i}"] + c)
                    do(dve.reciprocal(small[:, 24 + k:25 + k], small[:, 8 + k:9 + k]))
                    dve.tensor_scalar(probs[i % 2][:, c, 0:nk], probs[i % 2][:, c, 0:nk], small[:, 24 + k:25 + k], None, ALU.mult).then_inc(probs_ready, 1)
            job_done(dve, J["att_o7"])
            for c in range(CC):
                job_drained(dve, J["val"] + c)
            for k in range(TAPS):
                for c in range(CC):
                    src = cin[:, c, :, k:k + 256]
                    dst = u[:, c, :].rearrange("p (s n) -> p s n", s=2)
                    tap = col[:, Q_CW + c * TAPS + k:Q_CW + c * TAPS + k + 1]
                    if k == 0:
                        do(dve.tensor_scalar(dst, src, tap, col[:, Q_CB + c:Q_CB + c + 1], ALU.mult, ALU.add))
                    else:
                        do(dve.scalar_tensor_tensor(out=dst, in0=src, scalar=tap, in1=dst, op0=ALU.mult, op1=ALU.add))
            dve.sem_inc(conv_done, 1)
            for t in range(TILES):
                job_drained(dve, J["ut"] + t)
            normalize(range(TILES), lambda t: ut[:, t, :], lambda t: ut[:, t, :])
            dve.sem_inc(un_ready, 1)
            merged("merge0", range(TILES))
            dve.wait_ge(loads["gmod"], 32)
            dve.wait_ge(loads["lngb"], 32)
            post_norm(range(TILES), None)
            modulate(range(TILES))
            router(0, range(TILES))
            dve.wait_ge(loads["gmod"], 64)
            dve.wait_ge(loads["lngb"], 64)
            for p in range(4):
                experts(p, p, p)

            modulation(1)
            modulate(range(TILES))
            dve.wait_ge(loads["mlc"], 64)
            for half in range(2):
                for t in range(TILES):
                    n = J["mv"] + 4 * half + t
                    job_done(dve, n)
                    drains(dve.tensor_tensor(mv_[:, t, half * 512:(half + 1) * 512], bank(n)[:, :], mlb[:, half * 512:(half + 1) * 512], ALU.add), n)
            job_done(dve, J["ht1_1"] + 7)
            for half in range(2):
                for i in range(2):
                    n = J["mo"] + 2 * half + i
                    job_done(dve, n)
                    drains(dve.tensor_tensor(og[:, i, half * 512:(half + 1) * 512], bank(n)[:, :], mlb[:, 1024 + half * 512:1024 + (half + 1) * 512], ALU.add), n)
            for m in range(4):
                job_drained(dve, J["mo"] + m)
                dve.sem_inc(o_ready, 1)
            n = J["mg"]
            job_done(dve, n)
            drains(dve.tensor_tensor(gt[:, :, :], bank(n)[:, 0:64].rearrange("p (t n) -> p t n", t=TILES),
                                     mlb[:, 2048:2064].unsqueeze(1).broadcast_to([P, TILES, 16]), ALU.add), n)
            job_drained(dve, n)
            gt5 = gt.rearrange("p t (d k h) -> p t d k h", d=2, k=2)
            f = gt5[:, :, :, 1, :]
            ig = gt5[:, :, :, 0, :]
            v4 = lambda ap: ap.rearrange("p t (d h) -> p t d h", d=2)
            do(dve.tensor_scalar(v4(lf), f, -1.0, None, ALU.mult))
            dve.tensor_tensor(v4(la), v4(lf), f, ALU.max).then_inc(lf_a, 1)
            dve.wait_ge(lf_a, 1)
            do(dve.tensor_scalar(v4(lf), f, 0.0, None, ALU.min))
            dve.wait_ge(lf_e, 1)
            dve.tensor_tensor(lf, lf, le, ALU.subtract).then_inc(lf_ready, 1)
            n = J["cum"]
            job_done(dve, n)
            drains(dve.tensor_copy(bc[:, :, :], bank(n)[:, 0:32].rearrange("p (t n) -> p t n", t=TILES)), n)
            job_drained(dve, n)
            dve.tensor_tensor(v4(cg), ig, v4(bc), ALU.subtract).then_inc(cg_ready, 1)
            for hd in range(MH):
                b0 = J[f"ml{hd}"]
                for d in range(2):
                    job_done(dve, b0 + d)
                    for i in range(2):
                        r = 2 * d + i
                        ins = dve.tensor_tensor(cm[:, r, :], bank(b0 + d)[:, :], mask[:, r, :], ALU.add)
                        if i == 1:
                            drains(ins, b0 + d)
                            job_drained(dve, b0 + d)
                        else:
                            do(ins)
                        do(dve.tensor_reduce(den[:, r:r + 1], cm[:, r, :], AX.X, ALU.max))
                        dve.tensor_scalar(nm[:, r:r + 1], den[:, r:r + 1], 0.0, -1.0, ALU.max, ALU.mult).then_inc(nm_ready, 1)
                for i in range(2):
                    n = b0 + 2 + i
                    job_done(dve, n)
                    for d in range(2):
                        r = 2 * d + i
                        dve.wait_ge(wm_ready, 4 * hd + r + 1 if d == 1 else 4 * hd + i + 1)
                        ins = dve.tensor_tensor_reduce(out=cm[:, r, :], in0=cm[:, r, :], in1=bank(n)[:, :], scale=MDQ ** -0.5, scalar=0.0,
                                                       op0=ALU.mult, op1=ALU.add, accum_out=den[:, r:r + 1])
                        if d == 1:
                            drains(ins, n)
                            job_drained(dve, n)
                        else:
                            do(ins)
                        do(dve.tensor_scalar(den[:, 4 + r:5 + r], den[:, r:r + 1], -1.0, None, ALU.mult))
                        do(dve.tensor_tensor(den[:, r:r + 1], den[:, r:r + 1], den[:, 4 + r:5 + r], ALU.max))
                        do(dve.tensor_tensor(den[:, r:r + 1], den[:, r:r + 1], thr[:, r:r + 1], ALU.max))
                        do(dve.reciprocal(den[:, 4 + r:5 + r], den[:, r:r + 1]))
                    do(dve.tensor_scalar(cm[:, i, :], cm[:, i, :], den[:, 4 + i:5 + i], None, ALU.mult))
                    if hd:
                        job_done(dve, J[f"ml{hd - 1}"] + 4 + i)
                    dve.scalar_tensor_tensor(out=am[:, i, :], in0=cm[:, 2 + i, :], scalar=den[:, 6 + i:7 + i], in1=cm[:, i, :],
                                             op0=ALU.mult, op1=ALU.add).then_inc(am_ready, 1)
            for i in range(2):
                for hd in range(MH):
                    job_drained(dve, J[f"ml{hd}"] + 6 + i)
            for i in range(2):
                for hd in range(MH):
                    mean_var(hh[:, i, hd * MDV:(hd + 1) * MDV], 4 * i + hd)
            var_out(8)
            root(8)
            dve.wait_ge(sig_ready, 1)
            for i in range(2):
                for hd in range(MH):
                    k = 4 * i + hd
                    y = hh[:, i, hd * MDV:(hd + 1) * MDV]
                    do(dve.tensor_scalar(y, y, mv[:, k, 0:1], rstd[:, k:k + 1], ALU.subtract, ALU.mult))
                do(dve.tensor_tensor(hh[:, i, :], hh[:, i, :], normg, ALU.mult))
                dve.tensor_tensor(hh[:, i, :], hh[:, i, :], og[:, i, :], ALU.mult).then_inc(y_ready, 1)
            merged("merge1", LAT)
            dve.wait_ge(loads["gmod"], 96)
            dve.wait_ge(loads["lngb"], 96)
            post_norm(LAT, None)
            modulate(LAT)
            router(1, LAT)
            dve.wait_ge(loads["gmod"], 128)
            dve.wait_ge(loads["lngb"], 128)
            for p in (4, 5):
                experts(p, p - 4, p - 2)


def constants():
    f = np.float32
    i = np.arange(P)
    con = np.zeros((P, C_END), f)
    con[:, C_ID:C_ID + P] = np.eye(P, dtype=f)
    con[:, C_LT:C_LT + P] = i[:, None] <= i[None, :]
    con[:, C_UT:C_UT + P] = i[:, None] >= i[None, :]
    con[:, C_ONE:C_ONE + P] = 1.0
    inv = (10000.0 ** (-np.arange(16, dtype=f) / f(16))).astype(f)
    tok = np.arange(2 * P)
    row, colp = (tok // 64).astype(f), (tok % 64).astype(f)
    ang = np.stack([row[:, None] * inv, colp[:, None] * inv], 1)
    cos = np.stack([np.cos(ang), np.cos(ang)], 2).reshape(2, P, HEAD)
    sin = np.stack([-np.sin(ang), np.sin(ang)], 2).reshape(2, P, HEAD)
    for t in range(2):
        con[:, C_COS + t * HEAD:C_COS + (t + 1) * HEAD] = cos[t]
        con[:, C_SIN + t * HEAD:C_SIN + (t + 1) * HEAD] = sin[t]
    con[:, C_IOTA:C_IOTA + TOPK] = np.arange(TOPK)
    mask = np.full((P, 4, 4, P), NEG, f)
    for d in range(2):
        for t in range(2):
            mask[:, 2 * d + t, 0:2] = 0.0
            q, s = i[:, None], i[None, :]
            mask[:, 2 * d + t, 2 + t] = np.where(s <= q if d == 0 else s >= q, 0.0, NEG)
            if t == 1 and d == 0:
                mask[:, 1, 2] = 0.0
            if t == 0 and d == 1:
                mask[:, 2, 3] = 0.0
    sel = np.zeros((8, 8, P), f)
    for r in range(8):
        sel[r, r] = 1.0
    return con, mask.reshape(P, 4, 512), sel


def kernel(**inputs):
    import concourse.bacc as _bacc
    from concourse.bass_utils import run_bass_kernel_spmd as _run

    v = {k: np.asarray(b) for k, b in inputs.items()}
    con, mask, sel = constants()

    def chunks(b, n):
        return b.reshape(n, P).T

    order = np.arange(1792)
    order[1024:1536] = 1024 + np.concatenate([np.arange(HEAD) + HEAD * (c + 4 * g) for c in range(4) for g in range(2)])
    b_in, mb = v["ab_b_in"][0][order], v["ml_b_in"][0]
    col = np.concatenate([
        chunks(b_in[0:512], 4), chunks(b_in[512:1024], 4), chunks(v["ab_conv_b"][0], 4), chunks(v["ab_conv_ln_g"][0], 4),
        chunks(v["ab_conv_ln_b"][0], 4), v["ab_conv_w"][0].reshape(TAPS, 4, P).transpose(2, 1, 0).reshape(P, 4 * TAPS),
        chunks(mb[0:512], 4), chunks(mb[512:1024], 4)], axis=1)
    keys = np.stack([v["peer_k1"], v["peer_k2"]], 2)
    arrays = {
        "x": v["x"][0], "ctx": v["ctx"][0],
        "cvec": np.stack([v["c"][0], v["c_ctx"]]).reshape(2, KD, P).transpose(2, 1, 0),
        "con": con, "mask": mask, "sel": sel, "col": col,
        "w_mod": v["w_mod"], "b_mod": v["b_mod"], "ln1_g": v["ln1_g"], "ln1_b": v["ln1_b"], "ln2_g": v["ln2_g"], "ln2_b": v["ln2_b"],
        "ab_w_in": v["ab_w_in"][0][:, order], "ab_b_in": b_in,
        "qk_g": np.concatenate([np.tile(v["ab_q_norm_g"][0], NQH), np.tile(v["ab_k_norm_g"][0], NKV)]),
        "ab_w_out": v["ab_w_out"][0], "ab_b_out": v["ab_b_out"][0],
        "ml_w_in": v["ml_w_in"][0], "ml_b_in": mb, "ml_norm_g": v["ml_norm_g"][0], "ml_w_out": v["ml_w_out"][0], "ml_b_out": v["ml_b_out"][0],
        "w_q": v["peer_w_q"], "keys": keys.transpose(0, 4, 1, 2, 3).reshape(2, P, 16, NK),
        "uv0": np.concatenate([v["peer_u"][0], v["peer_v"][0]], axis=1), "uv1": np.concatenate([v["peer_u"][1], v["peer_v"][1]], axis=1),
    }
    nc = _bacc.Bacc("TRN2", target_bir_lowering=False, num_devices=1)
    given, aps = {}, {}
    for name, b in arrays.items():
        b = np.ascontiguousarray(b)
        given[f"in_{name}"] = b
        aps[name] = nc.dram_tensor(f"in_{name}", b.shape, mybir.dt.from_np(b.dtype), kind="ExternalInput").ap()
    aps["mod_d"] = nc.dram_tensor("mod_d", (2, 2, 6 * D), F32, kind="Internal").ap()
    aps["out"] = nc.dram_tensor("out_x", (2 * P, D), F32, kind="ExternalOutput").ap()
    build(nc, aps, False)
    r = _run(nc, [given], core_ids=[0])
    return r.results[0]["out_x"].reshape(1, 2 * P, D)
```

```python
import concourse.bass as bass
import numpy as np
from concourse import mybir
from contextlib import ExitStack

F32 = mybir.dt.float32
U32 = mybir.dt.uint32
ALU = mybir.AluOpType
ACT = mybir.ActivationFunctionType
AX = mybir.AxisListType

P = 128
D = 1024
KD = D // P
TILES = 4
LAT = (2, 3)
EPS = 1e-6
ALPHA = 4 ** 0.25
HEAD = 64
NQH, NKV = 8, 2
QKW = (NQH + NKV) * HEAD
CC = 4
TAPS = 31
PAD = TAPS // 2
CW = 256 + 2 * PAD
UW = 256
ST = 256
NS = 2
MH, MDQ, MDV = 4, 128, 256
PH, NK, TOPK = 8, 128, 16
E = PH * TOPK
NB = 6
RING = 8
GPT = E // RING
GROUP = 2
NDIAG = RING
WIDE, DEEP = 4, 4
NCAND = WIDE * TOPK + (TOPK - WIDE) * DEEP
NEG = -1.0e30
LOWEST = -3.0e38

C_ID, C_LT, C_UT, C_ONE, C_COS, C_SIN, C_IOTA, C_END = 0, 128, 256, 384, 512, 640, 768, 784
Q_VB, Q_GB, Q_CB, Q_LG, Q_LB, Q_CW, Q_MQ, Q_MK, Q_END = 0, 4, 8, 12, 16, 20, 144, 148, 152


UNIT_STAGES = ("gate", "val", "q", "mq", "mk", "merge", "mv", "mo")
MODS = 6 * D // UW
CONV_PIECES = 8


def kind(name):
    return name if name in ("ln1", "ln2") else name.rstrip("0123456789")


def part(st):
    return int(st[0][len(kind(st[0])):])


def order():
    def parts(name, n, l, s):
        return [(f"{name}{i}", l, s) for i in range(n)]

    def mixer0(s):
        o = [("ln1", 0, s)] + parts("gate", 2, 0, s) + parts("val", 2, 0, s) + parts("q", 2, 0, s) + [("kv", 0, s), ("rope", 0, s)]
        o += parts("att", 4, 0, s)
        per = (MODS - 8) // CONV_PIECES
        for c in range(CONV_PIECES):
            o += [("mod", 0, 8 + per * c + k) for k in range(per)] if s == 0 else []
            o.append((f"conv{c}", 0, s))
        o += [("chan", 0, s)] + parts("merge", 4, 0, s) + [("post", 0, s), ("ln2", 0, s)]
        return o + parts("r", 8, 0, s)

    def picks(t):
        return [("picka", t // 4, t), ("pickb", t // 4, t)]

    walk = [("mod", 0, k) for k in range(8)] + mixer0(0) + picks(0) + [("begin", 0, 0)]
    q = 0

    def experts(k):
        nonlocal q
        walk.append(("experts", q, k))
        q += k

    def spread(stages, groups):
        total, done, went = sum(COST[kind(st[0])] for st in stages), 0, 0
        for st in stages:
            walk.append(st)
            went += COST[kind(st[0])]
            k = round(went / total * groups) - done
            if k > 0:
                experts(k)
                done += k

    experts(1)
    walk.append(picks(1)[0])
    experts(1)
    walk.append(picks(1)[1])
    experts(1)
    spread(mixer0(1) + picks(2), 2 * GPT - 5)
    experts(2)
    spread(picks(3) + [("mod", 1, k) for k in range(MODS)] + [("ln1", 1, 0)]
           + parts("mk", 2, 1, 0) + parts("mv", 4, 1, 0) + [("mg", 1, 0)], 2 * GPT)
    walk += [("ln1", 1, 1)] + parts("mq", 2, 1, 1) + parts("mk", 2, 1, 1) + parts("mv", 4, 1, 1) + parts("mo", 4, 1, 1) + [("mg", 1, 1)]
    walk += [("gatesum", 1, 1), ("decay0", 1, 1)]
    for hd in range(MH):
        walk += ([(f"decay{hd + 1}", 1, 1)] if hd < MH - 1 else []) + [(f"head{hd}", 1, 1)]
    walk += [("heads", 1, 1)] + parts("merge", 4, 1, 1) + [("post", 1, 1), ("ln2", 1, 1)] + parts("r", 8, 1, 1)
    walk += picks(4) + [("begin", 1, 0)]
    experts(1)
    walk.append(picks(5)[0])
    experts(1)
    walk.append(picks(5)[1])
    experts(2 * GPT - 2)
    return walk


COST = {"ln1": 14, "gate": 6, "val": 6, "q": 6, "kv": 8, "rope": 14, "att": 13, "conv": 7, "chan": 12, "merge": 6,
        "post": 16, "ln2": 14, "r": 10, "picka": 15, "pickb": 16, "mod": 5, "mk": 6, "mv": 6, "mg": 5}


def sooner(walk):
    out = []
    for st in walk:
        if st[0] == "experts" and out and out[-1][0] != "experts" and (kind(out[-1][0]) in UNIT_STAGES or out[-1][0] in ("mod", "kv", "mg")):
            last = out.pop()
            out += [("experts", st[1], 1), last]
            if st[2] > 1:
                out.append(("experts", st[1] + 1, st[2] - 1))
        else:
            out.append(st)
    return out


def att_jobs(s):
    return 2 if s == 0 else 4


def plan(walk):
    base, n, units = {}, 0, []
    for st in walk:
        name, l, s = st
        k = kind(name)
        count = {"mod": 1, "ln1": 4, "ln2": 4, "kv": 2, "rope": 3, "chan": 4, "mg": 1, "r": 4, "gatesum": 2, "decay": 2,
                 "head": 6, "heads": 4}.get(k, 2 if k in UNIT_STAGES else 0)
        if k == "att":
            i = part(st)
            count = (4 if i == 0 else 0) + (4 if i < 3 else 0) + att_jobs(s) + 1
        base[st] = n
        n += count
        if k in UNIT_STAGES or k in ("mod", "kv", "mg"):
            units.append(n - 1)
        elif k == "r":
            units.append(base[st] + 1)
    return base, units


def att_base(J, s, i):
    def at(k):
        return J[f"att{k}", 0, s]
    score = at(0) if i == 0 else at(i - 1) + (4 if i == 1 else 0)
    turned = at(i) + (4 if i == 0 else 0) + (4 if i < 3 else 0)
    return score, turned, turned + att_jobs(s)


def expert_runs(q, count):
    runs, end = [], q + count
    while q < end:
        k = q % GPT
        pairs = (min(end - q, GPT - 2 - k)) // 2 if q % 2 == 0 and 0 < k < GPT - 2 else 0
        if pairs >= 2:
            runs.append((q, pairs))
            q += 2 * pairs
        else:
            runs.append((q, 0))
            q += 1
    return runs


def build(nc, a):
    WALK = order()
    J, UNIT_LAST = plan(WALK)
    AHEAD = sooner(WALK)
    for lo, hi in (("chan", "ln2"),):
        between = WALK[WALK.index((lo, 0, 1)):WALK.index((hi, 0, 1))]
        assert not any(st[0] == "experts" and st[1] // GPT != (st[1] + st[2]) // GPT for st in between)
    first_ends = next(i for i, st in enumerate(AHEAD) if st[0] == "experts" and st[1] + st[2] >= GPT)
    assert first_ends < AHEAD.index(("chan", 0, 1)) < AHEAD.index(("ln2", 0, 1)) < next(
        i for i, st in enumerate(AHEAD) if st[0] == "experts" and st[1] + st[2] >= 2 * GPT)
    with ExitStack() as ctx:
        def sb(name, shape, dt=F32):
            return ctx.enter_context(nc.sbuf_tensor(name, shape, dt))

        def sem(name):
            return ctx.enter_context(nc.semaphore(name))

        banks = [ctx.enter_context(nc.psum_tensor(f"bank{i}", [P, 512], F32)) for i in range(NB)]
        expert_sum = ctx.enter_context(nc.psum_tensor("expert_sum", [P, D], F32))

        x = sb("x", [P, TILES, D])
        h = sb("h", [P, TILES, D])
        ht = sb("ht", [P, KD, ST])
        rows = sb("rows", [P, 2, D])
        gmod = sb("gmod", [P, 2, D])
        lngb = sb("lngb", [P, 2, D])
        w = sb("w", [P, 2, KD, UW])
        con = sb("con", [P, C_END])
        col = sb("col", [P, Q_END])
        cvec = sb("cvec", [P, KD, 2])
        kt = sb("kt", [P, TILES * P])
        vv = sb("vv", [P, TILES, P])
        stats = sb("stats", [P, 12])
        mv = sb("mv", [P, 8, 2])
        std = sb("std", [P, 20])
        rstd = sb("rstd", [P, 20])
        gates = sb("gates", [P, TILES * E])
        eid = sb("eid", [P, TILES * E], U32)
        rows_idx = sb("rows_idx", [P, 2, RING], U32)
        dots = sb("dots", [P, 2 * RING])
        gel = sb("gel", [P, 2 * RING])
        wexp = sb("wexp", [P, 2 * RING])
        diag = sb("diag", [P, NDIAG, P])
        small = sb("small", [P, 32])
        gt = sb("gt", [P, TILES, 16])
        lf = sb("lf", [P, TILES, 8])
        la = sb("la", [P, TILES, 8])
        le = sb("le", [P, TILES, 8])
        bc = sb("bc", [P, TILES, 8])
        cg = sb("cg", [P, TILES, 8])
        nm = sb("nm", [P, 8])
        thr = sb("thr", [P, 8])
        den = sb("den", [P, 8])
        top = sb("top", [P, 8])
        ring_all = sb("ring", [P, RING * 2 * D])
        ring = ring_all[:, :].rearrange("p (r n) -> p r n", r=RING)
        AREA = 11000
        arena = sb("arena", [P, AREA])
        at, where = 0, arena

        def cut(n):
            nonlocal at
            at += n
            assert at <= (AREA if where is arena else RING * 2 * D), at
            return where[:, at - n:at]

        ident = con[:, C_ID:C_ID + P]
        bm0 = ring_all[0:2, 0:6 * D]
        bm1 = arena[0:2, 8208:8208 + 2 * D]
        sg = cut(1024).rearrange("p (c n) -> p c n", c=CC)
        ut = sg.rearrange("p c n -> p (c n)").rearrange("p (t n) -> p t n", t=NS)
        u = cut(1024).rearrange("p (c n) -> p c n", c=CC)
        pr1 = arena[:, 0:2048].rearrange("p (c n) -> p c n", c=4)
        pr0 = cut(2048).rearrange("p (c n) -> p c n", c=4)
        probs = (pr0, pr1)
        pt_ = cut(2048)
        pt = pt_.rearrange("p (c n) -> p c n", c=4)
        tmp1, tmp2 = pt_[:, 0:QKW], pt_[:, QKW:2 * QKW]
        cin = cut(CC * CW).rearrange("p (c n) -> p c n", c=CC)
        qk = cut(NS * QKW).rearrange("p (t n) -> p t n", t=NS)
        qt = cut(1024).rearrange("p (c n) -> p c n", c=4)
        assert at <= AREA - 1408
        qkvb, qkg = arena[:, AREA - 1408:AREA - 640], arena[:, AREA - 640:AREA]
        at = 0
        keys = cut(2048).rearrange("p (c n) -> p c n", c=16)
        qh = cut(512).rearrange("p (s n) -> p s n", s=2)
        tv = cut(512).rearrange("p (t c k) -> p t c k", t=NS, c=16)
        ti = cut(512).bitcast(U32).rearrange("p (t c k) -> p t c k", t=NS, c=16)
        tif = cut(256).rearrange("p (c k) -> p c k", c=16)
        cand = cut(PH * NCAND).rearrange("p (h n) -> p h n", h=PH)
        hot = cut(2048).rearrange("p (h i j) -> p h i j", h=PH, i=TOPK)
        sc = cut(128).rearrange("p (h k) -> p h k", h=PH)
        pos = cut(128).bitcast(U32).rearrange("p (h k) -> p h k", h=PH)
        high = cut(128).bitcast(U32).rearrange("p (h k) -> p h k", h=PH)
        first = cut(128).rearrange("p (h k) -> p h k", h=PH)
        second = cut(128).rearrange("p (h k) -> p h k", h=PH)
        e1 = cut(128).rearrange("p (h k) -> p h k", h=PH)
        e2 = cut(128).rearrange("p (h k) -> p h k", h=PH)
        left = cut(256)
        assert at <= AREA - 1408
        at = 0
        mkt = cut(2048).rearrange("p (h n) -> p h n", h=MH)
        mval = cut(4096).rearrange("p (t n) -> p t n", t=TILES)
        mlb = cut(2064)
        at, where = 0, ring_all
        mqt = cut(1024).rearrange("p (h n) -> p h n", h=MH)
        mask = cut(2048).rearrange("p (r n) -> p r n", r=4)
        sel = cut(1024).rearrange("p (r n) -> p r n", r=8)
        cms = [cut(2048).rearrange("p (r n) -> p r n", r=4) for _ in range(2)]
        am = cut(1024).rearrange("p (r n) -> p r n", r=2)
        att = cut(1024).rearrange("p (r n) -> p r n", r=2)
        ct_ = cut(512)
        normg = cut(1024)
        og = h[:, 0:2, :]
        hh = h[:, 2:4, :]

        bank_full = [sem(f"bank_full{i}") for i in range(NB)]
        bank_drained = [sem(f"bank_drained{i}") for i in range(NB)]
        w_loaded = [sem(f"w_loaded{i}") for i in range(2)]
        loads = {n: sem(f"in_{n}") for n in (
            "con", "x", "cvec", "bmod", "modstore", "rows", "gmod", "lngb", "qkvb", "keys", "mlb", "mlc")}
        dve_step = sem("dve_step")
        act_step = sem("act_step")
        pool_step = sem("pool_step")
        silu_ready = sem("silu_ready")
        h_ready = sem("h_ready")
        rows_used = sem("rows_used")
        lngb_used = sem("lngb_used")
        var_ready = sem("var_ready")
        std_ready = sem("std_ready")
        post_done = sem("post_done")
        qk_ready = sem("qk_ready")
        rowmax_ready = sem("rowmax_ready")
        probs_ready = sem("probs_ready")
        conv_done = sem("conv_done")
        un_ready = sem("un_ready")
        sc_ready = sem("sc_ready")
        scexp_ready = sem("scexp_ready")
        eid_ready = sem("eid_ready")
        idx_staged = sem("idx_staged")
        slots_free = sem("slots_free")
        row_in = [sem(f"row_in{i}") for i in range(RING)]
        dots_ready = sem("dots_ready")
        gelu_ready = sem("gelu_ready")
        wexp_ready = sem("wexp_ready")
        diag_ready = sem("diag_ready")
        sum_taken = sem("sum_taken")
        lf_a = sem("lf_a")
        lf_e = sem("lf_e")
        lf_ready = sem("lf_ready")
        cg_ready = sem("cg_ready")
        nm_ready = sem("nm_ready")
        wm_ready = sem("wm_ready")
        am_ready = sem("am_ready")
        sig_ready = sem("sig_ready")
        y_ready = sem("y_ready")
        stored = sem("stored")

        def bank(n):
            return banks[n % NB]

        def job_done(eng, n):
            eng.wait_ge(bank_full[n % NB], n // NB + 1)

        def job_drained(eng, n):
            eng.wait_ge(bank_drained[n % NB], n // NB + 1)

        def jobs_drained(eng, last, first=0):
            for n in range(max(first, last - NB + 1), last + 1):
                job_drained(eng, n)

        def drains(ins, n):
            ins.then_inc(bank_drained[n % NB], 1)

        def walk_all(stages, experts, walk=WALK):
            for st in walk:
                if st[0] == "experts":
                    experts(st[1], st[2])
                elif kind(st[0]) in stages:
                    stages[kind(st[0])](st)

        block = ctx.enter_context(nc.Block())

        @block.sync
        def _(sp):
            unit_no = [0]
            ROWS_USERS = [st for st in WALK if st[0] in ("ln1", "ln2", "merge3")]

            def load_unit(src):
                n = unit_no[0]
                unit_no[0] += 1
                if n >= 2:
                    job_done(sp, UNIT_LAST[n - 2])
                cols = src.shape[1]
                sp.dma_start(w[:, n % 2, :, 0:cols], src.rearrange("(k p) n -> p k n", p=P)).then_inc(w_loaded[n % 2], 16)

            def unit(mat, lo):
                load_unit(mat[:, lo:lo + UW])

            def mod_row(l, s, i, dst, name):
                sp.dma_start(dst, a["mod_d"][l, 1 - s, i * D:(i + 1) * D].partition_broadcast(P)).then_inc(loads[name], 16)

            def everywhere(vec, dst, name):
                sp.dma_start(dst, vec.partition_broadcast(P)).then_inc(loads[name], 16)

            def store_mod(l, part):
                for k in range(8 * part, 8 * part + 8):
                    job_drained(sp, J["mod", l, k])
                src = bm0[:, part * 2 * D:(part + 1) * 2 * D] if l == 0 else bm1
                sp.dma_start(a["mod_d"][l, :, part * 2 * D:(part + 1) * 2 * D], src).then_inc(loads["modstore"], 16)

            def free_rows(st):
                sp.wait_ge(rows_used, ROWS_USERS.index(st))

            def shift_scale(l, s, i, st):
                if ROWS_USERS.index(st):
                    free_rows(st)
                for k in range(2):
                    mod_row(l, s, i + k, rows[:, k, :], "rows")

            def mod(st):
                _, l, k = st
                if l == 1 and k == 0:
                    sp.wait_ge(eid_ready, 4)
                    everywhere(a["ml_b_in"][1024:3088], mlb, "mlb")
                if l == 1 and k % 8 == 0:
                    if k:
                        sp.wait_ge(loads["modstore"], 16 * (3 + k // 8))
                    sp.dma_start(bm1, a["b_mod"][1, k * UW:(k + 8) * UW].partition_broadcast(2)).then_inc(loads["bmod"], 16)
                unit(a["w_mod"][l], k * UW)
                if l == 1 and k % 8 == 7:
                    store_mod(1, k // 8)

            def ln1(st):
                _, l, s = st
                if l == 0 and s == 0:
                    unit(a["ab_w_in"], 512)
                    unit(a["ab_w_in"], 512 + UW)
                    store_mod(0, 0)
                    sp.wait_ge(loads["modstore"], 16)
                    shift_scale(0, 0, 0, st)
                elif l == 0:
                    pass
                else:
                    sp.wait_ge(loads["modstore"], 96)
                    shift_scale(1, s, 0, st)
                    if s == 1:
                        sp.wait_ge(slots_free, RING + 4 * E)
                        sp.dma_start(mask[:, :, :], a["mask"]).then_inc(loads["mlc"], 16)
                        sp.dma_start(sel[0:8, :, :], a["sel"]).then_inc(loads["mlc"], 16)
                        everywhere(a["ml_norm_g"], normg, "mlc")

            def gate(st):
                if st[2] == 1:
                    unit(a["ab_w_in"], 512 + UW * part(st))

            def val(st):
                unit(a["ab_w_in"], UW * part(st))

            def q(st):
                if st[2] == 0 and part(st) == 0:
                    everywhere(a["ab_b_in"][1024:1792], qkvb, "qkvb")
                    everywhere(a["qk_g"], qkg, "qkvb")
                unit(a["ab_w_in"], 1024 + UW * part(st))

            def kv(st):
                unit(a["ab_w_in"], 1536)

            def chan(st):
                s = st[2]
                for k in range(2):
                    unit(a["ab_w_out"], UW * k)
                if s == 0:
                    store_mod(0, 1)
                    store_mod(0, 2)
                    sp.wait_ge(loads["modstore"], 48)
                free_rows(("merge3", 0, s))
                everywhere(a["ab_b_out"], rows[:, 0, :], "rows")
                mod_row(0, s, 2, gmod[:, s, :], "gmod")
                if s == 1:
                    sp.wait_ge(lngb_used, 2)
                everywhere(a["ln1_g"][0], lngb[:, 0, :], "lngb")
                everywhere(a["ln1_b"][0], lngb[:, 1, :], "lngb")

            def merge(st):
                name, l, s = st
                if l == 1 and name == "merge0":
                    free_rows(("merge3", 1, 1))
                    everywhere(a["ml_b_out"], rows[:, 0, :], "rows")
                    mod_row(1, 1, 2, gmod[:, 0, :], "gmod")
                    sp.wait_ge(lngb_used, 4)
                    everywhere(a["ln1_g"][1], lngb[:, 0, :], "lngb")
                    everywhere(a["ln1_b"][1], lngb[:, 1, :], "lngb")
                if l or part(st) >= 2:
                    unit(a["ml_w_out" if l else "ab_w_out"], UW * part(st))

            def post(st):
                _, l, s = st
                unit(a["w_q"][l], 0)
                unit(a["w_q"][l], UW)
                if l == 1:
                    mod_row(1, 1, 5, gmod[:, 1, :], "gmod")
                shift_scale(l, s, 3, ("ln2", l, s))
                sp.dma_start(keys[:, :, :], a["keys"][l]).then_inc(loads["keys"], 16)

            def ln2(st):
                _, l, s = st
                sp.wait_ge(lngb_used, (1 + 2 * s) if l == 0 else 5)
                if l == 0:
                    mod_row(0, s, 5, gmod[:, s, :], "gmod")
                everywhere(a["ln2_g"][l], lngb[:, 0, :], "lngb")
                everywhere(a["ln2_b"][l], lngb[:, 1, :], "lngb")

            def router(st):
                name, l, s = st
                c = part(st)
                if c >= 2:
                    unit(a["w_q"][l], UW * c)
                if c == 7 and l == 0 and s == 0:
                    shift_scale(0, 1, 0, ("ln1", 0, 1))

            def mlstm_in(lo):
                return lambda st: unit(a["ml_w_in"], lo + UW * part(st))

            def mg(st):
                load_unit(a["ml_w_in"][:, 3072:3088])

            sp.dma_start(cvec[:, :, :], a["cvec"]).then_inc(loads["cvec"], 16)
            sp.dma_start(bm0, a["b_mod"][0].partition_broadcast(2)).then_inc(loads["bmod"], 16)
            unit(a["w_mod"][0], 0)
            unit(a["w_mod"][0], UW)
            for t in range(TILES):
                sp.dma_start(x[:, t, :], (a["ctx"] if t < 2 else a["x"])[(t % 2) * P:(t % 2 + 1) * P, :]).then_inc(loads["x"], 16)
            sp.dma_start(con[:, :], a["con"]).then_inc(loads["con"], 16)
            sp.dma_start(col[:, :], a["col"]).then_inc(loads["con"], 16)

            def mod_first(st):
                if st[1] or st[2] >= 2:
                    mod(st)

            walk_all({"mod": mod_first, "ln1": ln1, "gate": gate, "val": val, "q": q, "kv": kv, "chan": chan, "merge": merge,
                      "post": post, "ln2": ln2, "r": router, "mq": mlstm_in(0), "mk": mlstm_in(512),
                      "mv": mlstm_in(1024), "mo": mlstm_in(2048), "mg": mg}, lambda q, k: None)
            for n in range(2):
                sp.wait_ge(post_done, 11 + n)
                sp.dma_start(a["out"][n * P:(n + 1) * P, :], x[:, 2 + n, :]).then_inc(stored, 16)
            sp.wait_ge(stored, 32)

        @block.gpsimd
        def _(pool):
            pool.sem_inc(slots_free, RING)
            for p in range(6):
                l = p // 4
                if p in (0, 4):
                    pool.wait_ge(eid_ready, p + 1)
                with pool.Fori(0, GPT // 2) as i:
                    for j in range(2 * RING):
                        pool.wait_ge(slots_free, p * E + i * 2 * RING + j + 1)
                        pool.sem_inc(pool_step, 1)
                        pool.wait_ge(idx_staged, p * GPT + i * 2 + j // RING + 1)
                        pool.sem_inc(pool_step, 1)
                        pool.indirect_dma_start(
                            out=ring[:, j % RING, :], out_offset=None, in_=a[f"uv{l}"][:, :],
                            in_offset=bass.IndirectOffsetOnAxis(ap=rows_idx[:, j // RING, j % RING:j % RING + 1], axis=0),
                        ).then_inc(row_in[j % RING], 16)

        @block.tensor
        def _(pe):
            unit_no = [0]

            def next_unit():
                n = unit_no[0]
                unit_no[0] += 1
                pe.wait_ge(w_loaded[n % 2], 16 * (n // 2 + 1))
                return w[:, n % 2]

            def open_bank(n):
                if n >= NB:
                    job_drained(pe, n - NB)

            def group(n, out, pairs):
                open_bank(n)
                for i, (l, r) in enumerate(pairs):
                    mm = pe.matmul(out, l, r, start=(i == 0), stop=(i == len(pairs) - 1))
                mm.then_inc(bank_full[n % NB], 1)

            def turn(n, parts):
                open_bank(n)
                for out, src in parts:
                    k = src.shape[0]
                    mm = pe.transpose(out, src, con[0:k, C_ID:C_ID + k])
                mm.then_inc(bank_full[n % NB], 1)

            def by_channel(n, wu, c):
                group(n, bank(n)[:, 0:ST], [(wu[:, k, c * P:(c + 1) * P], ht[:, k, :]) for k in range(KD)])

            def by_token(n, wu, i):
                group(n, bank(n)[:, 0:UW], [(ht[:, k, i * P:(i + 1) * P], wu[:, k, :]) for k in range(KD)])

            def mod(st):
                if st == ("mod", 0, 0):
                    pe.wait_ge(silu_ready, 1)
                n = J[st]
                wu = next_unit()
                group(n, bank(n)[0:2, 0:UW], [(cvec[:, k, :], wu[:, k, :]) for k in range(KD)])

            h_tiles = [0]

            def turn_h(st):
                if st == ("ln1", 0, 0):
                    pe.wait_ge(loads["con"], 32)
                s = st[2]
                for i in range(NS):
                    h_tiles[0] += 1
                    pe.wait_ge(h_ready, h_tiles[0])
                    for j in range(2):
                        n = J[st] + 2 * i + j
                        turn(n, [(bank(n)[:, c * P:(c + 1) * P], h[:, NS * s + i, (4 * j + c) * P:(4 * j + c + 1) * P]) for c in range(4)])
                jobs_drained(pe, J[st] + 3)

            def channels(st):
                wu = next_unit()
                for c in range(2):
                    by_channel(J[st] + c, wu, c)

            def tokens(st):
                if st[0] in ("merge0",):
                    jobs_drained(pe, J[st] - 1)
                wu = next_unit()
                for i in range(NS):
                    by_token(J[st] + i, wu, i)

            def rope(st):
                s = st[2]
                for i in range(NS):
                    pe.wait_ge(qk_ready, NS * s + i + 1)
                    n = J[st] + i
                    turn(n, [(bank(n)[:, c * P:(c + 1) * P], qk[:, i, c * P:(c + 1) * P]) for c in range(4)])
                n = J[st] + 2
                turn(n, [(bank(n)[:, i * P:(i + 1) * P], qk[:, i, 512:640]) for i in range(NS)])
                jobs_drained(pe, n)

            def scores(s, i):
                t, g, nk = i // 2, i % 2, ST * (1 + s)
                for c in range(4):
                    n = att_base(J, s, i)[0] + c
                    group(n, bank(n)[:, 0:nk], [(qt[64 * g:64 * g + 64, c, t * P:(t + 1) * P], kt[64 * g:64 * g + 64, 0:nk])])

            def attention(st):
                s, i = st[2], int(st[0][3])
                g = i % 2
                if i == 0:
                    scores(s, 0)
                if i < 3:
                    scores(s, i + 1)
                pe.wait_ge(probs_ready, 16 * s + 4 * (i + 1))
                _, turned, n = att_base(J, s, i)
                nkc = att_jobs(s)
                for kc in range(nkc):
                    m = turned + kc
                    turn(m, [(bank(m)[:, b * P:(b + 1) * P], probs[i % 2][:, hq, kc * P:(kc + 1) * P]) for b, hq in enumerate((0, 2, 1, 3))])
                open_bank(n)
                jobs_drained(pe, n - 1, turned)
                for odd in range(2):
                    for kc in range(nkc):
                        mm = pe.matmul(bank(n)[64 * odd:64 * odd + 64, 0:256], vv[:, kc, g * 64:(g + 1) * 64],
                                       pt[:, kc, 256 * odd:256 * odd + 256], start=(kc == 0), stop=(kc == nkc - 1))
                mm.then_inc(bank_full[n % NB], 1)

            def chan(st):
                s = st[2]
                pe.wait_ge(conv_done, s + 1)
                for i in range(NS):
                    n = J[st] + i
                    turn(n, [(bank(n)[:, c * P:(c + 1) * P], u[:, c, i * P:(i + 1) * P]) for c in range(CC)])
                pe.wait_ge(un_ready, s + 1)
                for b in range(2):
                    n = J[st] + 2 + b
                    turn(n, [(bank(n)[:, (2 * c + i) * P:(2 * c + i + 1) * P], ut[:, i, (2 * b + c) * P:(2 * b + c + 1) * P])
                             for c in range(2) for i in range(NS)])

            def router(st):
                name, l, s = st
                if name == "r0":
                    pe.wait_ge(loads["keys"], 16 * (2 * l + s + 1 - l))
                wu = next_unit()
                for c in range(2):
                    by_channel(J[st] + c, wu, c)
                for c in range(2):
                    n = J[st] + 2 + c
                    open_bank(n)
                    job_drained(pe, n - 2)
                    for i in range(NS):
                        mm = pe.matmul(bank(n)[:, i * NK:(i + 1) * NK], qh[:, c, i * P:(i + 1) * P], keys[:, 2 * part(st) + c, :], start=True, stop=True)
                    mm.then_inc(bank_full[n % NB], 1)

            def experts(q0, count):
                def rows8(q, half, first, last):
                    for j in range(RING):
                        pe.wait_ge(diag_ready, q * RING + j + 1)
                        for c in range(2):
                            mm = pe.matmul(expert_sum[:, c * 512:(c + 1) * 512], diag[:, j % NDIAG, :],
                                           ring[:, j, D + c * 512:D + (c + 1) * 512],
                                           start=(first and j == 0), stop=(last and j == RING - 1))
                        mm.then_inc(slots_free, 1)

                for q, pairs in expert_runs(q0, count):
                    if q % GPT == 0 and q:
                        pe.wait_ge(sum_taken, q // GPT)
                    if pairs:
                        with pe.Fori(0, pairs) as i:
                            rows8(q + 2 * i, 0, False, False)
                            rows8(q + 2 * i + 1, 1, False, False)
                    else:
                        rows8(q, q % 2, q % GPT == 0, q % GPT == GPT - 1)

            def mg(st):
                n = J[st]
                open_bank(n)
                wu = next_unit()
                for i in range(NS):
                    for k in range(KD):
                        mm = pe.matmul(bank(n)[:, i * 16:(i + 1) * 16], ht[:, k, i * P:(i + 1) * P], wu[:, k, 0:16], start=(k == 0), stop=(k == KD - 1))
                mm.then_inc(bank_full[n % NB], 1)

            def gatesum(st):
                n = J[st]
                open_bank(n)
                pe.wait_ge(lf_ready, 1)
                lt, utr, one = con[:, C_LT:C_LT + P], con[:, C_UT:C_UT + P], con[:, C_ONE:C_ONE + P]
                before = {(0, t): list(range(t)) for t in range(TILES)}
                before.update({(1, 0): [1], (1, 1): [], (1, 2): [3, 0, 1], (1, 3): [0, 1]})
                for t in range(TILES):
                    for d in range(2):
                        terms = [(utr if d else lt, t)] + [(one, b) for b in before[d, t]]
                        for i, (m, b) in enumerate(terms):
                            mm = pe.matmul(bank(n)[:, t * 8 + 4 * d:t * 8 + 4 * d + 4], m, lf[:, b, 4 * d:4 * d + 4], start=(i == 0), stop=(i == len(terms) - 1))
                mm.then_inc(bank_full[n % NB], 1)
                pe.wait_ge(cg_ready, 1)
                n += 1
                turn(n, [(bank(n)[0:8, t * P:(t + 1) * P], cg[:, t, :]) for t in range(TILES)])
                job_drained(pe, n)
                pe.wait_ge(loads["mlc"], 48)
                for st_ in (("mq1", 1, 1), ("mk1", 1, 1), ("mv3", 1, 1)):
                    jobs_drained(pe, J[st_] + 1)

            def decay(st):
                for d in range(2):
                    n = J[st] + d
                    group(n, bank(n)[:, :], [(sel[0:8, 4 * d + part(st), :], ct_[0:8, :])])

            def head(st):
                hd, b0 = part(st), J[st]
                for i in range(2):
                    group(b0 + i, bank(b0 + i)[:, :], [(mqt[:, hd, i * P:(i + 1) * P], mkt[:, hd, :])])
                for i in range(2):
                    pe.wait_ge(am_ready, 2 * hd + i + 1)
                    n = b0 + 2 + i
                    turn(n, [(bank(n)[:, kc * P:(kc + 1) * P], am[:, i, kc * P:(kc + 1) * P]) for kc in range(4)])
                for i in range(2):
                    job_drained(pe, b0 + 2 + i)
                    n = b0 + 4 + i
                    group(n, bank(n)[:, 0:MDV], [(att[:, i, kc * P:(kc + 1) * P], mval[:, kc, hd * MDV:(hd + 1) * MDV]) for kc in range(4)])

            def heads(st):
                for i in range(NS):
                    pe.wait_ge(y_ready, i + 1)
                    for j in range(2):
                        n = J[st] + 2 * i + j
                        turn(n, [(bank(n)[:, c * P:(c + 1) * P], hh[:, i, (4 * j + c) * P:(4 * j + c + 1) * P]) for c in range(4)])

            walk_all({"mod": mod, "ln1": turn_h, "ln2": turn_h, "gate": channels, "val": channels, "mq": channels, "mk": channels,
                      "q": tokens, "kv": tokens, "merge": tokens, "mv": tokens, "mo": tokens, "rope": rope, "att": attention,
                      "chan": chan, "r": router, "mg": mg, "gatesum": gatesum,
                      "decay": decay, "head": head, "heads": heads}, experts)

        @block.scalar
        def _(act):
            stds = [0]

            def copy_out(n, dst, src):
                job_done(act, n)
                drains(act.activation(dst, src, ACT.Copy), n)

            def square_root(cols):
                stds[0] += 1
                act.wait_ge(var_ready, stds[0])
                act.activation(std[:, 0:cols], std[:, 0:cols], ACT.Sqrt).then_inc(std_ready, 1)

            def four(ap):
                return ap.rearrange("p (c n) -> p c n", c=4)

            def turn_h(st):
                if st == ("ln1", 0, 0):
                    act.wait_ge(loads["con"], 32)
                square_root(4)
                for i in range(NS):
                    for j in range(2):
                        n = J[st] + 2 * i + j
                        copy_out(n, ht[:, 4 * j:4 * j + 4, i * P:(i + 1) * P], four(bank(n)[:, :]))

            def gate(st):
                for c in range(2 * part(st), 2 * part(st) + 2):
                    n = J[st] + c % 2
                    job_done(act, n)
                    drains(act.activation(sg[:, c, :], bank(n)[:, 0:ST], ACT.Sigmoid, bias=col[:, Q_GB + c:Q_GB + c + 1]), n)

            def rope(st):
                s = st[2]
                square_root(20)
                for i in range(NS):
                    n = J[st] + i
                    copy_out(n, qt[:, :, i * P:(i + 1) * P], four(bank(n)[:, :]))
                copy_out(J[st] + 2, kt[:, s * ST:(s + 1) * ST], bank(J[st] + 2)[:, 0:ST])

            def exps(s, i):
                nk = ST * (1 + s)
                if i >= 2:
                    job_done(act, att_base(J, s, i - 2)[2] - 1)
                for c in range(4):
                    n = att_base(J, s, i)[0] + c
                    act.wait_ge(rowmax_ready, 16 * s + 4 * i + c + 1)
                    job_done(act, n)
                    k = (4 * i + c) % 8
                    drains(act.activation(probs[i % 2][:, c, 0:nk], bank(n)[:, 0:nk], ACT.Exp, bias=small[:, k:k + 1],
                                          scale=HEAD ** -0.5, accum_out=small[:, 8 + k:9 + k]), n)

            def attention(st):
                s, i = st[2], int(st[0][3])
                if i == 0:
                    exps(s, 0)
                else:
                    job_done(act, att_base(J, s, i - 1)[2])
                if i < 3:
                    exps(s, i + 1)
                t, g = i // 2, i % 2
                _, turned, n = att_base(J, s, i)
                for kc in range(att_jobs(s)):
                    copy_out(turned + kc, pt[:, kc, :], bank(turned + kc)[:, :])
                copy_out(n, ht[:, 4 + 2 * g:6 + 2 * g, t * P:(t + 1) * P], bank(n)[:, 0:256].rearrange("p (c n) -> p c n", c=2))

            def chan(st):
                for i in range(NS):
                    copy_out(J[st] + i, ut[:, i, :], bank(J[st] + i)[:, :])
                square_root(4)
                for c in range(CC):
                    n = J[st] + 2 + c // 2
                    job_done(act, n)
                    ins = act.activation(ht[:, c, :], bank(n)[:, (c % 2) * ST:(c % 2 + 1) * ST], ACT.Silu,
                                         bias=col[:, Q_LB + c:Q_LB + c + 1], scale=col[:, Q_LG + c:Q_LG + c + 1])
                    if c % 2:
                        drains(ins, n)

            def router(st):
                for c in range(2):
                    if part(st):
                        job_done(act, J[f"r{part(st) - 1}", st[1], st[2]] + 2 + c)
                    copy_out(J[st] + c, qh[:, c, :], bank(J[st] + c)[:, 0:ST])

            def picks(st):
                act.wait_ge(sc_ready, st[2] + 1)
                act.activation(sc[:, :, :], sc[:, :, :], ACT.Exp).then_inc(scexp_ready, 1)

            def experts(q0, count):
                def rows8(q, half):
                    for j in range(0, RING, GROUP):
                        b = half * RING + j
                        act.wait_ge(dots_ready, q * RING + j + GROUP)
                        act.activation(gel[:, b:b + GROUP], dots[:, b:b + GROUP], ACT.Gelu).then_inc(gelu_ready, 1)
                        act.wait_ge(wexp_ready, q * (RING // GROUP) + j // GROUP + 1)
                        for k in range(GROUP):
                            act.wait_ge(slots_free, q * RING + j + k + 1 + RING - NDIAG)
                            act.activation(diag[:, (j + k) % NDIAG, :], ident, ACT.Copy, scale=wexp[:, b + k:b + k + 1]).then_inc(diag_ready, 1)

                for q, pairs in expert_runs(q0, count):
                    if pairs:
                        with act.Fori(0, pairs) as i:
                            rows8(q + 2 * i, 0)
                            rows8(q + 2 * i + 1, 1)
                    else:
                        rows8(q, q % 2)
                    if q % GPT == GPT - 1:
                        square_root(4)

            def to_channels(dst, first):
                def stage(st):
                    lo = ST * st[2] if kind(st[0]) == "mk" else 0
                    for c in range(2 * part(st), 2 * part(st) + 2):
                        n = J[st] + c % 2
                        job_done(act, n)
                        drains(act.activation(dst[:, c, lo:lo + ST], bank(n)[:, 0:ST], ACT.Identity, bias=col[:, first + c:first + c + 1]), n)
                return stage

            def gatesum(st):
                jobs_drained(act, J["mo3", 1, 1] + 1)
                act.activation(og[:, :, :], og[:, :, :], ACT.Sigmoid).then_inc(sig_ready, 1)
                act.wait_ge(lf_a, 1)
                act.activation(le[:, :, :], la[:, :, :], ACT.Exp, scale=-1.0).then_inc(act_step, 1)
                act.wait_ge(act_step, 1)
                act.activation(le[:, :, :], le[:, :, :], ACT.Ln, bias=con[:, C_ONE:C_ONE + 1]).then_inc(lf_e, 1)
                copy_out(J[st] + 1, ct_[0:8, :], bank(J[st] + 1)[0:8, :])

            def decay(st):
                hd = part(st)
                cm, b = cms[hd % 2], 4 * (hd % 2)
                for d in range(2):
                    for i in range(2):
                        r = 2 * d + i
                        act.wait_ge(nm_ready, 4 * hd + r + 1)
                        act.activation(cm[:, r, :], cm[:, r, :], ACT.Exp, bias=nm[:, b + r:b + r + 1])
                        act.activation(thr[:, b + r:b + r + 1], bc[:, 2 + i, 4 * d + hd:4 * d + hd + 1], ACT.Exp,
                                       bias=nm[:, b + r:b + r + 1], scale=-1.0).then_inc(wm_ready, 1)

            def head(st):
                hd = part(st)
                for i in range(2):
                    if hd:
                        job_done(act, J[f"head{hd - 1}", 1, 1] + 4 + i)
                    copy_out(J[st] + 2 + i, att[:, i, :], bank(J[st] + 2 + i)[:, :])
                for i in range(2):
                    n = J[st] + 4 + i
                    copy_out(n, hh[:, i, hd * MDV:(hd + 1) * MDV], bank(n)[:, 0:MDV])

            def heads(st):
                square_root(8)
                for i in range(NS):
                    for j in range(2):
                        n = J[st] + 2 * i + j
                        copy_out(n, ht[:, 4 * j:4 * j + 4, i * P:(i + 1) * P], four(bank(n)[:, :]))

            act.wait_ge(loads["cvec"], 16)
            act.activation(cvec[:, :, :], cvec[:, :, :], ACT.Silu).then_inc(silu_ready, 1)
            walk_all({"ln1": turn_h, "ln2": turn_h, "gate": gate, "rope": rope, "att": attention, "chan": chan,
                      "post": lambda st: square_root(4), "r": router, "picka": picks, "mq": to_channels(mqt, Q_MQ),
                      "mk": to_channels(mkt, Q_MK), "gatesum": gatesum, "decay": decay, "head": head, "heads": heads}, experts, AHEAD)

        @block.vector
        def _(dve):
            cnt = {}

            def count(name, by=1):
                cnt[name] = cnt.get(name, 0) + by
                return cnt[name]

            def do(ins):
                ins.then_inc(dve_step, 1)
                dve.wait_ge(dve_step, count("step"))

            def chains(ins):
                ins.then_inc(dve_step, 1)
                dve.wait_ge(dve_step, count("step") - 1)

            def chains_end():
                dve.wait_ge(dve_step, cnt["step"])

            def loaded(name, n):
                dve.wait_ge(loads[name], 16 * count(name, n))

            def root(cols):
                dve.wait_ge(std_ready, count("std"))
                do(dve.reciprocal(rstd[:, 0:cols], std[:, 0:cols]))

            def mean_var(src, k):
                width = src.shape[1]
                parts = max(1, width // 512)
                for i in range(parts):
                    do(dve.bn_stats(stats[:, 6 * i:6 * i + 6], src[:, i * 512:min((i + 1) * 512, width)]))
                do(dve.bn_aggr(mv[:, k, :], stats[:, 0:6 * parts]))

            def var_out(cols):
                dve.tensor_scalar(std[:, 0:cols], mv[:, 0:cols, 1], EPS, None, ALU.add).then_inc(var_ready, 1)

            def normalize(tiles):
                for i, (src, _) in enumerate(tiles):
                    mean_var(src, i)
                var_out(4)
                root(4)
                for i, (src, dst) in enumerate(tiles):
                    do(dve.tensor_scalar(dst, src, mv[:, i, 0:1], rstd[:, i:i + 1], ALU.subtract, ALU.mult))

            def post_norm(tiles, s, y):
                for t in tiles:
                    do(dve.tensor_tensor(h[:, t, :], y if y is not None else h[:, t, :], gmod[:, s, :], ALU.mult))
                    if y is not None:
                        dve.sem_inc(sum_taken, 1)
                    do(dve.scalar_tensor_tensor(out=x[:, t, :], in0=x[:, t, :], scalar=ALPHA, in1=h[:, t, :], op0=ALU.mult, op1=ALU.add))
                normalize([(x[:, t, :], x[:, t, :]) for t in tiles])
                for t in tiles:
                    do(dve.tensor_tensor(x[:, t, :], x[:, t, :], lngb[:, 0, :], ALU.mult))
                    dve.tensor_tensor(x[:, t, :], x[:, t, :], lngb[:, 1, :], ALU.add).then_inc(post_done, 1)
                    dve.wait_ge(post_done, count("post"))

            def mod(st):
                _, l, k = st
                bm, lo = (bm0, k * UW) if l == 0 else (bm1, k % 8 * UW)
                if k == 0 or (l == 1 and k % 8 == 0):
                    loaded("bmod", 1)
                n = J[st]
                job_done(dve, n)
                drains(dve.tensor_tensor(bm[:, lo:lo + UW], bank(n)[0:2, 0:UW], bm[:, lo:lo + UW], ALU.add), n)

            def modulate(st):
                s = st[2]
                if st == ("ln1", 0, 0):
                    dve.wait_ge(loads["x"], 64)
                    dve.wait_ge(loads["con"], 32)
                tiles = [NS * s + i for i in range(NS)]
                normalize([(x[:, t, :], h[:, t, :]) for t in tiles])
                loaded("rows", 2)
                do(dve.tensor_scalar(rows[:, 1, :], rows[:, 1, :], 1.0, None, ALU.add))
                for t in tiles:
                    do(dve.tensor_tensor(h[:, t, :], h[:, t, :], rows[:, 1, :], ALU.mult))
                    dve.tensor_tensor(h[:, t, :], h[:, t, :], rows[:, 0, :], ALU.add).then_inc(h_ready, 1)
                    dve.wait_ge(h_ready, count("h"))
                dve.sem_inc(rows_used, 1)

            def val(st):
                if part(st) == 0:
                    do(dve.memset(cin[:, :, 0:PAD], 0.0))
                    do(dve.memset(cin[:, :, PAD + ST:CW], 0.0))
                for c in range(2 * part(st), 2 * part(st) + 2):
                    n = J[st] + c % 2
                    job_drained(dve, J[f"gate{part(st)}", 0, st[2]] + c % 2)
                    job_done(dve, n)
                    drains(dve.scalar_tensor_tensor(out=cin[:, c, PAD:PAD + ST], in0=bank(n)[:, 0:ST], scalar=col[:, Q_VB + c:Q_VB + c + 1],
                                                    in1=sg[:, c, :], op0=ALU.add, op1=ALU.mult), n)

            def q(st):
                c = part(st)
                if st[2] == 0 and c == 0:
                    loaded("qkvb", 2)
                for i in range(NS):
                    n = J[st] + i
                    job_done(dve, n)
                    drains(dve.tensor_tensor(qk[:, i, c * UW:(c + 1) * UW], bank(n)[:, 0:UW], qkvb[:, c * UW:(c + 1) * UW], ALU.add), n)

            def kv(st):
                for i in range(NS):
                    n = J[st] + i
                    job_done(dve, n)
                    do(dve.tensor_tensor(qk[:, i, 512:640], bank(n)[:, 0:128], qkvb[:, 512:640], ALU.add))
                    drains(dve.tensor_tensor(vv[:, NS * st[2] + i, :], bank(n)[:, 128:256], qkvb[:, 640:768], ALU.add), n)

            def heads_of(ap):
                return ap.rearrange("p (h d) -> p h d", d=HEAD)

            NH = NQH + NKV

            def rope(st):
                s = st[2]
                jobs_drained(dve, J[st] - 1)
                for i in range(NS):
                    do(dve.tensor_tensor(tmp1, qk[:, i, :], qk[:, i, :], ALU.mult))
                    do(dve.tensor_reduce(std[:, NH * i:NH * (i + 1)], heads_of(tmp1), AX.X, ALU.add))
                dve.tensor_scalar(std[:, :], std[:, :], 1.0 / HEAD, EPS, ALU.mult, ALU.add).then_inc(var_ready, 1)
                root(NS * NH)
                for i in range(NS):
                    hq = heads_of(qk[:, i, :])
                    do(dve.tensor_tensor(hq, hq, rstd[:, NH * i:NH * (i + 1)].unsqueeze(2).broadcast_to([P, NH, HEAD]), ALU.mult))
                    last = dve.tensor_tensor(qk[:, i, :], qk[:, i, :], qkg, ALU.mult)
                    if s == 1:
                        do(last)
                        cs = con[:, C_COS + i * HEAD:C_COS + (i + 1) * HEAD]
                        sn = con[:, C_SIN + i * HEAD:C_SIN + (i + 1) * HEAD].rearrange("p (a b f) -> p a b f", a=2, b=2)
                        do(dve.tensor_tensor(heads_of(tmp1), hq, cs.unsqueeze(1).broadcast_to([P, NH, HEAD]), ALU.mult))
                        q4 = qk[:, i, :].rearrange("p (h a b f) -> p h a b f", a=2, b=2, f=16)
                        t4 = tmp2.rearrange("p (h a b f) -> p h a b f", a=2, b=2, f=16)
                        for b in range(2):
                            do(dve.tensor_tensor(t4[:, :, :, b, :], q4[:, :, :, 1 - b, :],
                                                 sn[:, :, b, :].unsqueeze(1).broadcast_to([P, NH, 2, 16]), ALU.mult))
                        last = dve.tensor_tensor(qk[:, i, :], tmp1, tmp2, ALU.add)
                    last.then_inc(qk_ready, 1)
                    dve.wait_ge(qk_ready, count("qk"))

            def row_max(s, i):
                for c in range(4):
                    n = att_base(J, s, i)[0] + c
                    k = (4 * i + c) % 8
                    job_done(dve, n)
                    do(dve.tensor_reduce(small[:, 16 + k:17 + k], bank(n)[:, 0:ST * (1 + s)], AX.X, ALU.max))
                    dve.tensor_scalar(small[:, k:k + 1], small[:, 16 + k:17 + k], -(HEAD ** -0.5), None, ALU.mult).then_inc(rowmax_ready, 1)

            def attention(st):
                s, i = st[2], int(st[0][3])
                if i == 0:
                    row_max(s, 0)
                if i < 3:
                    row_max(s, i + 1)
                for c in range(4):
                    k = (4 * i + c) % 8
                    job_drained(dve, att_base(J, s, i)[0] + c)
                    do(dve.reciprocal(small[:, 24 + k:25 + k], small[:, 8 + k:9 + k]))
                    pr = probs[i % 2][:, c, 0:ST * (1 + s)]
                    dve.tensor_scalar(pr, pr, small[:, 24 + k:25 + k], None, ALU.mult).then_inc(probs_ready, 1)

            def conv(st):
                s, piece = st[2], part(st)
                if piece == 0:
                    job_done(dve, att_base(J, s, 3)[2])
                    for v in range(2):
                        jobs_drained(dve, J[f"val{v}", 0, s] + 1)
                for k in range(8 * (piece % 4), min(TAPS, 8 * (piece % 4) + 8)):
                    for c in (2 * (piece // 4), 2 * (piece // 4) + 1):
                        src, dst = cin[:, c, k:k + ST], u[:, c, :]
                        tap = col[:, Q_CW + c * TAPS + k:Q_CW + c * TAPS + k + 1]
                        if k == 0:
                            chains(dve.tensor_scalar(dst, src, tap, col[:, Q_CB + c:Q_CB + c + 1], ALU.mult, ALU.add))
                        else:
                            chains(dve.scalar_tensor_tensor(out=dst, in0=src, scalar=tap, in1=dst, op0=ALU.mult, op1=ALU.add))
                chains_end()
                if piece == CONV_PIECES - 1:
                    dve.sem_inc(conv_done, 1)

            def chan(st):
                for i in range(NS):
                    job_drained(dve, J[st] + i)
                normalize([(ut[:, i, :], ut[:, i, :]) for i in range(NS)])
                dve.sem_inc(un_ready, 1)

            def merge(st):
                name, l, s = st
                lo = part(st) * UW
                if part(st) == 0:
                    loaded("rows", 1)
                for i in range(NS):
                    n = J[st] + i
                    job_done(dve, n)
                    drains(dve.tensor_tensor(h[:, NS * s + i, lo:lo + UW], bank(n)[:, 0:UW], rows[:, 0, lo:lo + UW], ALU.add), n)
                if part(st) == 3:
                    jobs_drained(dve, J[st] + 1)
                    dve.sem_inc(rows_used, 1)

            def post(st):
                _, l, s = st
                loaded("gmod", 1)
                loaded("lngb", 2)
                jobs_drained(dve, J[st] - 1)
                post_norm([NS * s + i for i in range(NS)], s if l == 0 else 0, None)
                dve.sem_inc(lngb_used, 1)

            def top16(pair):
                for v, _, src, _ in pair:
                    chains(dve.max(v[:, 0:8], src))
                for v, ix, src, _ in pair:
                    chains(dve.max_index(ix[:, 0:8], v[:, 0:8], src))
                for v, _, src, spare in pair:
                    chains(dve.match_replace(spare, v[:, 0:8], src, LOWEST))
                for v, _, _, spare in pair:
                    chains(dve.max(v[:, 8:16], spare))
                for v, ix, _, spare in pair:
                    chains(dve.max_index(ix[:, 8:16], v[:, 8:16], spare))

            def router(st):
                for k in range(2):
                    c = 2 * part(st) + k
                    n = J[st] + 2 + k
                    job_done(dve, n)
                    top16([(tv[:, i, c, :], ti[:, i, c, :], bank(n)[:, i * NK:(i + 1) * NK], left[:, i * NK:(i + 1) * NK]) for i in range(NS)])
                    chains_end()
                    dve.sem_inc(bank_drained[n % NB], 1)

            def picka(st):
                i = st[2] % 2
                tvp = tv[:, i].rearrange("p (h s) k -> p h s k", s=2)
                v1, v2 = tvp[:, :, 0, :], tvp[:, :, 1, :]
                do(dve.tensor_tensor(cand[:, :, 0:WIDE * TOPK].rearrange("p h (i j) -> p h i j", i=WIDE),
                                     v1[:, :, 0:WIDE].unsqueeze(3).broadcast_to([P, PH, WIDE, TOPK]),
                                     v2.unsqueeze(2).broadcast_to([P, PH, WIDE, TOPK]), ALU.add))
                do(dve.tensor_tensor(cand[:, :, WIDE * TOPK:NCAND].rearrange("p h (i j) -> p h i j", j=DEEP),
                                     v1[:, :, WIDE:TOPK].unsqueeze(3).broadcast_to([P, PH, TOPK - WIDE, DEEP]),
                                     v2[:, :, 0:DEEP].unsqueeze(2).broadcast_to([P, PH, TOPK - WIDE, DEEP]), ALU.add))
                for b in range(0, PH, 2):
                    top16([(sc[:, b + k, :], pos[:, b + k, :], cand[:, b + k, :], left[:, k * P:k * P + NCAND]) for k in range(2)])
                chains_end()
                do(dve.tensor_copy(small[:, 0:8], sc[:, :, 0]))
                dve.tensor_tensor(sc, sc, small[:, 0:8].unsqueeze(2).broadcast_to([P, PH, TOPK]), ALU.subtract).then_inc(sc_ready, 1)

            def pickb(st):
                t = st[2]
                i, lo = t % 2, (t % 4) * E
                do(dve.tensor_copy(tif, ti[:, i]))
                tip = tif.rearrange("p (h s) k -> p h s k", s=2)
                do(dve.tensor_scalar(high, pos, 4, None, ALU.logical_shift_right))
                do(dve.tensor_copy(second, high))
                do(dve.tensor_scalar(high, pos, 2, None, ALU.logical_shift_right))
                do(dve.tensor_copy(first, high))
                do(dve.scalar_tensor_tensor(out=first, in0=first, scalar=float(WIDE - WIDE * TOPK // DEEP), in1=second, op0=ALU.add, op1=ALU.max))
                do(dve.tensor_scalar(e2, first, float(DEEP), float(WIDE * TOPK - WIDE * DEEP), ALU.mult, ALU.add))
                do(dve.scalar_tensor_tensor(out=e2, in0=first, scalar=float(TOPK), in1=e2, op0=ALU.mult, op1=ALU.min))
                do(dve.tensor_copy(second, pos))
                do(dve.tensor_tensor(second, second, e2, ALU.subtract))
                for b, place, dst in ((0, first, e1), (1, second, e2)):
                    do(dve.tensor_tensor(hot.rearrange("p h i j -> p (h i) j"), place.rearrange("p h k -> p (h k)").unsqueeze(2).broadcast_to([P, E, TOPK]),
                                         con[:, C_IOTA:C_IOTA + TOPK].unsqueeze(1).broadcast_to([P, E, TOPK]), ALU.is_equal))
                    do(dve.tensor_tensor(hot, hot, tip[:, :, b, :].unsqueeze(2).broadcast_to([P, PH, TOPK, TOPK]), ALU.mult))
                    do(dve.tensor_reduce(dst, hot, AX.X, ALU.add))
                do(dve.scalar_tensor_tensor(out=eid[:, lo:lo + E].rearrange("p (h k) -> p h k", h=PH), in0=e1, scalar=float(NK), in1=e2, op0=ALU.mult, op1=ALU.add))
                dve.wait_ge(scexp_ready, t + 1)
                do(dve.tensor_reduce(small[:, 8:16], sc, AX.X, ALU.add))
                do(dve.reciprocal(small[:, 8:16], small[:, 8:16]))
                dve.tensor_tensor(gates[:, lo:lo + E].rearrange("p (h k) -> p h k", h=PH), sc,
                                  small[:, 8:16].unsqueeze(2).broadcast_to([P, PH, TOPK]), ALU.mult).then_inc(eid_ready, 1)
                dve.wait_ge(eid_ready, t + 1)

            def stage_rows(column, half):
                dve.tensor_copy(rows_idx[:, half, :], eid[:, bass.ds(column, RING)]).then_inc(idx_staged, 1)

            def begin(st):
                stage_rows(0, 0)
                stage_rows(RING, 1)

            def experts(q0, count_):
                def rows8(q, half, t, column, ahead):
                    for j in range(RING):
                        b = half * RING + j
                        dve.wait_ge(row_in[j], (q + 1) * 16)
                        r = ring[:, j, 0:D]
                        dve.tensor_tensor_reduce(out=r, in0=r, in1=h[:, t, :], scale=1.0, scalar=0.0, op0=ALU.mult,
                                                 op1=ALU.add, accum_out=dots[:, b:b + 1]).then_inc(dots_ready, 1)
                        if j % GROUP == GROUP - 1:
                            f = j - GROUP + 1
                            dve.wait_ge(gelu_ready, q * (RING // GROUP) + j // GROUP + 1)
                            dve.tensor_tensor(wexp[:, b - GROUP + 1:b + 1], gel[:, b - GROUP + 1:b + 1],
                                              gates[:, bass.ds(column + f, GROUP)], ALU.mult).then_inc(wexp_ready, 1)
                    if ahead:
                        stage_rows(column + 2 * RING, half)

                for q, pairs in expert_runs(q0, count_):
                    l, p = q // (4 * GPT), q // GPT
                    t = p if l == 0 else p - 2
                    column = (q - l * 4 * GPT) * RING
                    if pairs:
                        with dve.Fori(0, pairs) as i:
                            rows8(q + 2 * i, 0, t, column + i * 2 * RING, True)
                            rows8(q + 2 * i + 1, 1, t, column + i * 2 * RING + RING, True)
                    else:
                        rows8(q, q % 2, t, column, q + 2 not in (4 * GPT, 4 * GPT + 1, 6 * GPT, 6 * GPT + 1))
                    if q % GPT == GPT - 1:
                        if p in (0, 1, 2, 4):
                            cnt["gmod"], cnt["lngb"] = EXPERT_ROWS[p]
                            loaded("gmod", 0)
                            loaded("lngb", 0)
                        dve.wait_ge(slots_free, RING + (p + 1) * E)
                        post_norm([t], (p // 2) if l == 0 else 1, expert_sum[:, :])
                        if p in (0, 3, 5):
                            dve.sem_inc(lngb_used, 1)

            EXPERT_ROWS = {0: (2, 4), 1: (4, 8), 2: (4, 8), 4: (6, 12)}

            def values(st):
                name, l, s = st
                lo = part(st) * UW
                if name == "mv0" and s == 0:
                    loaded("mlb", 1)
                for i in range(NS):
                    n = J[st] + i
                    job_done(dve, n)
                    if name[:2] == "mv":
                        drains(dve.tensor_tensor(mval[:, NS * s + i, lo:lo + UW], bank(n)[:, 0:UW], mlb[:, lo:lo + UW], ALU.add), n)
                    else:
                        drains(dve.tensor_tensor(og[:, i, lo:lo + UW], bank(n)[:, 0:UW], mlb[:, D + lo:D + lo + UW], ALU.add), n)

            def mg(st):
                n, s = J[st], st[2]
                job_done(dve, n)
                drains(dve.tensor_tensor(gt[:, NS * s:NS * s + NS, :], bank(n)[:, 0:32].rearrange("p (t n) -> p t n", t=NS),
                                         mlb[:, 2048:2064].unsqueeze(1).broadcast_to([P, NS, 16]), ALU.add), n)
                job_drained(dve, n)

            def gatesum(st):
                gt5 = gt[:, :, :].rearrange("p t (d k h) -> p t d k h", d=2, k=2)
                f, ig = gt5[:, :, :, 1, :], gt5[:, :, :, 0, :]

                def by_dir(tile):
                    return tile[:, :, :].rearrange("p t (d h) -> p t d h", d=2)

                do(dve.tensor_scalar(by_dir(lf), f, -1.0, None, ALU.mult))
                dve.tensor_tensor(by_dir(la), by_dir(lf), f, ALU.max).then_inc(lf_a, 1)
                dve.wait_ge(lf_a, 1)
                do(dve.tensor_scalar(by_dir(lf), f, 0.0, None, ALU.min))
                dve.wait_ge(lf_e, 1)
                dve.tensor_tensor(lf[:, :, :], lf[:, :, :], le[:, :, :], ALU.subtract).then_inc(lf_ready, 1)
                n = J[st]
                job_done(dve, n)
                drains(dve.tensor_copy(bc[:, :, :], bank(n)[:, 0:32].rearrange("p (t n) -> p t n", t=TILES)), n)
                job_drained(dve, n)
                dve.tensor_tensor(by_dir(cg), ig, by_dir(bc), ALU.subtract).then_inc(cg_ready, 1)
                dve.wait_ge(loads["mlc"], 48)

            def decay(st):
                hd, b0 = part(st), J[st]
                cm, b = cms[hd % 2], 4 * (hd % 2)
                if hd >= 2:
                    dve.wait_ge(am_ready, 2 * hd - 2)
                for d in range(2):
                    job_done(dve, b0 + d)
                    for i in range(2):
                        chains(dve.tensor_tensor(cm[:, 2 * d + i, :], bank(b0 + d)[:, :], mask[:, 2 * d + i, :], ALU.add))
                    for i in range(2):
                        chains(dve.tensor_reduce(top[:, b + 2 * d + i:b + 2 * d + i + 1], cm[:, 2 * d + i, :], AX.X, ALU.max))
                    chains_end()
                    dve.sem_inc(bank_drained[(b0 + d) % NB], 1)
                    for i in range(2):
                        r = b + 2 * d + i
                        dve.tensor_scalar(nm[:, r:r + 1], top[:, r:r + 1], 0.0, -1.0, ALU.max, ALU.mult).then_inc(nm_ready, 1)

            def head(st):
                hd, b0 = part(st), J[st]
                cm, b = cms[hd % 2], 4 * (hd % 2)
                for i in range(2):
                    n = b0 + i
                    job_done(dve, n)
                    for d in range(2):
                        r = 2 * d + i
                        dve.wait_ge(wm_ready, 4 * hd + r + 1)
                        chains(dve.tensor_tensor_reduce(out=cm[:, r, :], in0=cm[:, r, :], in1=bank(n)[:, :], scale=MDQ ** -0.5, scalar=0.0,
                                                        op0=ALU.mult, op1=ALU.add, accum_out=den[:, r:r + 1]))
                    for r in (i, 2 + i):
                        chains(dve.tensor_scalar(den[:, 4 + r:5 + r], den[:, r:r + 1], -1.0, None, ALU.mult))
                    for r in (i, 2 + i):
                        chains(dve.tensor_tensor(den[:, r:r + 1], den[:, r:r + 1], den[:, 4 + r:5 + r], ALU.max))
                    for r in (i, 2 + i):
                        chains(dve.tensor_tensor(den[:, r:r + 1], den[:, r:r + 1], thr[:, b + r:b + r + 1], ALU.max))
                    for r in (i, 2 + i):
                        chains(dve.reciprocal(den[:, 4 + r:5 + r], den[:, r:r + 1]))
                    chains_end()
                    dve.sem_inc(bank_drained[n % NB], 1)
                    do(dve.tensor_scalar(cm[:, i, :], cm[:, i, :], den[:, 4 + i:5 + i], None, ALU.mult))
                    if hd:
                        job_done(dve, J[f"head{hd - 1}", 1, 1] + 2 + i)
                    dve.scalar_tensor_tensor(out=am[:, i, :], in0=cm[:, 2 + i, :], scalar=den[:, 6 + i:7 + i], in1=cm[:, i, :],
                                             op0=ALU.mult, op1=ALU.add).then_inc(am_ready, 1)

            def heads(st):
                for hd in range(MH):
                    for i in range(NS):
                        job_drained(dve, J[f"head{hd}", 1, 1] + 4 + i)
                for i in range(NS):
                    for hd in range(MH):
                        mean_var(hh[:, i, hd * MDV:(hd + 1) * MDV], 4 * i + hd)
                var_out(8)
                root(8)
                dve.wait_ge(sig_ready, 1)
                for i in range(NS):
                    for hd in range(MH):
                        k = 4 * i + hd
                        y = hh[:, i, hd * MDV:(hd + 1) * MDV]
                        do(dve.tensor_scalar(y, y, mv[:, k, 0:1], rstd[:, k:k + 1], ALU.subtract, ALU.mult))
                    do(dve.tensor_tensor(hh[:, i, :], hh[:, i, :], normg, ALU.mult))
                    dve.tensor_tensor(hh[:, i, :], hh[:, i, :], og[:, i, :], ALU.mult).then_inc(y_ready, 1)

            do(dve.memset(mv[:, :, :], 0.0))
            walk_all({"mod": mod, "ln1": modulate, "ln2": modulate, "val": val, "q": q, "kv": kv, "rope": rope, "att": attention,
                      "conv": conv, "chan": chan, "merge": merge, "post": post, "r": router, "picka": picka, "pickb": pickb,
                      "begin": begin, "mv": values, "mo": values, "mg": mg, "gatesum": gatesum, "decay": decay, "head": head,
                      "heads": heads}, experts, AHEAD)


def constants():
    f = np.float32
    i = np.arange(P)
    con = np.zeros((P, C_END), f)
    con[:, C_ID:C_ID + P] = np.eye(P, dtype=f)
    con[:, C_LT:C_LT + P] = i[:, None] <= i[None, :]
    con[:, C_UT:C_UT + P] = i[:, None] >= i[None, :]
    con[:, C_ONE:C_ONE + P] = 1.0
    inv = (10000.0 ** (-np.arange(16, dtype=f) / f(16))).astype(f)
    tok = np.arange(2 * P)
    row, colp = (tok // 64).astype(f), (tok % 64).astype(f)
    ang = np.stack([row[:, None] * inv, colp[:, None] * inv], 1)
    cos = np.stack([np.cos(ang), np.cos(ang)], 2).reshape(2, P, HEAD)
    sin = np.stack([-np.sin(ang), np.sin(ang)], 2).reshape(2, P, HEAD)
    for t in range(2):
        con[:, C_COS + t * HEAD:C_COS + (t + 1) * HEAD] = cos[t]
        con[:, C_SIN + t * HEAD:C_SIN + (t + 1) * HEAD] = sin[t]
    con[:, C_IOTA:C_IOTA + TOPK] = np.arange(TOPK)
    mask = np.full((P, 4, 4, P), NEG, f)
    for d in range(2):
        for t in range(2):
            mask[:, 2 * d + t, 0:2] = 0.0
            q, s = i[:, None], i[None, :]
            mask[:, 2 * d + t, 2 + t] = np.where(s <= q if d == 0 else s >= q, 0.0, NEG)
            if t == 1 and d == 0:
                mask[:, 1, 2] = 0.0
            if t == 0 and d == 1:
                mask[:, 2, 3] = 0.0
    sel = np.zeros((8, 8, P), f)
    for r in range(8):
        sel[r, r] = 1.0
    return con, mask.reshape(P, 4, 512), sel


def kernel(**inputs):
    import concourse.bacc as _bacc
    from concourse.bass_utils import run_bass_kernel_spmd as _run

    v = {k: np.asarray(b) for k, b in inputs.items()}
    con, mask, sel = constants()

    def chunks(b, n):
        return b.reshape(n, P).T

    order = np.arange(1792)
    order[1024:1536] = 1024 + np.concatenate([np.arange(HEAD) + HEAD * (c + 4 * g) for c in range(4) for g in range(2)])
    b_in, mb = v["ab_b_in"][0][order], v["ml_b_in"][0]
    col = np.concatenate([
        chunks(b_in[0:512], 4), chunks(b_in[512:1024], 4), chunks(v["ab_conv_b"][0], 4), chunks(v["ab_conv_ln_g"][0], 4),
        chunks(v["ab_conv_ln_b"][0], 4), v["ab_conv_w"][0].reshape(TAPS, 4, P).transpose(2, 1, 0).reshape(P, 4 * TAPS),
        chunks(mb[0:512], 4), chunks(mb[512:1024], 4)], axis=1)
    keys = np.stack([v["peer_k1"], v["peer_k2"]], 2)
    arrays = {
        "x": v["x"][0], "ctx": v["ctx"][0],
        "cvec": np.stack([v["c"][0], v["c_ctx"]]).reshape(2, KD, P).transpose(2, 1, 0),
        "con": con, "mask": mask, "sel": sel, "col": col,
        "w_mod": v["w_mod"], "b_mod": v["b_mod"], "ln1_g": v["ln1_g"], "ln1_b": v["ln1_b"], "ln2_g": v["ln2_g"], "ln2_b": v["ln2_b"],
        "ab_w_in": v["ab_w_in"][0][:, order], "ab_b_in": b_in,
        "qk_g": np.concatenate([np.tile(v["ab_q_norm_g"][0], NQH), np.tile(v["ab_k_norm_g"][0], NKV)]),
        "ab_w_out": v["ab_w_out"][0], "ab_b_out": v["ab_b_out"][0],
        "ml_w_in": v["ml_w_in"][0], "ml_b_in": mb, "ml_norm_g": v["ml_norm_g"][0], "ml_w_out": v["ml_w_out"][0], "ml_b_out": v["ml_b_out"][0],
        "w_q": v["peer_w_q"], "keys": keys.transpose(0, 4, 1, 2, 3).reshape(2, P, 16, NK),
        "uv0": np.concatenate([v["peer_u"][0], v["peer_v"][0]], axis=1), "uv1": np.concatenate([v["peer_u"][1], v["peer_v"][1]], axis=1),
    }
    nc = _bacc.Bacc("TRN2", target_bir_lowering=False, num_devices=1)
    given, aps = {}, {}
    for name, b in arrays.items():
        b = np.ascontiguousarray(b)
        given[f"in_{name}"] = b
        aps[name] = nc.dram_tensor(f"in_{name}", b.shape, mybir.dt.from_np(b.dtype), kind="ExternalInput").ap()
    aps["mod_d"] = nc.dram_tensor("mod_d", (2, 2, 6 * D), F32, kind="Internal").ap()
    aps["out"] = nc.dram_tensor("out_x", (2 * P, D), F32, kind="ExternalOutput").ap()
    build(nc, aps)
    r = _run(nc, [given], core_ids=[0])
    return r.results[0]["out_x"].reshape(1, 2 * P, D)
```

```python
import concourse.bass as bass
import numpy as np
from concourse import mybir
from contextlib import ExitStack

F32 = mybir.dt.float32
U32 = mybir.dt.uint32
ALU = mybir.AluOpType
ACT = mybir.ActivationFunctionType
AX = mybir.AxisListType

P = 128
D = 1024
KD = D // P
TILES = 4
LAT = (2, 3)
EPS = 1e-6
ALPHA = 4 ** 0.25
HEAD = 64
NQH, NKV = 8, 2
QKW = (NQH + NKV) * HEAD
CC = 4
TAPS = 31
PAD = TAPS // 2
CW = 256 + 2 * PAD
UW = 256
ST = 256
NS = 2
MH, MDQ, MDV = 4, 128, 256
PH, NK, TOPK = 8, 128, 16
E = PH * TOPK
HALF = PH // 2
NB = 6
RING = 8
GPT = E // RING
GROUP = 1
NDIAG = RING
NW = 3
WIDE, DEEP = 4, 4
NCAND = WIDE * TOPK + (TOPK - WIDE) * DEEP
NEG = -1.0e30
LOWEST = -3.0e38

C_ID, C_LT, C_UT, C_ONE, C_COS, C_SIN, C_IOTA, C_END = 0, 128, 256, 384, 512, 640, 768, 784
Q_VB, Q_GB, Q_CB, Q_LG, Q_LB, Q_CW, Q_MQ, Q_MK, Q_END = 0, 4, 8, 12, 16, 20, 144, 148, 152


UNIT_STAGES = ("gate", "val", "q", "mq", "mk", "merge", "mv", "mo")
MODS = 6 * D // UW
CONV_PIECES = 8


def kind(name):
    return name if name in ("ln1", "ln2") else name.rstrip("0123456789")


def part(st):
    return int(st[0][len(kind(st[0])):])


def order():
    def parts(name, n, l, s):
        return [(f"{name}{i}", l, s) for i in range(n)]

    def mixer0(s):
        ready = [("ln1", 0, s)] + parts("gate", 2, 0, s) + parts("val", 2, 0, s)
        qs, conv = parts("q", 2, 0, s) + [("kv", 0, s)], parts("conv", CONV_PIECES, 0, s)
        sc, av = parts("sc", 4, 0, s), parts("av", 4, 0, s)
        if s == 1:
            o = ready + qs + [("rope", 0, s)] + [st for pair in zip(sc, av) for st in pair] + conv
        else:
            mods = [("mod", 0, k) for k in range(8, MODS)]
            o = ready + [st for pair in zip(conv[:3], qs) for st in pair] + [conv[3]] + mods[:4] + [("rope", 0, s)]
            o += [sc[0], sc[1], av[0], sc[2], av[1], sc[3], av[2], av[3]]
            for c in range(4):
                o += mods[4 + 3 * c:7 + 3 * c] + [conv[4 + c]]
        o += [("chan", 0, s)] + parts("merge", 4, 0, s) + [("post", 0, s), ("ln2", 0, s)]
        return o + parts("r", 8, 0, s)[:4]

    def picks(t):
        return [(f"pick{x}{half}", t // 4, t) for half in range(2) for x in "ab"]

    mods = [("mod", 0, k) for k in range(8)]
    walk = mods[:4] + [("norm", 0, 0)] + mods[4:] + mixer0(0) + picks(0)[:2] + [("begin", 0, 0)]
    q = 0

    def experts(k):
        nonlocal q
        walk.append(("experts", q, k))
        q += k

    def spread(stages, groups):
        total, done, went = sum(COST[kind(st[0])] for st in stages), 0, 0
        for st in stages:
            walk.append(st)
            went += COST[kind(st[0])]
            k = round(went / total * groups) - done
            if k > 0:
                experts(k)
                done += k

    def first_experts(l, s, t):
        for st in parts("r", 8, l, s)[4:] + picks(t)[2:] + picks(t + 1):
            if st[0][:5] != "pickb":
                experts(1)
            walk.append(st)

    first_experts(0, 0, 0)
    experts(1)
    spread(mixer0(1) + picks(2)[:2], 2 * GPT - 10)
    experts(2)
    first_experts(0, 1, 2)
    spread([("mod", 1, k) for k in range(MODS)] + [("ln1", 1, 0)]
           + parts("mk", 2, 1, 0) + parts("mv", 4, 1, 0) + [("mg", 1, 0)], 2 * GPT - 7)
    walk += [(n, 1, 1) for n in (
        "ln1", "mg", "logf", "mq0", "gatesum", "mk0", "turnsum", "mv0", "mv1", "mv2", "sel0", "score0", "decay0", "mv3",
        "sel1", "decay1", "score1", "sel2", "head0", "decay2", "mq1", "mk1", "score2", "sel3", "head1", "decay3",
        "score3", "head2", "mo0", "mo1", "mo2", "mo3", "og", "head3")]
    walk += [("heads", 1, 1)] + parts("merge", 4, 1, 1) + [("post", 1, 1), ("ln2", 1, 1)] + parts("r", 8, 1, 1)[:4]
    walk += picks(4)[:2] + [("begin", 1, 0)]
    first_experts(1, 1, 4)
    experts(2 * GPT - 7)

    out = []
    for st in walk:
        if st[0] != "experts":
            out.append(st)
            continue
        q, end = st[1], st[1] + st[2]
        while q < end:
            stop = min(end, (q // GPT + 1) * GPT)
            out.append(("experts", q, stop - q))
            if stop % GPT == 0:
                out.append(("close", stop // GPT - 1, 0))
            q = stop
    return out


COST = {"ln1": 12, "gate": 8, "val": 8, "q": 8, "kv": 8, "rope": 14, "sc": 12, "av": 0, "conv": 8, "chan": 12, "merge": 8,
        "post": 15, "ln2": 12, "r": 10, "picka": 7, "pickb": 9, "mod": 5, "mk": 6, "mv": 6, "mg": 5}


def sooner(walk, kinds):
    out = []
    for st in walk:
        if st[0] == "rope" or st[0] == "head3" and "r" in kinds:
            behind = len(out)
            while kind(out[behind - 1][0]) in ("mod", "mo", "og"):
                behind -= 1
            out.insert(behind, st)
        elif st[0] == "experts" and out and out[-1][0] != "experts" and kind(out[-1][0]) in kinds:
            last = out.pop()
            out += [("experts", st[1], 1), last]
            if st[2] > 1:
                out.append(("experts", st[1] + 1, st[2] - 1))
        else:
            out.append(st)
    for i in range(1, len(out) - 1):
        if out[i][0] == "close" and out[i - 1][0] == "experts" and kind(out[i + 1][0]) in UNIT_STAGES + ("sc", "conv", "mod", "picka", "pickb"):
            out[i], out[i + 1] = out[i + 1], out[i]
    return out


def att_jobs(s):
    return 2 if s == 0 else 4


def plan(walk):
    base, n, units = {}, 0, []
    for st in walk:
        name, l, s = st
        k = kind(name)
        count = {"mod": 1, "ln1": 4, "ln2": 4, "kv": 2, "rope": 3, "chan": 4, "mg": 1, "r": 4, "sc": 4, "gatesum": 1, "turnsum": 1, "score": 2,
                 "head": 4, "heads": 4}.get(k, 2 if k in UNIT_STAGES else 0)
        if k == "av":
            count = att_jobs(s) + 1
        base[st] = n
        n += count
        if k in UNIT_STAGES or k in ("mod", "kv", "mg"):
            units.append(n - 1)
        elif k == "r":
            units.append(base[st] + 1)
    return base, units


def expert_runs(q, count):
    runs, end = [], q + count
    while q < end:
        k = q % GPT
        pairs = (min(end - q, GPT - 2 - k)) // 2 if q % 2 == 0 and 0 < k < GPT - 2 else 0
        if pairs >= 2:
            runs.append((q, pairs))
            q += 2 * pairs
        else:
            runs.append((q, 0))
            q += 1
    return runs


def build(nc, a):
    WALK = order()
    J, UNIT_LAST = plan(WALK)
    PLAIN = UNIT_STAGES + ("mod", "kv", "mg")
    SCALAR_WALK, VECTOR_WALK = sooner(WALK, PLAIN + ("sc",)), sooner(WALK, PLAIN + ("sc", "r"))
    first, second = (VECTOR_WALK.index(("close", p, 0)) for p in range(2))
    assert first < VECTOR_WALK.index(("chan", 0, 1)) < VECTOR_WALK.index(("ln2", 0, 1)) < second
    with ExitStack() as ctx:
        def sb(name, shape, dt=F32):
            return ctx.enter_context(nc.sbuf_tensor(name, shape, dt))

        def sem(name):
            return ctx.enter_context(nc.semaphore(name))

        banks = [ctx.enter_context(nc.psum_tensor(f"bank{i}", [P, 512], F32)) for i in range(NB)]
        expert_sum = ctx.enter_context(nc.psum_tensor("expert_sum", [P, D], F32))

        x = sb("x", [P, TILES, D])
        h = sb("h", [P, TILES, D])
        ht = sb("ht", [P, KD, ST])
        rows = sb("rows", [P, 2, D])
        gmod = sb("gmod", [P, 2, D])
        lngb = sb("lngb", [P, 2, D])
        w = sb("w", [P, NW, KD, UW])
        con = sb("con", [P, C_END])
        col = sb("col", [P, Q_END])
        cvec = sb("cvec", [P, KD, 2])
        kt = sb("kt", [P, TILES * P])
        vv = sb("vv", [P, TILES, P])
        stats = sb("stats", [P, 12])
        mv = sb("mv", [P, 8, 2])
        std = sb("std", [P, 20])
        rstd = sb("rstd", [P, 20])
        gates = sb("gates", [P, TILES * E])
        eid = sb("eid", [P, TILES * E], U32)
        rows_idx = sb("rows_idx", [P, 2, RING], U32)
        dots = sb("dots", [P, 2 * RING])
        gel = sb("gel", [P, 2 * RING])
        wexp = sb("wexp", [P, 2 * RING])
        diag = sb("diag", [P, NDIAG, P])
        small = sb("small", [P, 32])
        gt = sb("gt", [P, TILES, 16])
        lf = sb("lf", [P, TILES, 8])
        la = sb("la", [P, TILES, 8])
        le = sb("le", [P, TILES, 8])
        bc = sb("bc", [P, TILES, 8])
        cg = sb("cg", [P, TILES, 8])
        nm = sb("nm", [P, 8])
        thr = sb("thr", [P, 8])
        den = sb("den", [P, 8])
        top = sb("top", [P, 8])
        ring_all = sb("ring", [P, RING * 2 * D])
        ring = ring_all[:, :].rearrange("p (r n) -> p r n", r=RING)
        AREA = 9720
        arena = sb("arena", [P, AREA])
        at, where = 0, arena

        def cut(n):
            nonlocal at
            at += n
            assert at <= (AREA if where is arena else RING * 2 * D), at
            return where[:, at - n:at]

        ident = con[:, C_ID:C_ID + P]
        bms = (ring_all[0:2, 0:6 * D], arena[0:2, 0:6 * D])
        sg = cut(1024).rearrange("p (c n) -> p c n", c=CC)
        ut = sg.rearrange("p c n -> p (c n)").rearrange("p (t n) -> p t n", t=NS)
        u1 = cut(1024).rearrange("p (c n) -> p c n", c=CC)
        us = (ring_all[:, 8 * D:9 * D].rearrange("p (c n) -> p c n", c=CC), u1)
        pr1 = arena[:, 0:2048].rearrange("p (c n) -> p c n", c=4)
        pr0_ = cut(2048)
        pr0 = pr0_.rearrange("p (c n) -> p c n", c=4)
        qk = pr0_[:, 0:NS * QKW].rearrange("p (t n) -> p t n", t=NS)
        probs = (pr0, pr1)
        pt_ = cut(2048)
        pt = pt_.rearrange("p (c n) -> p c n", c=4)
        tmp1, tmp2 = pt_[:, 0:QKW], pt_[:, QKW:2 * QKW]
        cin = cut(CC * CW).rearrange("p (c n) -> p c n", c=CC)
        qt = cut(1024).rearrange("p (c n) -> p c n", c=4)
        assert at <= AREA - 1408
        qkvb, qkg = arena[:, AREA - 1408:AREA - 640], arena[:, AREA - 640:AREA]
        at = 0
        keys = cut(2048).rearrange("p (c n) -> p c n", c=16)
        qh = cut(512).rearrange("p (s n) -> p s n", s=2)
        tv = cut(512).rearrange("p (t c k) -> p t c k", t=NS, c=16)
        ti = cut(512).bitcast(U32).rearrange("p (t c k) -> p t c k", t=NS, c=16)
        tif = cut(256).rearrange("p (c k) -> p c k", c=16)
        cand = cut(PH * NCAND).rearrange("p (h n) -> p h n", h=PH)
        hot = cut(2048).rearrange("p (h i j) -> p h i j", h=PH, i=TOPK)
        sc = cut(128).rearrange("p (h k) -> p h k", h=PH)
        pos = cut(128).bitcast(U32).rearrange("p (h k) -> p h k", h=PH)
        high = cut(128).bitcast(U32).rearrange("p (h k) -> p h k", h=PH)
        first = cut(128).rearrange("p (h k) -> p h k", h=PH)
        second = cut(128).rearrange("p (h k) -> p h k", h=PH)
        e1 = cut(128).rearrange("p (h k) -> p h k", h=PH)
        e2 = cut(128).rearrange("p (h k) -> p h k", h=PH)
        left = cut(256)
        assert at <= AREA - 1408
        at = 0
        mkt = cut(2048).rearrange("p (h n) -> p h n", h=MH)
        mval = cut(4096).rearrange("p (t n) -> p t n", t=TILES)
        mlb = cut(2064)
        at, where = 0, ring_all
        mqt = cut(1024).rearrange("p (h n) -> p h n", h=MH)
        mask = cut(2048).rearrange("p (r n) -> p r n", r=4)
        sel = cut(1024).rearrange("p (r n) -> p r n", r=8)
        cms = [cut(2048).rearrange("p (r n) -> p r n", r=4) for _ in range(2)]
        am = cut(1024).rearrange("p (r n) -> p r n", r=2)
        att = cut(1024).rearrange("p (r n) -> p r n", r=2)
        ct_ = cut(512)
        normg = cut(1024)
        og = h[:, 0:2, :]
        hh = h[:, 2:4, :]

        bank_full = [sem(f"bank_full{i}") for i in range(NB)]
        bank_drained = [sem(f"bank_drained{i}") for i in range(NB)]
        w_loaded = [sem(f"w_loaded{i}") for i in range(NW)]
        loads = {n: sem(f"in_{n}") for n in (
            "con", "x", "cvec", "bmod", "modstore", "rows", "gmod", "lngb", "qkvb", "keys", "mlb", "mlc")}
        dve_step = sem("dve_step")
        act_step = sem("act_step")
        pool_step = sem("pool_step")
        silu_ready = sem("silu_ready")
        h_ready = sem("h_ready")
        rows_used = sem("rows_used")
        lngb_used = sem("lngb_used")
        var_ready = sem("var_ready")
        std_ready = sem("std_ready")
        post_done = sem("post_done")
        qk_ready = sem("qk_ready")
        rowmax_ready = sem("rowmax_ready")
        probs_ready = sem("probs_ready")
        conv_done = sem("conv_done")
        un_ready = sem("un_ready")
        sc_ready = sem("sc_ready")
        scexp_ready = sem("scexp_ready")
        eid_ready = sem("eid_ready")
        idx_staged = sem("idx_staged")
        slots_free = sem("slots_free")
        row_in = [sem(f"row_in{i}") for i in range(RING)]
        dots_ready = sem("dots_ready")
        gelu_ready = sem("gelu_ready")
        wexp_ready = sem("wexp_ready")
        diag_ready = sem("diag_ready")
        sum_taken = sem("sum_taken")
        lf_a = sem("lf_a")
        lf_e = sem("lf_e")
        lf_ready = sem("lf_ready")
        cg_ready = sem("cg_ready")
        decay_full = sem("decay_full")
        decay_taken = sem("decay_taken")
        nm_ready = sem("nm_ready")
        wm_ready = sem("wm_ready")
        am_ready = sem("am_ready")
        sig_ready = sem("sig_ready")
        y_ready = sem("y_ready")
        stored = sem("stored")

        def bank(n):
            return banks[n % NB]

        def job_done(eng, n):
            eng.wait_ge(bank_full[n % NB], n // NB + 1)

        def job_drained(eng, n):
            eng.wait_ge(bank_drained[n % NB], n // NB + 1)

        def jobs_drained(eng, last, first=0):
            for n in range(max(first, last - NB + 1), last + 1):
                job_drained(eng, n)

        def drains(ins, n):
            ins.then_inc(bank_drained[n % NB], 1)

        def walk_all(stages, experts, walk=WALK):
            for st in walk:
                if st[0] == "experts":
                    experts(st[1], st[2])
                elif kind(st[0]) in stages:
                    stages[kind(st[0])](st)

        block = ctx.enter_context(nc.Block())

        @block.sync
        def _(sp):
            unit_no = [0]
            ROWS_USERS = [st for st in WALK if st[0] in ("ln1", "ln2", "merge3")]

            def load_unit(src):
                n = unit_no[0]
                unit_no[0] += 1
                if n >= NW:
                    job_done(sp, UNIT_LAST[n - NW])
                cols = src.shape[1]
                sp.dma_start(w[:, n % NW, :, 0:cols], src.rearrange("(k p) n -> p k n", p=P)).then_inc(w_loaded[n % NW], 16)

            def unit(mat, lo):
                load_unit(mat[:, lo:lo + UW])

            def mod_row(l, s, i, dst, name):
                sp.dma_start(dst, a["mod_d"][l, 1 - s, i * D:(i + 1) * D].partition_broadcast(P)).then_inc(loads[name], 16)

            def everywhere(vec, dst, name):
                sp.dma_start(dst, vec.partition_broadcast(P)).then_inc(loads[name], 16)

            def store_mod(l, part):
                for k in range(8 * part, 8 * part + 8):
                    job_drained(sp, J["mod", l, k])
                src = bms[l][:, part * 2 * D:(part + 1) * 2 * D]
                sp.dma_start(a["mod_d"][l, :, part * 2 * D:(part + 1) * 2 * D], src).then_inc(loads["modstore"], 16)

            def free_rows(st):
                sp.wait_ge(rows_used, ROWS_USERS.index(st))

            def shift_scale(l, s, i, st):
                if ROWS_USERS.index(st):
                    free_rows(st)
                for k in range(2):
                    mod_row(l, s, i + k, rows[:, k, :], "rows")

            def mod(st):
                _, l, k = st
                if l == 1 and k == NW:
                    sp.wait_ge(eid_ready, 8)
                    sp.dma_start(bms[1], a["b_mod"][1].partition_broadcast(2)).then_inc(loads["bmod"], 16)
                    everywhere(a["ml_b_in"][1024:3088], mlb, "mlb")
                if l == 1 and k in (10, 18):
                    store_mod(1, k // 8 - 1)
                unit(a["w_mod"][l], k * UW)

            def ln1(st):
                _, l, s = st
                if l == 0 and s == 0:
                    unit(a["ab_w_in"], 512)
                    unit(a["ab_w_in"], 512 + UW)
                    store_mod(0, 0)
                    sp.wait_ge(loads["modstore"], 16)
                    shift_scale(0, 0, 0, st)
                elif l == 0:
                    pass
                else:
                    if s == 0:
                        store_mod(1, 2)
                    sp.wait_ge(loads["modstore"], 96)
                    shift_scale(1, s, 0, st)

            def gatesum(st):
                sp.wait_ge(slots_free, RING + 4 * E)
                sp.dma_start(mask[:, :, :], a["mask"]).then_inc(loads["mlc"], 16)
                sp.dma_start(sel[0:8, :, :], a["sel"]).then_inc(loads["mlc"], 16)
                everywhere(a["ml_norm_g"], normg, "mlc")

            def gate(st):
                if st[2] == 1:
                    unit(a["ab_w_in"], 512 + UW * part(st))

            def val(st):
                unit(a["ab_w_in"], UW * part(st))

            def q(st):
                if st[2] == 0 and part(st) == 0:
                    everywhere(a["ab_b_in"][1024:1792], qkvb, "qkvb")
                    everywhere(a["qk_g"], qkg, "qkvb")
                unit(a["ab_w_in"], 1024 + UW * part(st))

            def kv(st):
                unit(a["ab_w_in"], 1536)

            def chan(st):
                s = st[2]
                for k in range(2):
                    unit(a["ab_w_out"], UW * k)
                if s == 0:
                    store_mod(0, 1)
                    store_mod(0, 2)
                    sp.wait_ge(loads["modstore"], 48)
                free_rows(("merge3", 0, s))
                everywhere(a["ab_b_out"], rows[:, 0, :], "rows")
                mod_row(0, s, 2, gmod[:, s, :], "gmod")
                if s == 1:
                    sp.wait_ge(lngb_used, 2)
                everywhere(a["ln1_g"][0], lngb[:, 0, :], "lngb")
                everywhere(a["ln1_b"][0], lngb[:, 1, :], "lngb")

            def merge(st):
                name, l, s = st
                if l == 1 and name == "merge0":
                    free_rows(("merge3", 1, 1))
                    everywhere(a["ml_b_out"], rows[:, 0, :], "rows")
                    mod_row(1, 1, 2, gmod[:, 0, :], "gmod")
                    sp.wait_ge(lngb_used, 4)
                    everywhere(a["ln1_g"][1], lngb[:, 0, :], "lngb")
                    everywhere(a["ln1_b"][1], lngb[:, 1, :], "lngb")
                if l or part(st) >= 2:
                    unit(a["ml_w_out" if l else "ab_w_out"], UW * part(st))

            def post(st):
                _, l, s = st
                unit(a["w_q"][l], 0)
                unit(a["w_q"][l], UW)
                if l == 1:
                    mod_row(1, 1, 5, gmod[:, 1, :], "gmod")
                shift_scale(l, s, 3, ("ln2", l, s))
                sp.dma_start(keys[:, :, :], a["keys"][l]).then_inc(loads["keys"], 16)

            def ln2(st):
                _, l, s = st
                sp.wait_ge(lngb_used, (1 + 2 * s) if l == 0 else 5)
                if l == 0:
                    mod_row(0, s, 5, gmod[:, s, :], "gmod")
                everywhere(a["ln2_g"][l], lngb[:, 0, :], "lngb")
                everywhere(a["ln2_b"][l], lngb[:, 1, :], "lngb")

            def router(st):
                name, l, s = st
                c = part(st)
                if c >= 2:
                    unit(a["w_q"][l], UW * c)
                if c == 7 and l == 0 and s == 0:
                    shift_scale(0, 1, 0, ("ln1", 0, 1))

            def mlstm_in(lo):
                return lambda st: unit(a["ml_w_in"], lo + UW * part(st))

            def mg(st):
                load_unit(a["ml_w_in"][:, 3072:3088])

            sp.dma_start(cvec[:, :, :], a["cvec"]).then_inc(loads["cvec"], 16)
            sp.dma_start(bms[0], a["b_mod"][0].partition_broadcast(2)).then_inc(loads["bmod"], 16)
            for k in range(NW):
                unit(a["w_mod"][0], UW * k)
            for t in range(TILES):
                sp.dma_start(x[:, t, :], (a["ctx"] if t < 2 else a["x"])[(t % 2) * P:(t % 2 + 1) * P, :]).then_inc(loads["x"], 16)
            sp.dma_start(con[:, :], a["con"]).then_inc(loads["con"], 16)
            sp.dma_start(col[:, :], a["col"]).then_inc(loads["con"], 16)

            def mod_first(st):
                if st[1] or st[2] >= NW:
                    mod(st)

            walk_all({"mod": mod_first, "ln1": ln1, "gate": gate, "val": val, "q": q, "kv": kv, "chan": chan, "merge": merge,
                      "post": post, "ln2": ln2, "r": router, "mq": mlstm_in(0), "mk": mlstm_in(512),
                      "mv": mlstm_in(1024), "mo": mlstm_in(2048), "gatesum": gatesum, "mg": mg}, lambda q, k: None)
            for n in range(2):
                sp.wait_ge(post_done, 11 + n)
                sp.dma_start(a["out"][n * P:(n + 1) * P, :], x[:, 2 + n, :]).then_inc(stored, 16)
            sp.wait_ge(stored, 32)

        @block.gpsimd
        def _(pool):
            pool.sem_inc(slots_free, RING)
            for p in range(6):
                l = p // 4
                if p in (0, 4):
                    pool.wait_ge(eid_ready, 2 * p + 1)
                with pool.Fori(0, GPT // 2) as i:
                    for j in range(2 * RING):
                        pool.wait_ge(slots_free, p * E + i * 2 * RING + j + 1)
                        pool.sem_inc(pool_step, 1)
                        pool.wait_ge(idx_staged, p * GPT + i * 2 + j // RING + 1)
                        pool.sem_inc(pool_step, 1)
                        pool.indirect_dma_start(
                            out=ring[:, j % RING, :], out_offset=None, in_=a[f"uv{l}"][:, :],
                            in_offset=bass.IndirectOffsetOnAxis(ap=rows_idx[:, j // RING, j % RING:j % RING + 1], axis=0),
                        ).then_inc(row_in[j % RING], 16)

        @block.tensor
        def _(pe):
            unit_no = [0]

            def next_unit():
                n = unit_no[0]
                unit_no[0] += 1
                pe.wait_ge(w_loaded[n % NW], 16 * (n // NW + 1))
                return w[:, n % NW]

            def open_bank(n):
                if n >= NB:
                    job_drained(pe, n - NB)

            def group(n, out, pairs):
                open_bank(n)
                for i, (l, r) in enumerate(pairs):
                    mm = pe.matmul(out, l, r, start=(i == 0), stop=(i == len(pairs) - 1))
                mm.then_inc(bank_full[n % NB], 1)

            def turn(n, parts):
                open_bank(n)
                for out, src in parts:
                    k = src.shape[0]
                    mm = pe.transpose(out, src, con[0:k, C_ID:C_ID + k])
                mm.then_inc(bank_full[n % NB], 1)

            def by_channel(n, wu, c):
                group(n, bank(n)[:, 0:ST], [(wu[:, k, c * P:(c + 1) * P], ht[:, k, :]) for k in range(KD)])

            def by_token(n, wu, i):
                group(n, bank(n)[:, 0:UW], [(ht[:, k, i * P:(i + 1) * P], wu[:, k, :]) for k in range(KD)])

            def mod(st):
                if st == ("mod", 0, 0):
                    pe.wait_ge(silu_ready, 1)
                n = J[st]
                wu = next_unit()
                group(n, bank(n)[0:2, 0:UW], [(cvec[:, k, :], wu[:, k, :]) for k in range(KD)])

            h_tiles = [0]

            def turn_h(st):
                if st == ("ln1", 0, 0):
                    pe.wait_ge(loads["con"], 32)
                s = st[2]
                for i in range(NS):
                    h_tiles[0] += 1
                    pe.wait_ge(h_ready, h_tiles[0])
                    for j in range(2):
                        n = J[st] + 2 * i + j
                        turn(n, [(bank(n)[:, c * P:(c + 1) * P], h[:, NS * s + i, (4 * j + c) * P:(4 * j + c + 1) * P]) for c in range(4)])
                jobs_drained(pe, J[st] + 3)

            def channels(st):
                wu = next_unit()
                for c in range(2):
                    by_channel(J[st] + c, wu, c)

            def tokens(st):
                if st[0] in ("merge0",):
                    jobs_drained(pe, J[st] - 1)
                wu = next_unit()
                for i in range(NS):
                    by_token(J[st] + i, wu, i)

            def rope(st):
                s = st[2]
                for i in range(NS):
                    pe.wait_ge(qk_ready, NS * s + i + 1)
                    n = J[st] + i
                    turn(n, [(bank(n)[:, c * P:(c + 1) * P], qk[:, i, c * P:(c + 1) * P]) for c in range(4)])
                n = J[st] + 2
                turn(n, [(bank(n)[:, i * P:(i + 1) * P], qk[:, i, 512:640]) for i in range(NS)])
                jobs_drained(pe, n)

            def scores(st):
                s, i = st[2], part(st)
                t, g, nk = i // 2, i % 2, ST * (1 + s)
                for c in range(4):
                    n = J[st] + c
                    group(n, bank(n)[:, 0:nk], [(qt[64 * g:64 * g + 64, c, t * P:(t + 1) * P], kt[64 * g:64 * g + 64, 0:nk])])

            def attention(st):
                s, i = st[2], part(st)
                g, nkc = i % 2, att_jobs(s)
                turned, n = J[st], J[st] + nkc
                pe.wait_ge(probs_ready, 16 * s + 4 * (i + 1))
                for kc in range(nkc):
                    m = turned + kc
                    turn(m, [(bank(m)[:, b * P:(b + 1) * P], probs[i % 2][:, hq, kc * P:(kc + 1) * P]) for b, hq in enumerate((0, 2, 1, 3))])
                open_bank(n)
                jobs_drained(pe, n - 1, turned)
                for odd in range(2):
                    for kc in range(nkc):
                        mm = pe.matmul(bank(n)[64 * odd:64 * odd + 64, 0:256], vv[:, kc, g * 64:(g + 1) * 64],
                                       pt[:, kc, 256 * odd:256 * odd + 256], start=(kc == 0), stop=(kc == nkc - 1))
                mm.then_inc(bank_full[n % NB], 1)

            def chan(st):
                s = st[2]
                pe.wait_ge(conv_done, s + 1)
                for i in range(NS):
                    n = J[st] + i
                    turn(n, [(bank(n)[:, c * P:(c + 1) * P], us[s][:, c, i * P:(i + 1) * P]) for c in range(CC)])
                pe.wait_ge(un_ready, s + 1)
                for b in range(2):
                    n = J[st] + 2 + b
                    turn(n, [(bank(n)[:, (2 * c + i) * P:(2 * c + i + 1) * P], ut[:, i, (2 * b + c) * P:(2 * b + c + 1) * P])
                             for c in range(2) for i in range(NS)])

            def router(st):
                name, l, s = st
                if name == "r0":
                    pe.wait_ge(loads["keys"], 16 * (2 * l + s + 1 - l))
                wu = next_unit()
                for c in range(2):
                    by_channel(J[st] + c, wu, c)
                for c in range(2):
                    n = J[st] + 2 + c
                    open_bank(n)
                    job_drained(pe, n - 2)
                    for i in range(NS):
                        mm = pe.matmul(bank(n)[:, i * NK:(i + 1) * NK], qh[:, c, i * P:(i + 1) * P], keys[:, 2 * part(st) + c, :], start=True, stop=True)
                    mm.then_inc(bank_full[n % NB], 1)

            def experts(q0, count):
                def rows8(q, half, first, last):
                    for j in range(RING):
                        pe.wait_ge(diag_ready, q * RING + j + 1)
                        for c in range(2):
                            mm = pe.matmul(expert_sum[:, c * 512:(c + 1) * 512], diag[:, j % NDIAG, :],
                                           ring[:, j, D + c * 512:D + (c + 1) * 512],
                                           start=(first and j == 0), stop=(last and j == RING - 1))
                        mm.then_inc(slots_free, 1)

                for q, pairs in expert_runs(q0, count):
                    if q % GPT == 0 and q:
                        pe.wait_ge(sum_taken, q // GPT)
                    if pairs:
                        with pe.Fori(0, pairs) as i:
                            rows8(q + 2 * i, 0, False, False)
                            rows8(q + 2 * i + 1, 1, False, False)
                    else:
                        rows8(q, q % 2, q % GPT == 0, q % GPT == GPT - 1)

            def mg(st):
                n = J[st]
                open_bank(n)
                wu = next_unit()
                for i in range(NS):
                    for k in range(KD):
                        mm = pe.matmul(bank(n)[:, i * 16:(i + 1) * 16], ht[:, k, i * P:(i + 1) * P], wu[:, k, 0:16], start=(k == 0), stop=(k == KD - 1))
                mm.then_inc(bank_full[n % NB], 1)

            def gatesum(st):
                n = J[st]
                open_bank(n)
                pe.wait_ge(lf_ready, 1)
                lt, utr, one = con[:, C_LT:C_LT + P], con[:, C_UT:C_UT + P], con[:, C_ONE:C_ONE + P]
                before = {(0, t): list(range(t)) for t in range(TILES)}
                before.update({(1, 0): [1], (1, 1): [], (1, 2): [3, 0, 1], (1, 3): [0, 1]})
                for t in range(TILES):
                    for d in range(2):
                        terms = [(utr if d else lt, t)] + [(one, b) for b in before[d, t]]
                        for i, (m, b) in enumerate(terms):
                            mm = pe.matmul(bank(n)[:, t * 8 + 4 * d:t * 8 + 4 * d + 4], m, lf[:, b, 4 * d:4 * d + 4], start=(i == 0), stop=(i == len(terms) - 1))
                mm.then_inc(bank_full[n % NB], 1)

            def turnsum(st):
                n = J[st]
                pe.wait_ge(cg_ready, 1)
                turn(n, [(bank(n)[0:8, t * P:(t + 1) * P], cg[:, t, :]) for t in range(TILES)])

            def sel_(st):
                hd = part(st)
                if hd == 0:
                    job_drained(pe, J["turnsum", 1, 1])
                    pe.wait_ge(loads["mlc"], 48)
                for d in range(2):
                    if hd:
                        pe.wait_ge(decay_taken, 2 * (hd - 1) + d + 1)
                    pe.matmul(expert_sum[:, d * 512:(d + 1) * 512], sel[0:8, 4 * d + hd, :], ct_[0:8, :], start=True, stop=True).then_inc(decay_full, 1)

            def score(st):
                jobs_drained(pe, J[f"mk{part(st) // 2}", 1, 1] + 1)
                for i in range(2):
                    group(J[st] + i, bank(J[st] + i)[:, :], [(mqt[:, part(st), i * P:(i + 1) * P], mkt[:, part(st), :])])

            def head(st):
                hd, b0 = part(st), J[st]
                for i in range(2):
                    pe.wait_ge(am_ready, 2 * hd + i + 1)
                    turn(b0 + i, [(bank(b0 + i)[:, kc * P:(kc + 1) * P], am[:, i, kc * P:(kc + 1) * P]) for kc in range(4)])
                for i in range(2):
                    job_drained(pe, J[f"mv{hd}", 1, 1] + i)
                for i in range(2):
                    job_drained(pe, b0 + i)
                    n = b0 + 2 + i
                    group(n, bank(n)[:, 0:MDV], [(att[:, i, kc * P:(kc + 1) * P], mval[:, kc, hd * MDV:(hd + 1) * MDV]) for kc in range(4)])

            def heads(st):
                for i in range(NS):
                    pe.wait_ge(y_ready, i + 1)
                    for j in range(2):
                        n = J[st] + 2 * i + j
                        turn(n, [(bank(n)[:, c * P:(c + 1) * P], hh[:, i, (4 * j + c) * P:(4 * j + c + 1) * P]) for c in range(4)])

            walk_all({"mod": mod, "ln1": turn_h, "ln2": turn_h, "gate": channels, "val": channels, "mq": channels, "mk": channels,
                      "q": tokens, "kv": tokens, "merge": tokens, "mv": tokens, "mo": tokens, "rope": rope, "sc": scores, "av": attention,
                      "chan": chan, "r": router, "mg": mg, "gatesum": gatesum, "turnsum": turnsum,
                      "sel": sel_, "score": score, "head": head, "heads": heads}, experts)

        @block.scalar
        def _(act):
            stds = [0]

            def copy_out(n, dst, src):
                job_done(act, n)
                drains(act.activation(dst, src, ACT.Copy), n)

            def square_root(cols):
                stds[0] += 1
                act.wait_ge(var_ready, stds[0])
                act.activation(std[:, 0:cols], std[:, 0:cols], ACT.Sqrt).then_inc(std_ready, 1)

            def four(ap):
                return ap.rearrange("p (c n) -> p c n", c=4)

            def turn_h(st):
                if st == ("ln1", 0, 0):
                    act.wait_ge(loads["con"], 32)
                else:
                    square_root(4)
                for i in range(NS):
                    for j in range(2):
                        n = J[st] + 2 * i + j
                        copy_out(n, ht[:, 4 * j:4 * j + 4, i * P:(i + 1) * P], four(bank(n)[:, :]))

            def gate(st):
                for c in range(2 * part(st), 2 * part(st) + 2):
                    n = J[st] + c % 2
                    job_done(act, n)
                    drains(act.activation(sg[:, c, :], bank(n)[:, 0:ST], ACT.Sigmoid, bias=col[:, Q_GB + c:Q_GB + c + 1]), n)

            def rope(st):
                s = st[2]
                square_root(20)
                for i in range(NS):
                    n = J[st] + i
                    copy_out(n, qt[:, :, i * P:(i + 1) * P], four(bank(n)[:, :]))
                copy_out(J[st] + 2, kt[:, s * ST:(s + 1) * ST], bank(J[st] + 2)[:, 0:ST])

            def scores(st):
                s, i = st[2], part(st)
                nk = ST * (1 + s)
                if i >= 2:
                    job_done(act, J[f"av{i - 2}", 0, s] + att_jobs(s) - 1)
                for c in range(4):
                    n = J[st] + c
                    act.wait_ge(rowmax_ready, 16 * s + 4 * i + c + 1)
                    job_done(act, n)
                    k = (4 * i + c) % 8
                    drains(act.activation(probs[i % 2][:, c, 0:nk], bank(n)[:, 0:nk], ACT.Exp, bias=small[:, k:k + 1],
                                          scale=HEAD ** -0.5, accum_out=small[:, 8 + k:9 + k]), n)

            def attention(st):
                s, i = st[2], part(st)
                t, g = i // 2, i % 2
                turned, n = J[st], J[st] + att_jobs(s)
                if i:
                    job_done(act, J[f"av{i - 1}", 0, s] + att_jobs(s))
                for kc in range(att_jobs(s)):
                    copy_out(turned + kc, pt[:, kc, :], bank(turned + kc)[:, :])
                copy_out(n, ht[:, 4 + 2 * g:6 + 2 * g, t * P:(t + 1) * P], bank(n)[:, 0:256].rearrange("p (c n) -> p c n", c=2))

            def chan(st):
                for i in range(NS):
                    copy_out(J[st] + i, ut[:, i, :], bank(J[st] + i)[:, :])
                square_root(4)
                for c in range(CC):
                    n = J[st] + 2 + c // 2
                    job_done(act, n)
                    ins = act.activation(ht[:, c, :], bank(n)[:, (c % 2) * ST:(c % 2 + 1) * ST], ACT.Silu,
                                         bias=col[:, Q_LB + c:Q_LB + c + 1], scale=col[:, Q_LG + c:Q_LG + c + 1])
                    if c % 2:
                        drains(ins, n)

            def router(st):
                for c in range(2):
                    if part(st):
                        job_done(act, J[f"r{part(st) - 1}", st[1], st[2]] + 2 + c)
                    copy_out(J[st] + c, qh[:, c, :], bank(J[st] + c)[:, 0:ST])

            def picks(st):
                half = part(st)
                hs = slice(4 * half, 4 * half + 4)
                act.wait_ge(sc_ready, 2 * st[2] + half + 1)
                act.activation(sc[:, hs, :], sc[:, hs, :], ACT.Exp).then_inc(scexp_ready, 1)

            def experts(q0, count):
                def rows8(q, half, column):
                    for j in range(0, RING, GROUP):
                        b = half * RING + j
                        act.wait_ge(dots_ready, q * RING + j + GROUP)
                        act.activation(gel[:, b:b + GROUP], dots[:, b:b + GROUP], ACT.Gelu).then_inc(gelu_ready, 1)
                        act.wait_ge(gelu_ready, q * (RING // GROUP) + j // GROUP + 1)
                        for k in range(GROUP):
                            act.activation(wexp[:, b + k:b + k + 1], gel[:, b + k:b + k + 1], ACT.Copy,
                                           scale=gates[:, bass.ds(column + j + k, 1)]).then_inc(wexp_ready, 1)
                        for k in range(GROUP):
                            act.wait_ge(wexp_ready, q * RING + j + k + 1)
                            act.wait_ge(slots_free, q * RING + j + k + 1 + RING - NDIAG)
                            act.activation(diag[:, (j + k) % NDIAG, :], ident, ACT.Copy, scale=wexp[:, b + k:b + k + 1]).then_inc(diag_ready, 1)

                for q, pairs in expert_runs(q0, count):
                    column = (q - q // (4 * GPT) * 4 * GPT) * RING
                    if pairs:
                        with act.Fori(0, pairs) as i:
                            rows8(q + 2 * i, 0, column + i * 2 * RING)
                            rows8(q + 2 * i + 1, 1, column + i * 2 * RING + RING)
                    else:
                        rows8(q, q % 2, column)

            def to_channels(dst, first):
                def stage(st):
                    lo = ST * st[2] if kind(st[0]) == "mk" else 0
                    for c in range(2 * part(st), 2 * part(st) + 2):
                        n = J[st] + c % 2
                        job_done(act, n)
                        drains(act.activation(dst[:, c, lo:lo + ST], bank(n)[:, 0:ST], ACT.Identity, bias=col[:, first + c:first + c + 1]), n)
                return stage

            def logf(st):
                act.wait_ge(lf_a, 1)
                act.activation(le[:, :, :], la[:, :, :], ACT.Exp, scale=-1.0).then_inc(act_step, 1)
                act.wait_ge(act_step, 1)
                act.activation(le[:, :, :], le[:, :, :], ACT.Ln, bias=con[:, C_ONE:C_ONE + 1]).then_inc(lf_e, 1)

            def turnsum(st):
                copy_out(J[st], ct_[0:8, :], bank(J[st])[0:8, :])

            def decay(st):
                hd = part(st)
                cm, b = cms[hd % 2], 4 * (hd % 2)
                for d in range(2):
                    for i in range(2):
                        r = 2 * d + i
                        act.wait_ge(nm_ready, 4 * hd + r + 1)
                        act.activation(cm[:, r, :], cm[:, r, :], ACT.Exp, bias=nm[:, b + r:b + r + 1])
                        act.activation(thr[:, b + r:b + r + 1], bc[:, 2 + i, 4 * d + hd:4 * d + hd + 1], ACT.Exp,
                                       bias=nm[:, b + r:b + r + 1], scale=-1.0).then_inc(wm_ready, 1)

            def head(st):
                hd = part(st)
                for i in range(2):
                    if hd:
                        job_done(act, J[f"head{hd - 1}", 1, 1] + 2 + i)
                    copy_out(J[st] + i, att[:, i, :], bank(J[st] + i)[:, :])
                for i in range(2):
                    n = J[st] + 2 + i
                    copy_out(n, hh[:, i, hd * MDV:(hd + 1) * MDV], bank(n)[:, 0:MDV])

            def output_gate(st):
                jobs_drained(act, J["mo3", 1, 1] + 1)
                act.activation(og[:, :, :], og[:, :, :], ACT.Sigmoid).then_inc(sig_ready, 1)

            def heads(st):
                square_root(8)
                for i in range(NS):
                    for j in range(2):
                        n = J[st] + 2 * i + j
                        copy_out(n, ht[:, 4 * j:4 * j + 4, i * P:(i + 1) * P], four(bank(n)[:, :]))

            act.wait_ge(loads["cvec"], 16)
            act.activation(cvec[:, :, :], cvec[:, :, :], ACT.Silu).then_inc(silu_ready, 1)
            walk_all({"ln1": turn_h, "ln2": turn_h, "gate": gate, "rope": rope, "sc": scores, "av": attention, "chan": chan,
                      "post": lambda st: square_root(4), "r": router, "picka": picks, "mq": to_channels(mqt, Q_MQ),
                      "mk": to_channels(mkt, Q_MK), "logf": logf, "turnsum": turnsum, "decay": decay, "head": head,
                      "og": output_gate, "heads": heads, "norm": lambda st: square_root(4),
                      "close": lambda st: square_root(4)}, experts, SCALAR_WALK)

        @block.vector
        def _(dve):
            cnt = {}

            def count(name, by=1):
                cnt[name] = cnt.get(name, 0) + by
                return cnt[name]

            def do(ins):
                ins.then_inc(dve_step, 1)
                dve.wait_ge(dve_step, count("step"))

            def chains(ins):
                ins.then_inc(dve_step, 1)
                dve.wait_ge(dve_step, count("step") - 1)

            def chains_end():
                dve.wait_ge(dve_step, cnt["step"])

            def loaded(name, n):
                dve.wait_ge(loads[name], 16 * count(name, n))

            def root(cols):
                dve.wait_ge(std_ready, count("std"))
                do(dve.reciprocal(rstd[:, 0:cols], std[:, 0:cols]))

            def mean_var(src, k):
                width = src.shape[1]
                parts = max(1, width // 512)
                for i in range(parts):
                    do(dve.bn_stats(stats[:, 6 * i:6 * i + 6], src[:, i * 512:min((i + 1) * 512, width)]))
                do(dve.bn_aggr(mv[:, k, :], stats[:, 0:6 * parts]))

            def var_out(cols):
                dve.tensor_scalar(std[:, 0:cols], mv[:, 0:cols, 1], EPS, None, ALU.add).then_inc(var_ready, 1)

            def turns(tiles):
                return chains if len(tiles) == 2 else do

            def normalize(tiles):
                for i, (src, _) in enumerate(tiles):
                    mean_var(src, i)
                var_out(4)
                root(4)
                for i, (src, dst) in enumerate(tiles):
                    turns(tiles)(dve.tensor_scalar(dst, src, mv[:, i, 0:1], rstd[:, i:i + 1], ALU.subtract, ALU.mult))
                chains_end()

            def post_norm(tiles, s, y):
                after = turns(tiles)
                for t in tiles:
                    after(dve.tensor_tensor(h[:, t, :], y if y is not None else h[:, t, :], gmod[:, s, :], ALU.mult))
                    if y is not None:
                        dve.sem_inc(sum_taken, 1)
                for t in tiles:
                    after(dve.scalar_tensor_tensor(out=x[:, t, :], in0=x[:, t, :], scalar=ALPHA, in1=h[:, t, :], op0=ALU.mult, op1=ALU.add))
                chains_end()
                normalize([(x[:, t, :], x[:, t, :]) for t in tiles])
                for t in tiles:
                    after(dve.tensor_tensor(x[:, t, :], x[:, t, :], lngb[:, 0, :], ALU.mult))
                chains_end()
                for t in tiles:
                    dve.tensor_tensor(x[:, t, :], x[:, t, :], lngb[:, 1, :], ALU.add).then_inc(post_done, 1)
                dve.wait_ge(post_done, count("post", len(tiles)))

            def mod(st):
                _, l, k = st
                bm, lo = bms[l], k * UW
                if k == 0:
                    loaded("bmod", 1)
                n = J[st]
                job_done(dve, n)
                drains(dve.tensor_tensor(bm[:, lo:lo + UW], bank(n)[0:2, 0:UW], bm[:, lo:lo + UW], ALU.add), n)

            def first_norm(st):
                dve.wait_ge(loads["x"], 64)
                dve.wait_ge(loads["con"], 32)
                normalize([(x[:, t, :], h[:, t, :]) for t in range(NS)])

            def modulate(st):
                s = st[2]
                tiles = [NS * s + i for i in range(NS)]
                if st != ("ln1", 0, 0):
                    normalize([(x[:, t, :], h[:, t, :]) for t in tiles])
                loaded("rows", 2)
                for t in tiles:
                    chains(dve.scalar_tensor_tensor(out=h[:, t, :], in0=rows[:, 1, :], scalar=1.0, in1=h[:, t, :], op0=ALU.add, op1=ALU.mult))
                chains_end()
                for t in tiles:
                    dve.tensor_tensor(h[:, t, :], h[:, t, :], rows[:, 0, :], ALU.add).then_inc(h_ready, 1)
                dve.wait_ge(h_ready, count("h", NS))
                dve.sem_inc(rows_used, 1)

            def val(st):
                if part(st) == 0:
                    do(dve.memset(cin[:, :, 0:PAD], 0.0))
                    do(dve.memset(cin[:, :, PAD + ST:CW], 0.0))
                for c in range(2 * part(st), 2 * part(st) + 2):
                    n = J[st] + c % 2
                    job_drained(dve, J[f"gate{part(st)}", 0, st[2]] + c % 2)
                    job_done(dve, n)
                    drains(dve.scalar_tensor_tensor(out=cin[:, c, PAD:PAD + ST], in0=bank(n)[:, 0:ST], scalar=col[:, Q_VB + c:Q_VB + c + 1],
                                                    in1=sg[:, c, :], op0=ALU.add, op1=ALU.mult), n)

            def q(st):
                c = part(st)
                if st[2] == 0 and c == 0:
                    loaded("qkvb", 2)
                for i in range(NS):
                    n = J[st] + i
                    job_done(dve, n)
                    drains(dve.tensor_tensor(qk[:, i, c * UW:(c + 1) * UW], bank(n)[:, 0:UW], qkvb[:, c * UW:(c + 1) * UW], ALU.add), n)

            def kv(st):
                for i in range(NS):
                    n = J[st] + i
                    job_done(dve, n)
                    do(dve.tensor_tensor(qk[:, i, 512:640], bank(n)[:, 0:128], qkvb[:, 512:640], ALU.add))
                    drains(dve.tensor_tensor(vv[:, NS * st[2] + i, :], bank(n)[:, 128:256], qkvb[:, 640:768], ALU.add), n)

            def heads_of(ap):
                return ap.rearrange("p (h d) -> p h d", d=HEAD)

            NH = NQH + NKV

            def rope(st):
                s = st[2]
                jobs_drained(dve, J["kv", 0, s] + 1)
                for i in range(NS):
                    do(dve.tensor_tensor(tmp1, qk[:, i, :], qk[:, i, :], ALU.mult))
                    do(dve.tensor_reduce(std[:, NH * i:NH * (i + 1)], heads_of(tmp1), AX.X, ALU.add))
                dve.tensor_scalar(std[:, :], std[:, :], 1.0 / HEAD, EPS, ALU.mult, ALU.add).then_inc(var_ready, 1)
                root(NS * NH)
                for i in range(NS):
                    hq = heads_of(qk[:, i, :])
                    do(dve.tensor_tensor(hq, hq, rstd[:, NH * i:NH * (i + 1)].unsqueeze(2).broadcast_to([P, NH, HEAD]), ALU.mult))
                    last = dve.tensor_tensor(qk[:, i, :], qk[:, i, :], qkg, ALU.mult)
                    if s == 1:
                        do(last)
                        cs = con[:, C_COS + i * HEAD:C_COS + (i + 1) * HEAD]
                        sn = con[:, C_SIN + i * HEAD:C_SIN + (i + 1) * HEAD].rearrange("p (a b f) -> p a b f", a=2, b=2)
                        do(dve.tensor_tensor(heads_of(tmp1), hq, cs.unsqueeze(1).broadcast_to([P, NH, HEAD]), ALU.mult))
                        q4 = qk[:, i, :].rearrange("p (h a b f) -> p h a b f", a=2, b=2, f=16)
                        t4 = tmp2.rearrange("p (h a b f) -> p h a b f", a=2, b=2, f=16)
                        for b in range(2):
                            do(dve.tensor_tensor(t4[:, :, :, b, :], q4[:, :, :, 1 - b, :],
                                                 sn[:, :, b, :].unsqueeze(1).broadcast_to([P, NH, 2, 16]), ALU.mult))
                        last = dve.tensor_tensor(qk[:, i, :], tmp1, tmp2, ALU.add)
                    last.then_inc(qk_ready, 1)
                    dve.wait_ge(qk_ready, count("qk"))

            def scores(st):
                s, i = st[2], part(st)
                for c in range(4):
                    n = J[st] + c
                    k = (4 * i + c) % 8
                    job_done(dve, n)
                    do(dve.tensor_reduce(small[:, 16 + k:17 + k], bank(n)[:, 0:ST * (1 + s)], AX.X, ALU.max))
                    dve.tensor_scalar(small[:, k:k + 1], small[:, 16 + k:17 + k], -(HEAD ** -0.5), None, ALU.mult).then_inc(rowmax_ready, 1)

            def attention(st):
                s, i = st[2], part(st)
                for c in range(4):
                    k = (4 * i + c) % 8
                    job_drained(dve, J[f"sc{i}", 0, s] + c)
                    do(dve.reciprocal(small[:, 24 + k:25 + k], small[:, 8 + k:9 + k]))
                    pr = probs[i % 2][:, c, 0:ST * (1 + s)]
                    dve.tensor_scalar(pr, pr, small[:, 24 + k:25 + k], None, ALU.mult).then_inc(probs_ready, 1)

            def conv(st):
                s, piece = st[2], part(st)
                if piece == 0 and s == 1:
                    job_done(dve, J["av3", 0, s] + att_jobs(s))
                if piece % 4 == 0:
                    jobs_drained(dve, J[f"val{piece // 4}", 0, s] + 1)
                for k in range(8 * (piece % 4), min(TAPS, 8 * (piece % 4) + 8)):
                    for c in (2 * (piece // 4), 2 * (piece // 4) + 1):
                        src, dst = cin[:, c, k:k + ST], us[s][:, c, :]
                        tap = col[:, Q_CW + c * TAPS + k:Q_CW + c * TAPS + k + 1]
                        if k == 0:
                            chains(dve.tensor_scalar(dst, src, tap, col[:, Q_CB + c:Q_CB + c + 1], ALU.mult, ALU.add))
                        else:
                            chains(dve.scalar_tensor_tensor(out=dst, in0=src, scalar=tap, in1=dst, op0=ALU.mult, op1=ALU.add))
                chains_end()
                if piece == CONV_PIECES - 1:
                    dve.sem_inc(conv_done, 1)

            def chan(st):
                for i in range(NS):
                    job_drained(dve, J[st] + i)
                normalize([(ut[:, i, :], ut[:, i, :]) for i in range(NS)])
                dve.sem_inc(un_ready, 1)

            def merge(st):
                name, l, s = st
                lo = part(st) * UW
                if part(st) == 0:
                    loaded("rows", 1)
                for i in range(NS):
                    n = J[st] + i
                    job_done(dve, n)
                    drains(dve.tensor_tensor(h[:, NS * s + i, lo:lo + UW], bank(n)[:, 0:UW], rows[:, 0, lo:lo + UW], ALU.add), n)
                if part(st) == 3:
                    jobs_drained(dve, J[st] + 1)
                    dve.sem_inc(rows_used, 1)

            def post(st):
                _, l, s = st
                loaded("gmod", 1)
                loaded("lngb", 2)
                jobs_drained(dve, J[st] - 1)
                post_norm([NS * s + i for i in range(NS)], s if l == 0 else 0, None)
                dve.sem_inc(lngb_used, 1)

            def top16(pair):
                for v, _, src, _ in pair:
                    chains(dve.max(v[:, 0:8], src))
                for v, ix, src, _ in pair:
                    chains(dve.max_index(ix[:, 0:8], v[:, 0:8], src))
                for v, _, src, spare in pair:
                    chains(dve.match_replace(spare, v[:, 0:8], src, LOWEST))
                for v, _, _, spare in pair:
                    chains(dve.max(v[:, 8:16], spare))
                for v, ix, _, spare in pair:
                    chains(dve.max_index(ix[:, 8:16], v[:, 8:16], spare))

            def router(st):
                for k in range(2):
                    c = 2 * part(st) + k
                    n = J[st] + 2 + k
                    job_done(dve, n)
                    top16([(tv[:, i, c, :], ti[:, i, c, :], bank(n)[:, i * NK:(i + 1) * NK], left[:, i * NK:(i + 1) * NK]) for i in range(NS)])
                    chains_end()
                    dve.sem_inc(bank_drained[n % NB], 1)

            def picka(st):
                i, half = st[2] % 2, part(st)
                hs = slice(HALF * half, HALF * half + HALF)
                tvp = tv[:, i].rearrange("p (h s) k -> p h s k", s=2)
                v1, v2 = tvp[:, hs, 0, :], tvp[:, hs, 1, :]
                chains(dve.tensor_tensor(cand[:, hs, 0:WIDE * TOPK].rearrange("p h (i j) -> p h i j", i=WIDE),
                                         v1[:, :, 0:WIDE].unsqueeze(3).broadcast_to([P, HALF, WIDE, TOPK]),
                                         v2.unsqueeze(2).broadcast_to([P, HALF, WIDE, TOPK]), ALU.add))
                do(dve.tensor_tensor(cand[:, hs, WIDE * TOPK:NCAND].rearrange("p h (i j) -> p h i j", j=DEEP),
                                     v1[:, :, WIDE:TOPK].unsqueeze(3).broadcast_to([P, HALF, TOPK - WIDE, DEEP]),
                                     v2[:, :, 0:DEEP].unsqueeze(2).broadcast_to([P, HALF, TOPK - WIDE, DEEP]), ALU.add))
                for b in range(HALF * half, HALF * half + HALF, 2):
                    top16([(sc[:, b + k, :], pos[:, b + k, :], cand[:, b + k, :], left[:, k * P:k * P + NCAND]) for k in range(2)])
                chains_end()
                do(dve.tensor_copy(small[:, 0:HALF], sc[:, hs, 0]))
                dve.tensor_tensor(sc[:, hs, :], sc[:, hs, :], small[:, 0:HALF].unsqueeze(2).broadcast_to([P, HALF, TOPK]), ALU.subtract).then_inc(sc_ready, 1)

            def pickb(st):
                t, half = st[2], part(st)
                hs = slice(HALF * half, HALF * half + HALF)
                i, lo = t % 2, (t % 4) * E + half * E // 2

                def out(tile):
                    return tile[:, lo:lo + E // 2].rearrange("p (h k) -> p h k", h=HALF)

                ks = slice(2 * HALF * half, 2 * HALF * half + 2 * HALF)
                do(dve.tensor_copy(tif[:, ks, :], ti[:, i, ks, :]))
                tip = tif.rearrange("p (h s) k -> p h s k", s=2)[:, hs]
                pl, hi, fi, se, x1, x2 = (b[:, hs, :] for b in (pos, high, first, second, e1, e2))
                do(dve.tensor_scalar(hi, pl, 4, None, ALU.logical_shift_right))
                do(dve.tensor_copy(se, hi))
                do(dve.tensor_scalar(hi, pl, 2, None, ALU.logical_shift_right))
                do(dve.tensor_copy(fi, hi))
                do(dve.scalar_tensor_tensor(out=fi, in0=fi, scalar=float(WIDE - WIDE * TOPK // DEEP), in1=se, op0=ALU.add, op1=ALU.max))
                do(dve.tensor_scalar(x2, fi, float(DEEP), float(WIDE * TOPK - WIDE * DEEP), ALU.mult, ALU.add))
                do(dve.scalar_tensor_tensor(out=x2, in0=fi, scalar=float(TOPK), in1=x2, op0=ALU.mult, op1=ALU.min))
                do(dve.tensor_copy(se, pl))
                do(dve.tensor_tensor(se, se, x2, ALU.subtract))
                for step in range(3):
                    for b, place, dst in ((0, fi, x1), (1, se, x2)):
                        h4 = hot[:, HALF * b:HALF * b + HALF]
                        if step == 0:
                            chains(dve.tensor_tensor(h4, place.unsqueeze(3).broadcast_to([P, HALF, TOPK, TOPK]),
                                                     con[:, C_IOTA:C_IOTA + TOPK].unsqueeze(1).unsqueeze(1).broadcast_to([P, HALF, TOPK, TOPK]), ALU.is_equal))
                        elif step == 1:
                            chains(dve.tensor_tensor(h4, h4, tip[:, :, b, :].unsqueeze(2).broadcast_to([P, HALF, TOPK, TOPK]), ALU.mult))
                        else:
                            chains(dve.tensor_reduce(dst, h4, AX.X, ALU.add))
                chains_end()
                do(dve.scalar_tensor_tensor(out=out(eid), in0=x1, scalar=float(NK), in1=x2, op0=ALU.mult, op1=ALU.add))
                dve.wait_ge(scexp_ready, 2 * t + half + 1)
                do(dve.tensor_reduce(small[:, 8:8 + HALF], sc[:, hs, :], AX.X, ALU.add))
                do(dve.reciprocal(small[:, 8:8 + HALF], small[:, 8:8 + HALF]))
                dve.tensor_tensor(out(gates), sc[:, hs, :],
                                  small[:, 8:8 + HALF].unsqueeze(2).broadcast_to([P, HALF, TOPK]), ALU.mult).then_inc(eid_ready, 1)
                dve.wait_ge(eid_ready, 2 * t + half + 1)

            def stage_rows(column, half):
                dve.tensor_copy(rows_idx[:, half, :], eid[:, bass.ds(column, RING)]).then_inc(idx_staged, 1)

            def begin(st):
                stage_rows(0, 0)
                stage_rows(RING, 1)

            def experts(q0, count_):
                def rows8(q, half, t, column, ahead):
                    for j in range(RING):
                        b = half * RING + j
                        dve.wait_ge(row_in[j], (q + 1) * 16)
                        r = ring[:, j, 0:D]
                        dve.tensor_tensor_reduce(out=r, in0=r, in1=h[:, t, :], scale=1.0, scalar=0.0, op0=ALU.mult,
                                                 op1=ALU.add, accum_out=dots[:, b:b + 1]).then_inc(dots_ready, 1)
                    if ahead:
                        stage_rows(column + 2 * RING, half)

                for q, pairs in expert_runs(q0, count_):
                    l, p = q // (4 * GPT), q // GPT
                    t = p if l == 0 else p - 2
                    column = (q - l * 4 * GPT) * RING
                    if pairs:
                        with dve.Fori(0, pairs) as i:
                            rows8(q + 2 * i, 0, t, column + i * 2 * RING, True)
                            rows8(q + 2 * i + 1, 1, t, column + i * 2 * RING + RING, True)
                    else:
                        rows8(q, q % 2, t, column, q + 2 not in (4 * GPT, 4 * GPT + 1, 6 * GPT, 6 * GPT + 1))

            def close(st):
                p = st[1]
                if p in EXPERT_ROWS:
                    cnt["gmod"], cnt["lngb"] = EXPERT_ROWS[p]
                    loaded("gmod", 0)
                    loaded("lngb", 0)
                dve.wait_ge(slots_free, RING + (p + 1) * E)
                post_norm([p if p < 4 else p - 2], p // 2 if p < 4 else 1, expert_sum[:, :])
                if p in (0, 3, 5):
                    dve.sem_inc(lngb_used, 1)

            EXPERT_ROWS = {0: (2, 4), 1: (4, 8), 2: (4, 8), 4: (6, 12)}

            def values(st):
                name, l, s = st
                lo = part(st) * UW
                if name == "mv0" and s == 0:
                    loaded("mlb", 1)
                for i in range(NS):
                    n = J[st] + i
                    job_done(dve, n)
                    if name[:2] == "mv":
                        drains(dve.tensor_tensor(mval[:, NS * s + i, lo:lo + UW], bank(n)[:, 0:UW], mlb[:, lo:lo + UW], ALU.add), n)
                    else:
                        drains(dve.tensor_tensor(og[:, i, lo:lo + UW], bank(n)[:, 0:UW], mlb[:, D + lo:D + lo + UW], ALU.add), n)

            def mg(st):
                n, s = J[st], st[2]
                job_done(dve, n)
                drains(dve.tensor_tensor(gt[:, NS * s:NS * s + NS, :], bank(n)[:, 0:32].rearrange("p (t n) -> p t n", t=NS),
                                         mlb[:, 2048:2064].unsqueeze(1).broadcast_to([P, NS, 16]), ALU.add), n)
                job_drained(dve, n)

            gt5 = gt[:, :, :].rearrange("p t (d k h) -> p t d k h", d=2, k=2)

            def by_dir(tile):
                return tile[:, :, :].rearrange("p t (d h) -> p t d h", d=2)

            def logf(st):
                f = gt5[:, :, :, 1, :]
                do(dve.tensor_scalar(by_dir(lf), f, -1.0, None, ALU.mult))
                dve.tensor_tensor(by_dir(la), by_dir(lf), f, ALU.max).then_inc(lf_a, 1)
                dve.wait_ge(lf_a, 1)
                do(dve.tensor_scalar(by_dir(lf), f, 0.0, None, ALU.min))
                dve.wait_ge(lf_e, 1)
                dve.tensor_tensor(lf[:, :, :], lf[:, :, :], le[:, :, :], ALU.subtract).then_inc(lf_ready, 1)

            def gatesum(st):
                n, ig = J[st], gt5[:, :, :, 0, :]
                job_done(dve, n)
                drains(dve.tensor_copy(bc[:, :, :], bank(n)[:, 0:32].rearrange("p (t n) -> p t n", t=TILES)), n)
                job_drained(dve, n)
                dve.tensor_tensor(by_dir(cg), ig, by_dir(bc), ALU.subtract).then_inc(cg_ready, 1)
                dve.wait_ge(loads["mlc"], 48)

            def decay(st):
                hd = part(st)
                cm, b = cms[hd % 2], 4 * (hd % 2)
                if hd >= 2:
                    dve.wait_ge(am_ready, 2 * hd - 2)
                for d in range(2):
                    dve.wait_ge(decay_full, 2 * hd + d + 1)
                    for i in range(2):
                        chains(dve.tensor_tensor(cm[:, 2 * d + i, :], expert_sum[:, d * 512:(d + 1) * 512], mask[:, 2 * d + i, :], ALU.add))
                    for i in range(2):
                        chains(dve.tensor_reduce(top[:, b + 2 * d + i:b + 2 * d + i + 1], cm[:, 2 * d + i, :], AX.X, ALU.max))
                    chains_end()
                    dve.sem_inc(decay_taken, 1)
                    for i in range(2):
                        r = b + 2 * d + i
                        dve.tensor_scalar(nm[:, r:r + 1], top[:, r:r + 1], 0.0, -1.0, ALU.max, ALU.mult).then_inc(nm_ready, 1)

            def head(st):
                hd, b0 = part(st), J[f"score{part(st)}", 1, 1]
                cm, b = cms[hd % 2], 4 * (hd % 2)
                for i in range(2):
                    n = b0 + i
                    job_done(dve, n)
                    for d in range(2):
                        r = 2 * d + i
                        dve.wait_ge(wm_ready, 4 * hd + r + 1)
                        chains(dve.tensor_tensor_reduce(out=cm[:, r, :], in0=cm[:, r, :], in1=bank(n)[:, :], scale=MDQ ** -0.5, scalar=0.0,
                                                        op0=ALU.mult, op1=ALU.add, accum_out=den[:, r:r + 1]))
                    for r in (i, 2 + i):
                        chains(dve.tensor_scalar(den[:, 4 + r:5 + r], den[:, r:r + 1], -1.0, None, ALU.mult))
                    for r in (i, 2 + i):
                        chains(dve.tensor_tensor(den[:, r:r + 1], den[:, r:r + 1], den[:, 4 + r:5 + r], ALU.max))
                    for r in (i, 2 + i):
                        chains(dve.tensor_tensor(den[:, r:r + 1], den[:, r:r + 1], thr[:, b + r:b + r + 1], ALU.max))
                    for r in (i, 2 + i):
                        chains(dve.reciprocal(den[:, 4 + r:5 + r], den[:, r:r + 1]))
                    chains_end()
                    dve.sem_inc(bank_drained[n % NB], 1)
                    do(dve.tensor_scalar(cm[:, i, :], cm[:, i, :], den[:, 4 + i:5 + i], None, ALU.mult))
                    if hd:
                        job_done(dve, J[f"head{hd - 1}", 1, 1] + i)
                    dve.scalar_tensor_tensor(out=am[:, i, :], in0=cm[:, 2 + i, :], scalar=den[:, 6 + i:7 + i], in1=cm[:, i, :],
                                             op0=ALU.mult, op1=ALU.add).then_inc(am_ready, 1)

            def head_stats(hd):
                for i in range(NS):
                    job_drained(dve, J[f"head{hd}", 1, 1] + 2 + i)
                    mean_var(hh[:, i, hd * MDV:(hd + 1) * MDV], 4 * i + hd)

            def output_gate(st):
                for hd in range(MH - 1):
                    head_stats(hd)
                dve.wait_ge(sig_ready, 1)
                for i in range(NS):
                    chains(dve.tensor_tensor(og[:, i, :], og[:, i, :], normg, ALU.mult))
                chains_end()

            def heads(st):
                head_stats(MH - 1)
                var_out(8)
                root(8)
                for hd in range(MH):
                    for i in range(NS):
                        k = 4 * i + hd
                        y = hh[:, i, hd * MDV:(hd + 1) * MDV]
                        chains(dve.tensor_scalar(y, y, mv[:, k, 0:1], rstd[:, k:k + 1], ALU.subtract, ALU.mult))
                chains_end()
                for i in range(NS):
                    dve.tensor_tensor(hh[:, i, :], hh[:, i, :], og[:, i, :], ALU.mult).then_inc(y_ready, 1)

            do(dve.memset(mv[:, :, :], 0.0))
            walk_all({"mod": mod, "ln1": modulate, "ln2": modulate, "val": val, "q": q, "kv": kv, "rope": rope, "sc": scores, "av": attention,
                      "conv": conv, "chan": chan, "merge": merge, "post": post, "r": router, "picka": picka, "pickb": pickb,
                      "begin": begin, "mv": values, "mo": values, "mg": mg, "logf": logf, "gatesum": gatesum, "decay": decay, "head": head,
                      "og": output_gate, "heads": heads, "norm": first_norm,
                      "close": close}, experts, VECTOR_WALK)


def constants():
    f = np.float32
    i = np.arange(P)
    con = np.zeros((P, C_END), f)
    con[:, C_ID:C_ID + P] = np.eye(P, dtype=f)
    con[:, C_LT:C_LT + P] = i[:, None] <= i[None, :]
    con[:, C_UT:C_UT + P] = i[:, None] >= i[None, :]
    con[:, C_ONE:C_ONE + P] = 1.0
    inv = (10000.0 ** (-np.arange(16, dtype=f) / f(16))).astype(f)
    tok = np.arange(2 * P)
    row, colp = (tok // 64).astype(f), (tok % 64).astype(f)
    ang = np.stack([row[:, None] * inv, colp[:, None] * inv], 1)
    cos = np.stack([np.cos(ang), np.cos(ang)], 2).reshape(2, P, HEAD)
    sin = np.stack([-np.sin(ang), np.sin(ang)], 2).reshape(2, P, HEAD)
    for t in range(2):
        con[:, C_COS + t * HEAD:C_COS + (t + 1) * HEAD] = cos[t]
        con[:, C_SIN + t * HEAD:C_SIN + (t + 1) * HEAD] = sin[t]
    con[:, C_IOTA:C_IOTA + TOPK] = np.arange(TOPK)
    mask = np.full((P, 4, 4, P), NEG, f)
    for d in range(2):
        for t in range(2):
            mask[:, 2 * d + t, 0:2] = 0.0
            q, s = i[:, None], i[None, :]
            mask[:, 2 * d + t, 2 + t] = np.where(s <= q if d == 0 else s >= q, 0.0, NEG)
            if t == 1 and d == 0:
                mask[:, 1, 2] = 0.0
            if t == 0 and d == 1:
                mask[:, 2, 3] = 0.0
    sel = np.zeros((8, 8, P), f)
    for r in range(8):
        sel[r, r] = 1.0
    return con, mask.reshape(P, 4, 512), sel


def kernel(**inputs):
    import concourse.bacc as _bacc
    from concourse.bass_utils import run_bass_kernel_spmd as _run

    v = {k: np.asarray(b) for k, b in inputs.items()}
    con, mask, sel = constants()

    def chunks(b, n):
        return b.reshape(n, P).T

    order = np.arange(1792)
    order[1024:1536] = 1024 + np.concatenate([np.arange(HEAD) + HEAD * (c + 4 * g) for c in range(4) for g in range(2)])
    b_in, mb = v["ab_b_in"][0][order], v["ml_b_in"][0]
    col = np.concatenate([
        chunks(b_in[0:512], 4), chunks(b_in[512:1024], 4), chunks(v["ab_conv_b"][0], 4), chunks(v["ab_conv_ln_g"][0], 4),
        chunks(v["ab_conv_ln_b"][0], 4), v["ab_conv_w"][0].reshape(TAPS, 4, P).transpose(2, 1, 0).reshape(P, 4 * TAPS),
        chunks(mb[0:512], 4), chunks(mb[512:1024], 4)], axis=1)
    keys = np.stack([v["peer_k1"], v["peer_k2"]], 2)
    arrays = {
        "x": v["x"][0], "ctx": v["ctx"][0],
        "cvec": np.stack([v["c"][0], v["c_ctx"]]).reshape(2, KD, P).transpose(2, 1, 0),
        "con": con, "mask": mask, "sel": sel, "col": col,
        "w_mod": v["w_mod"], "b_mod": v["b_mod"], "ln1_g": v["ln1_g"], "ln1_b": v["ln1_b"], "ln2_g": v["ln2_g"], "ln2_b": v["ln2_b"],
        "ab_w_in": v["ab_w_in"][0][:, order], "ab_b_in": b_in,
        "qk_g": np.concatenate([np.tile(v["ab_q_norm_g"][0], NQH), np.tile(v["ab_k_norm_g"][0], NKV)]),
        "ab_w_out": v["ab_w_out"][0], "ab_b_out": v["ab_b_out"][0],
        "ml_w_in": v["ml_w_in"][0], "ml_b_in": mb, "ml_norm_g": v["ml_norm_g"][0], "ml_w_out": v["ml_w_out"][0], "ml_b_out": v["ml_b_out"][0],
        "w_q": v["peer_w_q"], "keys": keys.transpose(0, 4, 1, 2, 3).reshape(2, P, 16, NK),
        "uv0": np.concatenate([v["peer_u"][0], v["peer_v"][0]], axis=1), "uv1": np.concatenate([v["peer_u"][1], v["peer_v"][1]], axis=1),
    }
    nc = _bacc.Bacc("TRN2", target_bir_lowering=False, num_devices=1)
    given, aps = {}, {}
    for name, b in arrays.items():
        b = np.ascontiguousarray(b)
        given[f"in_{name}"] = b
        aps[name] = nc.dram_tensor(f"in_{name}", b.shape, mybir.dt.from_np(b.dtype), kind="ExternalInput").ap()
    aps["mod_d"] = nc.dram_tensor("mod_d", (2, 2, 6 * D), F32, kind="Internal").ap()
    aps["out"] = nc.dram_tensor("out_x", (2 * P, D), F32, kind="ExternalOutput").ap()
    build(nc, aps)
    r = _run(nc, [given], core_ids=[0])
    return r.results[0]["out_x"].reshape(1, 2 * P, D)
```
